# Optimizing a Trainium2 kernel written in Bass

```python
import math
import jax, jax.numpy as jnp
from jax import lax
import numpy as np
import jax
import jax.numpy as jnp

D_MODEL = 1024
BATCH = 1
SEQ = 256
DEPTH = 2

EPS = 1e-6
SSD_HEAD_DIM = 64
SSD_INNER = D_MODEL
SSD_HEADS = SSD_INNER // SSD_HEAD_DIM
SSD_GROUPS = 2
SSD_STATE = 128
SSD_CONV = 4
SSD_CHUNK = 128
SSD_XBC = SSD_INNER + 2 * SSD_GROUPS * SSD_STATE
MLA_HEADS = D_MODEL // 128
MLA_NOPE = 128
MLA_ROPE = 64
MLA_V = 128
MLA_Q_LORA = D_MODEL // 2
MLA_KV_LORA = D_MODEL // 4
MLA_QBLOCK = 128
ROPE_THETA = 10000.0
GDN_HEAD_K = 128
GDN_HEAD_V = 128
GDN_V_HEADS = D_MODEL // GDN_HEAD_V
GDN_QK_HEADS = GDN_V_HEADS // 2
GDN_CONV = 4
GDN_CHUNK = 64
GDN_QK = GDN_QK_HEADS * GDN_HEAD_K
GDN_VW = GDN_V_HEADS * GDN_HEAD_V
GDN_QKV = 2 * GDN_QK + GDN_VW
N_BRANCH = 3
D_FF = 4 * D_MODEL
IN_SIZES = (SSD_INNER, SSD_XBC, SSD_HEADS, MLA_Q_LORA, MLA_KV_LORA, MLA_ROPE,
            GDN_QKV, GDN_VW, GDN_V_HEADS, GDN_V_HEADS, N_BRANCH * D_MODEL)
N_IN = (SSD_INNER + SSD_XBC + SSD_HEADS + MLA_Q_LORA + MLA_KV_LORA + MLA_ROPE
        + GDN_QKV + GDN_VW + 2 * GDN_V_HEADS + N_BRANCH * D_MODEL)


def rmsnorm(x, g):
    xf = x.astype(jnp.float32)
    y = xf * lax.rsqrt(jnp.mean(xf * xf, axis=-1, keepdims=True) + EPS)
    return (y * g.astype(jnp.float32)).astype(x.dtype)

def l2norm(x):
    xf = x.astype(jnp.float32)
    return xf * lax.rsqrt(jnp.sum(xf * xf, axis=-1, keepdims=True) + EPS)

def causal_dwconv(x, w):
    K, C = w.shape
    return lax.conv_general_dilated(
        x, w[:, None, :].astype(x.dtype), window_strides=(1,), padding=[(K - 1, 0)],
        dimension_numbers=('NWC', 'WIO', 'NWC'), feature_group_count=C)

def rope_tables(positions):
    inv = ROPE_THETA ** (-jnp.arange(0, MLA_ROPE, 2, dtype=jnp.float32) / MLA_ROPE)
    ang = positions.astype(jnp.float32)[..., None] * inv
    return jnp.cos(ang), jnp.sin(ang)

def apply_rope(t, cos, sin):
    half = t.shape[-1] // 2
    tf = t.astype(jnp.float32)
    t1, t2 = tf[..., :half], tf[..., half:]
    return jnp.concatenate([t1 * cos - t2 * sin, t2 * cos + t1 * sin], axis=-1).astype(t.dtype)

def ssd_chunked(X, dA, Bm, Cm):
    b, s, g, e, p = X.shape
    n = Bm.shape[-1]
    Q = SSD_CHUNK
    c = s // Q
    X = X.reshape(b, c, Q, g, e, p)
    Bc = Bm.reshape(b, c, Q, g, n)
    Cc = Cm.reshape(b, c, Q, g, n)
    A = jnp.transpose(dA.reshape(b, c, Q, g, e), (0, 3, 4, 1, 2))
    A_cum = jnp.cumsum(A, axis=-1)
    tril = jnp.tril(jnp.ones((Q, Q), dtype=bool))
    L = jnp.exp(jnp.where(tril, A_cum[..., :, None] - A_cum[..., None, :], -jnp.inf))
    CB = jnp.einsum('bclgn,bcsgn->bcgls', Cc, Bc)
    y_diag = jnp.einsum('bcgls,bgecls,bcsgep->bclgep', CB, L, X)
    decay_states = jnp.exp(A_cum[..., -1:] - A_cum)
    states = jnp.einsum('bclgn,bgecl,bclgep->bcgepn', Bc, decay_states, X)
    chunk_decay = jnp.exp(A_cum[..., -1])

    def step(h, inp):
        st, dec = inp
        return h * dec[..., None, None] + st, h

    _, h_prev = lax.scan(step, jnp.zeros_like(states[:, 0]),
                         (jnp.moveaxis(states, 1, 0), jnp.moveaxis(chunk_decay, -1, 0)))
    h_prev = jnp.moveaxis(h_prev, 0, 1)
    y_off = jnp.einsum('bclgn,bcgepn,bgecl->bclgep', Cc, h_prev, jnp.exp(A_cum))
    return (y_diag + y_off).reshape(b, s, g, e, p)

def ssd_mixer(z, xbc, dt_raw, conv_w, conv_b, dt_bias, a_log, d_skip, norm_g):
    Bsz, S, _ = z.shape
    G, E, P, N = SSD_GROUPS, SSD_HEADS // SSD_GROUPS, SSD_HEAD_DIM, SSD_STATE
    xbc = jax.nn.silu(causal_dwconv(xbc, conv_w) + conv_b.astype(xbc.dtype))
    xs, bm, cm = jnp.split(xbc, [SSD_INNER, SSD_INNER + G * N], axis=-1)
    xs = xs.astype(jnp.float32).reshape(Bsz, S, G, E, P)
    bm = bm.astype(jnp.float32).reshape(Bsz, S, G, N)
    cm = cm.astype(jnp.float32).reshape(Bsz, S, G, N)
    dt = jax.nn.softplus(dt_raw.astype(jnp.float32) + dt_bias.astype(jnp.float32)).reshape(Bsz, S, G, E)
    a = -jnp.exp(a_log.astype(jnp.float32)).reshape(G, E)
    y = ssd_chunked(xs * dt[..., None], dt * a, bm, cm)
    y = y + d_skip.astype(jnp.float32).reshape(G, E)[:, :, None] * xs
    y = y.reshape(Bsz, S, SSD_INNER) * jax.nn.silu(z.astype(jnp.float32))
    y = rmsnorm(y.reshape(Bsz, S, G, SSD_INNER // G), norm_g.reshape(G, SSD_INNER // G))
    return y.reshape(Bsz, S, SSD_INNER).astype(z.dtype)

def mla_mixer(cq, ckv, k_rope, cos, sin, q_norm_g, w_uq, kv_norm_g, w_ukv):
    Bsz, S, _ = cq.shape
    H = MLA_HEADS
    q = (rmsnorm(cq, q_norm_g) @ w_uq).reshape(Bsz, S, H, MLA_NOPE + MLA_ROPE)
    q_nope, q_pe = jnp.split(q, [MLA_NOPE], axis=-1)
    q_pe = apply_rope(q_pe, cos[:, :, None, :], sin[:, :, None, :])
    kv = (rmsnorm(ckv, kv_norm_g) @ w_ukv).reshape(Bsz, S, H, MLA_NOPE + MLA_V)
    k_nope, v = jnp.split(kv, [MLA_NOPE], axis=-1)
    k_pe = apply_rope(k_rope, cos, sin)
    nblk = S // MLA_QBLOCK
    scale = (MLA_NOPE + MLA_ROPE) ** -0.5
    kpos = jnp.arange(S)

    def to_blocks(t):
        return jnp.moveaxis(t.reshape((Bsz, nblk, MLA_QBLOCK) + t.shape[2:]), 1, 0)

    def attend(args):
        qn, qp, blk = args
        sc = (jnp.einsum('bqhd,bkhd->bhqk', qn, k_nope, preferred_element_type=jnp.float32)
              + jnp.einsum('bqhr,bkr->bhqk', qp, k_pe, preferred_element_type=jnp.float32))
        qpos = blk * MLA_QBLOCK + jnp.arange(MLA_QBLOCK)
        sc = jnp.where(kpos[None, :] <= qpos[:, None], sc * scale, -jnp.inf)
        pr = jax.nn.softmax(sc, axis=-1)
        return jnp.einsum('bhqk,bkhd->bqhd', pr.astype(v.dtype), v)

    o = lax.map(attend, (to_blocks(q_nope), to_blocks(q_pe), jnp.arange(nblk)))
    return jnp.moveaxis(o, 0, 1).reshape(Bsz, S, H * MLA_V)

def gated_delta_chunked(q, k, v, g, beta):
    Bsz, S, H, DK = k.shape
    DV = v.shape[-1]
    L = GDN_CHUNK
    C = S // L

    def chunks(t):
        return jnp.moveaxis(t.reshape((Bsz, C, L, H) + t.shape[3:]), 3, 1)

    q = chunks(q * (DK ** -0.5))
    k = chunks(k)
    v = chunks(v)
    g = jnp.cumsum(chunks(g), axis=-1)
    beta = chunks(beta)
    incl = jnp.tril(jnp.ones((L, L), dtype=bool))
    strict = jnp.tril(jnp.ones((L, L), dtype=bool), -1)
    decay = jnp.exp(jnp.where(incl, g[..., :, None] - g[..., None, :], -jnp.inf))
    kb = k * beta[..., None]
    a_mat = jnp.where(strict, jnp.einsum('bhcld,bhcmd->bhclm', kb, k) * decay, 0.0)
    rhs = jnp.concatenate([v * beta[..., None], kb * jnp.exp(g)[..., None]], axis=-1)
    sol = lax.linalg.triangular_solve(a_mat + jnp.eye(L, dtype=jnp.float32), rhs,
                                      left_side=True, lower=True)
    u, w = jnp.split(sol, [DV], axis=-1)
    qk = jnp.where(incl, jnp.einsum('bhcld,bhcmd->bhclm', q, k) * decay, 0.0)

    def step(state, inp):
        qc, kc, uc, wc, gc, ac = inp
        v_new = uc - jnp.einsum('bhld,bhdv->bhlv', wc, state)
        o = (jnp.einsum('bhld,bhdv->bhlv', qc * jnp.exp(gc)[..., None], state)
             + jnp.einsum('bhlm,bhmv->bhlv', ac, v_new))
        g_last = gc[..., -1:]
        state = (state * jnp.exp(g_last)[..., None]
                 + jnp.einsum('bhld,bhlv->bhdv', kc * jnp.exp(g_last - gc)[..., None], v_new))
        return state, o

    xs = tuple(jnp.moveaxis(t, 2, 0) for t in (q, k, u, w, g, qk))
    _, o = lax.scan(step, jnp.zeros((Bsz, H, DK, DV), jnp.float32), xs)
    return jnp.transpose(o, (1, 0, 3, 2, 4)).reshape(Bsz, S, H, DV)

def gdn_mixer(qkv, z, b_raw, a_raw, conv_w, dt_bias, a_log, norm_g):
    Bsz, S, _ = qkv.shape
    qkv = jax.nn.silu(causal_dwconv(qkv, conv_w))
    q, k, v = jnp.split(qkv, [GDN_QK, 2 * GDN_QK], axis=-1)
    rep = GDN_V_HEADS // GDN_QK_HEADS
    q = jnp.repeat(l2norm(q.reshape(Bsz, S, GDN_QK_HEADS, GDN_HEAD_K)), rep, axis=2)
    k = jnp.repeat(l2norm(k.reshape(Bsz, S, GDN_QK_HEADS, GDN_HEAD_K)), rep, axis=2)
    v = v.reshape(Bsz, S, GDN_V_HEADS, GDN_HEAD_V).astype(jnp.float32)
    beta = jax.nn.sigmoid(b_raw.astype(jnp.float32))
    g = -jnp.exp(a_log.astype(jnp.float32)) * jax.nn.softplus(a_raw.astype(jnp.float32) + dt_bias.astype(jnp.float32))
    o = gated_delta_chunked(q, k, v, g, beta)
    o = rmsnorm(o, norm_g) * jax.nn.silu(z.astype(jnp.float32).reshape(Bsz, S, GDN_V_HEADS, GDN_HEAD_V))
    return o.reshape(Bsz, S, GDN_VW).astype(z.dtype)

def hybrid_layer(x, cos, sin, norm1_g, w_in, ssd_conv_w, ssd_conv_b, ssd_dt_bias, ssd_a_log, ssd_d,
                 ssd_norm_g, mla_q_norm_g, mla_w_uq, mla_kv_norm_g, mla_w_ukv, gdn_conv_w, gdn_dt_bias,
                 gdn_a_log, gdn_norm_g, w_ssd_out, w_mla_out, w_gdn_out, w_out, norm2_g, w_up, w_down):
    xn = rmsnorm(x, norm1_g)
    proj = xn @ w_in
    split_at = [int(i) for i in np.cumsum(IN_SIZES)[:-1]]
    (ssd_z, ssd_xbc, ssd_dt, mla_cq, mla_ckv, mla_kr, gdn_qkv, gdn_z, gdn_b, gdn_a,
     gate_logits) = jnp.split(proj, split_at, axis=-1)
    y_ssd = ssd_mixer(ssd_z, ssd_xbc, ssd_dt, ssd_conv_w, ssd_conv_b, ssd_dt_bias, ssd_a_log, ssd_d, ssd_norm_g)
    y_mla = mla_mixer(mla_cq, mla_ckv, mla_kr, cos, sin, mla_q_norm_g, mla_w_uq, mla_kv_norm_g, mla_w_ukv)
    y_gdn = gdn_mixer(gdn_qkv, gdn_z, gdn_b, gdn_a, gdn_conv_w, gdn_dt_bias, gdn_a_log, gdn_norm_g)
    gates = jax.nn.sigmoid(gate_logits.astype(jnp.float32)).astype(x.dtype)
    g_ssd, g_mla, g_gdn = jnp.split(gates, N_BRANCH, axis=-1)
    mixed = g_ssd * (y_ssd @ w_ssd_out) + g_mla * (y_mla @ w_mla_out) + g_gdn * (y_gdn @ w_gdn_out)
    h = x + mixed @ w_out
    f = jnp.square(jax.nn.relu(rmsnorm(h, norm2_g) @ w_up)) @ w_down
    return h + f

def first_inputs(seed: int = 0) -> dict:
    key = jax.random.key(seed)
    ks = iter(jax.random.split(key, 40))

    def nrm(shape, scale):
        return jax.random.normal(next(ks), shape, jnp.float32) * scale

    def gain(shape):
        return 1.0 + nrm(shape, 0.02)

    def dt_bias_init(shape):
        dt = jnp.exp(jax.random.uniform(next(ks), shape, jnp.float32, math.log(1e-3), math.log(1e-1)))
        return dt + jnp.log(-jnp.expm1(-dt))

    def a_log_init(shape):
        return jnp.log(jax.random.uniform(next(ks), shape, jnp.float32, 1.0, 16.0))

    x = jax.random.normal(next(ks), (BATCH, SEQ, D_MODEL), jnp.float32)
    offset = jax.random.randint(next(ks), (BATCH, 1), 0, 1024, dtype=jnp.int32)
    positions = offset + jnp.arange(SEQ, dtype=jnp.int32)[None, :]
    return {
        'x': x,
        'positions': positions,
        'norm1_g': gain((DEPTH, D_MODEL)),
        'w_in': nrm((DEPTH, D_MODEL, N_IN), D_MODEL ** -0.5),
        'ssd_conv_w': nrm((DEPTH, SSD_CONV, SSD_XBC), SSD_CONV ** -0.5),
        'ssd_conv_b': nrm((DEPTH, SSD_XBC), 0.01),
        'ssd_dt_bias': dt_bias_init((DEPTH, SSD_HEADS)),
        'ssd_a_log': a_log_init((DEPTH, SSD_HEADS)),
        'ssd_d': gain((DEPTH, SSD_HEADS)),
        'ssd_norm_g': gain((DEPTH, SSD_INNER)),
        'mla_q_norm_g': gain((DEPTH, MLA_Q_LORA)),
        'mla_w_uq': nrm((DEPTH, MLA_Q_LORA, MLA_HEADS * (MLA_NOPE + MLA_ROPE)), MLA_Q_LORA ** -0.5),
        'mla_kv_norm_g': gain((DEPTH, MLA_KV_LORA)),
        'mla_w_ukv': nrm((DEPTH, MLA_KV_LORA, MLA_HEADS * (MLA_NOPE + MLA_V)), MLA_KV_LORA ** -0.5),
        'gdn_conv_w': nrm((DEPTH, GDN_CONV, GDN_QKV), GDN_CONV ** -0.5),
        'gdn_dt_bias': dt_bias_init((DEPTH, GDN_V_HEADS)),
        'gdn_a_log': a_log_init((DEPTH, GDN_V_HEADS)),
        'gdn_norm_g': gain((DEPTH, GDN_HEAD_V)),
        'w_ssd_out': nrm((DEPTH, SSD_INNER, D_MODEL), SSD_INNER ** -0.5),
        'w_mla_out': nrm((DEPTH, MLA_HEADS * MLA_V, D_MODEL), (MLA_HEADS * MLA_V) ** -0.5),
        'w_gdn_out': nrm((DEPTH, GDN_VW, D_MODEL), GDN_VW ** -0.5),
        'w_out': nrm((DEPTH, D_MODEL, D_MODEL), D_MODEL ** -0.5),
        'norm2_g': gain((DEPTH, D_MODEL)),
        'w_up': nrm((DEPTH, D_MODEL, D_FF), D_MODEL ** -0.5),
        'w_down': nrm((DEPTH, D_FF, D_MODEL), D_FF ** -0.5),
        'final_norm_g': gain((D_MODEL,)),
    }

def first_block(x, positions, norm1_g, w_in, ssd_conv_w, ssd_conv_b, ssd_dt_bias, ssd_a_log, ssd_d,
              ssd_norm_g, mla_q_norm_g, mla_w_uq, mla_kv_norm_g, mla_w_ukv, gdn_conv_w, gdn_dt_bias,
              gdn_a_log, gdn_norm_g, w_ssd_out, w_mla_out, w_gdn_out, w_out, norm2_g, w_up, w_down,
              final_norm_g):
    cos, sin = rope_tables(positions)
    for l in range(DEPTH):
        x = hybrid_layer(x, cos, sin, norm1_g[l], w_in[l], ssd_conv_w[l], ssd_conv_b[l], ssd_dt_bias[l],
                         ssd_a_log[l], ssd_d[l], ssd_norm_g[l], mla_q_norm_g[l], mla_w_uq[l],
                         mla_kv_norm_g[l], mla_w_ukv[l], gdn_conv_w[l], gdn_dt_bias[l], gdn_a_log[l],
                         gdn_norm_g[l], w_ssd_out[l], w_mla_out[l], w_gdn_out[l], w_out[l], norm2_g[l],
                         w_up[l], w_down[l])
    return rmsnorm(x, final_norm_g)


GRID_W = 64
CTX_LEN = 256
N_MIXERS = 2
NA_HEADS = 16
NA_HEAD_DIM = D_MODEL // NA_HEADS
WIN_H = 8
WIN_W = 16
HG_HEADS = 8
HG_EXPAND = 128
HG_FDIM = HG_HEADS * HG_EXPAND
HG_HEAD_V = D_MODEL // HG_HEADS
CHUNK = 64
D_FF_2 = -(-(8 * D_MODEL) // (3 * 256)) * 256
N_NA_LAYERS = (DEPTH + 1) // 2
N_HG_LAYERS = DEPTH // 2


def rms_norm(x, g):
    xf = x.astype(jnp.float32)
    y = xf * lax.rsqrt(jnp.mean(xf * xf, axis=-1, keepdims=True) + EPS)
    return (y * g.astype(jnp.float32)).astype(x.dtype)

def ada_mod(cvec, w, b):
    return jnp.split(jax.nn.silu(cvec) @ w + b, 6, axis=-1)

def swiglu(h, w_in, w_out):
    a, u = jnp.split(h @ w_in, 2, axis=-1)
    return (jax.nn.silu(a) * u) @ w_out

def na_mixer(h_lat, h_ctx, w_qkv, w_o, q_gain, k_gain, rpb, need_ctx_out):
    B, T, _ = h_lat.shape
    rows = T // GRID_W
    kh = min(WIN_H, rows)
    scale = NA_HEAD_DIM ** -0.5

    def qkv(h):
        n = h.shape[1]
        q, k, v = jnp.split(h @ w_qkv, 3, axis=-1)
        q = rms_norm(q.reshape(B, n, NA_HEADS, NA_HEAD_DIM), q_gain) * scale
        k = rms_norm(k.reshape(B, n, NA_HEADS, NA_HEAD_DIM), k_gain)
        return q, k, v.reshape(B, n, NA_HEADS, NA_HEAD_DIM)

    q_c, k_c, v_c = qkv(h_ctx)
    q_l, k_l, v_l = qkv(h_lat)

    out_ctx = None
    if need_ctx_out:
        s = jnp.einsum('bqhd,bkhd->bhqk', q_c, k_c)
        p = jax.nn.softmax(s.astype(jnp.float32), axis=-1).astype(v_c.dtype)
        o_c = jnp.einsum('bhqk,bkhd->bqhd', p, v_c)
        out_ctx = o_c.reshape(B, h_ctx.shape[1], D_MODEL) @ w_o

    grid = lambda a: a.reshape(B, rows, GRID_W, NA_HEADS, NA_HEAD_DIM)
    q_g, k_g, v_g = grid(q_l), grid(k_l), grid(v_l)
    row_start = jnp.clip(jnp.arange(rows) - kh // 2, 0, rows - kh)
    cols = jnp.arange(GRID_W)
    col_idx = jnp.clip(cols - WIN_W // 2, 0, GRID_W - WIN_W)[:, None] + jnp.arange(WIN_W)
    rpb_x = rpb[:, :, col_idx - cols[:, None] + (WIN_W - 1)]
    n_loc = kh * WIN_W

    def row_block(r):
        rs = row_start[r]
        q_row = lax.dynamic_index_in_dim(q_g, r, axis=1, keepdims=False)
        k_win = lax.dynamic_slice_in_dim(k_g, rs, kh, axis=1)[:, :, col_idx]
        v_win = lax.dynamic_slice_in_dim(v_g, rs, kh, axis=1)[:, :, col_idx]
        bias = rpb_x[:, rs + jnp.arange(kh) - r + (WIN_H - 1)]
        s_loc = jnp.einsum('bqhd,bjqwhd->bhqjw', q_row, k_win) + bias.transpose(0, 2, 1, 3)[None]
        s_ctx = jnp.einsum('bqhd,bkhd->bhqk', q_row, k_c)
        s = jnp.concatenate([s_loc.reshape(B, NA_HEADS, GRID_W, n_loc), s_ctx], axis=-1)
        p = jax.nn.softmax(s.astype(jnp.float32), axis=-1).astype(v_win.dtype)
        p_loc = p[..., :n_loc].reshape(B, NA_HEADS, GRID_W, kh, WIN_W)
        return (jnp.einsum('bhqjw,bjqwhd->bqhd', p_loc, v_win)
                + jnp.einsum('bhqk,bkhd->bqhd', p[..., n_loc:], v_c))

    o = lax.map(row_block, jnp.arange(rows))
    out_lat = o.transpose(1, 0, 2, 3, 4).reshape(B, T, D_MODEL) @ w_o
    return out_lat, out_ctx

def forget_gate(f_pre, lb):
    f32 = f_pre.astype(jnp.float32)
    log_f = jnp.logaddexp(jnp.log(lb), jnp.log1p(-lb) + jax.nn.log_sigmoid(f32))
    k = (1.0 - lb) * jax.nn.sigmoid(-f32)
    return k.astype(f_pre.dtype), log_f

def chunked_gated_scan(q, k, v, log_f, s0):
    B, N, H, _ = q.shape
    dv = v.shape[-1]
    nc = N // CHUNK
    chunks = lambda a: a.reshape(B, nc, CHUNK, H, a.shape[-1]).transpose(1, 0, 3, 2, 4)
    lower = jnp.tril(jnp.ones((CHUNK, CHUNK), dtype=bool))[:, :, None]

    def step(S, xs):
        qc, kc, vc, gc = xs
        b = jnp.cumsum(gc, axis=2)
        decay = jnp.exp(jnp.where(lower, b[:, :, :, None, :] - b[:, :, None, :, :], -jnp.inf))
        a = jnp.einsum('bhtk,bhtsk,bhsk->bhts', qc, decay, kc)
        o = jnp.einsum('bhts,bhsv->bhtv', a, vc) + jnp.einsum('bhtk,bhkv->bhtv', qc * jnp.exp(b), S)
        b_end = b[:, :, -1]
        S_new = (jnp.exp(b_end)[..., None] * S
                 + jnp.einsum('bhsk,bhsv->bhkv', kc * jnp.exp(b_end[:, :, None] - b), vc))
        return S_new, o

    s_fin, o = lax.scan(step, s0, (chunks(q), chunks(k), chunks(v), chunks(log_f)))
    return o.transpose(1, 0, 3, 2, 4).reshape(B, N, H, dv).astype(v.dtype), s_fin

def hgrn2_mixer(h_lat, h_ctx, w_in, lb, norm_g, w_o, need_ctx_out):
    B = h_lat.shape[0]
    splits = [HG_FDIM, HG_FDIM + D_MODEL, HG_FDIM + 2 * D_MODEL, 2 * HG_FDIM + 2 * D_MODEL]

    def project(h):
        n = h.shape[1]
        q, v, g, f_fwd, f_bwd = jnp.split(h @ w_in, splits, axis=-1)
        heads = lambda a: a.reshape(B, n, HG_HEADS, -1)
        return heads(jax.nn.silu(q)), heads(v), g, heads(f_fwd), heads(f_bwd)

    def bidirectional(q, v, f_fwd, f_bwd, s_fwd, s_bwd):
        k_f, lf_f = forget_gate(f_fwd, lb[0])
        k_b, lf_b = forget_gate(f_bwd, lb[1])
        o_f, s_fwd = chunked_gated_scan(q, k_f, v, lf_f, s_fwd)
        o_b, s_bwd = chunked_gated_scan(q[:, ::-1], k_b[:, ::-1], v[:, ::-1], lf_b[:, ::-1], s_bwd)
        return o_f + o_b[:, ::-1], s_fwd, s_bwd

    def readout(o, g):
        n = o.shape[1]
        return (rms_norm(o, norm_g).reshape(B, n, D_MODEL) * jax.nn.silu(g)) @ w_o

    zero = jnp.zeros((B, HG_HEADS, HG_EXPAND, HG_HEAD_V), jnp.float32)
    q_c, v_c, g_c, ff_c, fb_c = project(h_ctx)
    o_c, s_fwd, s_bwd = bidirectional(q_c, v_c, ff_c, fb_c, zero, zero)
    q_l, v_l, g_l, ff_l, fb_l = project(h_lat)
    o_l, _, _ = bidirectional(q_l, v_l, ff_l, fb_l, s_fwd, s_bwd)
    out_lat = readout(o_l, g_l)
    out_ctx = readout(o_c, g_c) if need_ctx_out else None
    return out_lat, out_ctx

def second_inputs(seed: int = 0) -> dict:
    key = jax.random.key(seed)
    ks = jax.random.split(key, 20)
    f32 = jnp.float32

    def w(k, shape, fan_in):
        return jax.random.normal(k, shape, f32) * fan_in ** -0.5

    def gain(k, shape):
        return 1.0 + 0.02 * jax.random.normal(k, shape, f32)

    return {
        'x': jax.random.normal(ks[0], (BATCH, SEQ, D_MODEL), f32),
        'c': jax.random.normal(ks[1], (BATCH, D_MODEL), f32),
        'ctx': jax.random.normal(ks[2], (BATCH, CTX_LEN, D_MODEL), f32),
        'c_ctx': jax.random.normal(ks[3], (D_MODEL,), f32),
        'ada_w': w(ks[4], (DEPTH, D_MODEL, 6 * D_MODEL), D_MODEL),
        'ada_b': 0.02 * jax.random.normal(ks[5], (DEPTH, 6 * D_MODEL), f32),
        'norm1_g': gain(ks[6], (DEPTH, D_MODEL)),
        'norm2_g': gain(ks[7], (DEPTH, D_MODEL)),
        'na_w_qkv': w(ks[8], (N_NA_LAYERS, D_MODEL, 3 * D_MODEL), D_MODEL),
        'na_w_o': w(ks[9], (N_NA_LAYERS, D_MODEL, D_MODEL), D_MODEL),
        'na_q_gain': gain(ks[10], (N_NA_LAYERS, NA_HEAD_DIM)),
        'na_k_gain': gain(ks[11], (N_NA_LAYERS, NA_HEAD_DIM)),
        'na_rpb': 0.2 * jax.random.normal(ks[12], (N_NA_LAYERS, NA_HEADS, 2 * WIN_H - 1, 2 * WIN_W - 1), f32),
        'hg_w_in': w(ks[13], (N_HG_LAYERS, D_MODEL, 3 * HG_FDIM + 2 * D_MODEL), D_MODEL),
        'hg_lower': 0.5 * jax.random.normal(ks[14], (DEPTH, 2, HG_FDIM), f32),
        'hg_norm_g': gain(ks[15], (N_HG_LAYERS, HG_HEAD_V)),
        'hg_w_o': w(ks[16], (N_HG_LAYERS, D_MODEL, D_MODEL), D_MODEL),
        'ffn_w_in': w(ks[17], (DEPTH, D_MODEL, 2 * D_FF_2), D_MODEL),
        'ffn_w_out': w(ks[18], (DEPTH, D_FF_2, D_MODEL), D_FF_2),
    }

def second_block(x, c, ctx, c_ctx, ada_w, ada_b, norm1_g, norm2_g, na_w_qkv, na_w_o, na_q_gain,
              na_k_gain, na_rpb, hg_w_in, hg_lower, hg_norm_g, hg_w_o, ffn_w_in, ffn_w_out):
    lbs = jnp.cumsum(jax.nn.softmax(hg_lower.astype(jnp.float32), axis=0), axis=0)
    lbs = (lbs - lbs[:1]).reshape(DEPTH, 2, HG_HEADS, HG_EXPAND)
    x_lat, x_ctx = x, ctx
    for i in range(DEPTH):
        last = i == DEPTH - 1
        j = i // N_MIXERS
        sh1, sc1, g1, sh2, sc2, g2 = [m[:, None, :] for m in ada_mod(c, ada_w[i], ada_b[i])]
        csh1, csc1, cg1, csh2, csc2, cg2 = ada_mod(c_ctx, ada_w[i], ada_b[i])
        h_lat = rms_norm(x_lat, norm1_g[i]) * (1 + sc1) + sh1
        h_ctx = rms_norm(x_ctx, norm1_g[i]) * (1 + csc1) + csh1
        if i % N_MIXERS == 0:
            out_lat, out_ctx = na_mixer(h_lat, h_ctx, na_w_qkv[j], na_w_o[j], na_q_gain[j],
                                        na_k_gain[j], na_rpb[j], not last)
        else:
            out_lat, out_ctx = hgrn2_mixer(h_lat, h_ctx, hg_w_in[j], lbs[i], hg_norm_g[j],
                                           hg_w_o[j], not last)
        x_lat = x_lat + g1 * out_lat
        x_lat = x_lat + g2 * swiglu(rms_norm(x_lat, norm2_g[i]) * (1 + sc2) + sh2, ffn_w_in[i], ffn_w_out[i])
        if not last:
            x_ctx = x_ctx + cg1 * out_ctx
            x_ctx = x_ctx + cg2 * swiglu(rms_norm(x_ctx, norm2_g[i]) * (1 + csc2) + csh2,
                                         ffn_w_in[i], ffn_w_out[i])
    return x_lat


def setup_inputs(seed=0):
    out = dict(first_inputs(seed))
    for name, value in second_inputs(seed + 1).items():
        if name != "x":
            out[name + "_2"] = value
    return out


def reference(
    x, positions, norm1_g, w_in, ssd_conv_w, ssd_conv_b, ssd_dt_bias, ssd_a_log, ssd_d,
    ssd_norm_g, mla_q_norm_g, mla_w_uq, mla_kv_norm_g, mla_w_ukv, gdn_conv_w, gdn_dt_bias,
    gdn_a_log, gdn_norm_g, w_ssd_out, w_mla_out, w_gdn_out, w_out, norm2_g, w_up, w_down,
    final_norm_g, c_2, ctx_2, c_ctx_2, ada_w_2, ada_b_2, norm1_g_2, norm2_g_2, na_w_qkv_2,
    na_w_o_2, na_q_gain_2, na_k_gain_2, na_rpb_2, hg_w_in_2, hg_lower_2, hg_norm_g_2, hg_w_o_2,
    ffn_w_in_2, ffn_w_out_2,
):
    x = first_block(
        x, positions, norm1_g, w_in, ssd_conv_w, ssd_conv_b, ssd_dt_bias, ssd_a_log, ssd_d,
        ssd_norm_g, mla_q_norm_g, mla_w_uq, mla_kv_norm_g, mla_w_ukv, gdn_conv_w, gdn_dt_bias,
        gdn_a_log, gdn_norm_g, w_ssd_out, w_mla_out, w_gdn_out, w_out, norm2_g, w_up, w_down,
        final_norm_g,
    )
    return second_block(
        x, c_2, ctx_2, c_ctx_2, ada_w_2, ada_b_2, norm1_g_2, norm2_g_2, na_w_qkv_2, na_w_o_2,
        na_q_gain_2, na_k_gain_2, na_rpb_2, hg_w_in_2, hg_lower_2, hg_norm_g_2, hg_w_o_2,
        ffn_w_in_2, ffn_w_out_2,
    )


_drawn_inputs = setup_inputs


def setup_inputs(seed=0):
    import zlib

    import numpy as np

    out = dict(_drawn_inputs(seed))
    spreads = {}
    factors = {'ssd_conv_b': 5.538,
     'ssd_d': 5.605,
     'ssd_norm_g': 3.997,
     'mla_q_norm_g': 8.0,
     'mla_kv_norm_g': 8.0,
     'gdn_norm_g': 7.365,
     'norm1_g_2': 6.145,
     'norm2_g_2': 3.082,
     'na_q_gain_2': 8.0,
     'na_k_gain_2': 8.0,
     'na_rpb_2': 7.372,
     'hg_lower_2': 6.313,
     'hg_norm_g_2': 8.0}
    for name, (base, spread) in spreads.items():
        noise = np.random.default_rng([zlib.crc32(name.encode()), seed]).standard_normal(out[name].shape)
        drawn = base * np.exp(spread * noise) if base else spread * noise
        out[name] = jnp.asarray(drawn.astype(out[name].dtype))
    for name, factor in factors.items():
        out[name] = (out[name] * factor).astype(out[name].dtype)
    return out
```

```python
import numpy as np
import concourse.bass as bass
from concourse import mybir
from contextlib import ExitStack

F32 = mybir.dt.float32
I32 = mybir.dt.int32
ALU = mybir.AluOpType
ACT = mybir.ActivationFunctionType
AX = mybir.AxisListType

EPS = 1e-6
T = 256
NEG = -1e30
RING = 3
SLOT = 4096
MAGIC = 12582912.0
TWO_PI_1 = 6.28125
TWO_PI_2 = 0.0019350051879882812
TWO_PI_3 = 3.019916050356e-07

MATS = {
    "win": (1024, 9728, 512), "wsm": (1024, 32, 32), "wuq": (512, 1536, 768), "wuk": (256, 1024, 1024),
    "wuv": (256, 1024, 1024), "wso": (1024, 1024, 512), "wmo": (1024, 1024, 512), "wgo": (1024, 1024, 512),
    "wo": (1024, 1024, 512), "wup": (1024, 4096, 512), "wdn": (4096, 1024, 128),
    "ada": (1024, 6144, 512), "nqkv": (1024, 3072, 512), "no": (1024, 1024, 512), "hin": (1024, 5120, 512),
    "ho": (1024, 1024, 512), "fi": (1024, 5632, 512), "fo": (2816, 1024, 128),
}

CONSTS = ["ident", "ones", "tri", "bd64", "btri", "bstrict", "cone0", "cone1", "m0", "causal",
          "t0", "t1", "t2", "t3", "t4", "t5"]
VEC1 = {"n1": 8, "n2": 8, "cw": 48, "cb": 12, "gw": 64, "qn": 4, "kn": 2, "sn": 8, "gn": 1, "sd": 8,
        "bias": 24, "alog": 24, "fn": 8, "inv": 1}
VEC2 = {"adab": 48, "n1": 8, "n2": 8, "qg": 1, "kg": 1, "hl": 32, "hn": 1}


def offsets(table):
    out, at = {}, 0
    for k, n in table.items():
        out[k] = (at, at + n)
        at += n
    return out, at


class Queue:

    def __init__(self, sem):
        self.sem, self.items, self.n, self.held = sem, [], 0, []

    def __call__(self, fn, waits, signal=True):
        waits = [*self.held, *waits]
        self.held = []
        self.items.append((fn, waits, signal))
        if signal:
            self.n += 1
        return (self.sem, self.n)

    def here(self):
        return (self.sem, self.n)

    def play(self, eng):
        seen = {}
        for fn, waits, signal in self.items:
            for sem, value in waits:
                if value > seen.get(sem.num, 0):
                    eng.wait_ge(sem, value)
                    seen[sem.num] = value
            i = fn(eng)
            if signal:
                i.then_inc(self.sem, 1)


class Elementwise(Queue):
    def tt(self, out, a, b, op, *w):
        return self(lambda e: e.tensor_tensor(out, a, b, op), w)

    def ts(self, out, a, s1, s2, op0, op1, *w):
        if op1 is None:
            return self(lambda e: e.tensor_scalar(out, a, s1, None, op0), w)
        return self(lambda e: e.tensor_scalar(out, a, s1, s2, op0, op1), w)

    def stt(self, out, a, s, b, op0, op1, *w):
        return self(lambda e: e.scalar_tensor_tensor(out=out, in0=a, scalar=s, in1=b, op0=op0, op1=op1), w)

    def cp(self, out, a, *w):
        return self(lambda e: e.tensor_copy(out, a), w)

    def red(self, out, a, op, *w):
        return self(lambda e: e.tensor_reduce(out, a, AX.X, op), w)

    def recip(self, out, a, *w):
        return self(lambda e: e.reciprocal(out, a), w)

    def fill(self, out, v, *w):
        return self(lambda e: e.memset(out, v), w)

    def scan(self, out, a, b, *w):
        return self(lambda e: e.tensor_tensor_scan(out, a, b, 0.0, ALU.mult, ALU.add), w)

    def pick(self, out, mask, data, *w):
        return self(lambda e: e.copy_predicated(out, mask, data), w)


class Scalar(Queue):
    def act(self, out, a, func, *w, bias=None, scale=1.0, acc=None):
        def fn(e):
            kw = {}
            if bias is not None:
                kw["bias"] = bias
            if acc is not None:
                kw["accum_out"] = acc
            return e.activation(out, a, func, scale=scale, **kw)
        return self(fn, w)

    def cp(self, out, a, *w):
        return self(lambda e: e.activation(out, a, ACT.Copy), w)


class Tensor(Queue):
    def mm(self, parts, *w):
        for i, (out, l, r, start, stop) in enumerate(parts):
            t = self(lambda e, o=out, l=l, r=r, s=start, p=stop: e.matmul(o, l, r, start=s, stop=p),
                     w if i == 0 else (), signal=i == len(parts) - 1)
        return t

    def tr(self, parts, ident, *w):
        for i, (out, a) in enumerate(parts):
            t = self(lambda e, o=out, a=a: e.transpose(o, a, ident), w if i == 0 else (),
                     signal=i == len(parts) - 1)
        return t


class Machine:
    def __init__(self, nc, ctx, d):
        self.nc, self.ctx, self.d = nc, ctx, d
        self.pe, self.dv, self.ac, self.po = (
            c(self.sem(n)) for c, n in ((Tensor, "pe"), (Elementwise, "dv"), (Scalar, "ac"), (Elementwise, "po")))
        self.sp = Queue(self.sem("sp"))
        self.spseen = []
        self.ps = self.pb("ps", [128, 8, 512])
        self.bfree = [[] for _ in range(8)]
        self.bheld = [False] * 8
        self.bi = 0
        self.ring = [self.sb(f"ring{i}", [128, SLOT]) for i in range(RING)]
        self.rsem = [self.sem(f"ring{i}") for i in range(RING)]
        self.rfree = [[] for _ in range(RING)]
        self.rheld = [False] * RING
        self.rn = 0
        self.plan = []
        self.loaded = {}
        self.flip = 0
        self.extra = []

    def sem(self, n):
        return self.ctx.enter_context(self.nc.semaphore("s_" + n))

    def sb(self, n, shape, dt=F32):
        return self.ctx.enter_context(self.nc.sbuf_tensor(n, shape, dt))

    def pb(self, n, shape):
        return self.ctx.enter_context(self.nc.psum_tensor(n, shape, F32))

    def bank(self):
        b = self.bi
        self.bi = (b + 1) % 8
        assert not self.bheld[b]
        self.bheld[b] = True
        return b, self.bfree[b]

    def give(self, b, *tokens):
        self.bfree[b] = list(tokens)
        self.bheld[b] = False

    def barrier(self):
        now = [q.here() for q in (self.pe, self.dv, self.ac, self.po)]
        for q in (self.pe, self.dv, self.ac, self.po):
            q.held = list(now)
        self.extra = list(now)

    def dma(self, out, src, sem, waits=(), count=[0]):
        self.sp.items.append((lambda e: e.dma_start(out, src).then_inc(sem, 16), list(waits), False))

    def weight(self, name, layer, c):
        s = self.rn % RING
        use = self.rn // RING + 1
        self.rn += 1
        assert not self.rheld[s]
        self.rheld[s] = True
        k, _, cols = MATS[name]
        kt = k // 128
        ap = self.ring[s][:, 0:kt * cols]
        self.dma(ap, self.d[name][layer, c], self.rsem[s], self.rfree[s])
        return ap.rearrange("p (k n) -> p k n", k=kt), (self.rsem[s], 16 * use), s

    def done(self, s, token):
        self.rfree[s] = [token]
        self.rheld[s] = False

    def lin(self, name, layer, chunks, x, n, evac, *w):
        kt = MATS[name][0] // 128
        tiles = MATS[name][2] // 128
        per = 512 // n
        at = 0
        for c in chunks:
            wt, tok, s = self.weight(name, layer, c)
            for g in range(0, tiles, per):
                m = min(per, tiles - g)
                b, fr = self.bank()
                parts = [(self.ps[:, b, j * n:(j + 1) * n], wt[:, k, (g + j) * 128:(g + j + 1) * 128], x[:, k, 0:n],
                          k == 0, k == kt - 1) for j in range(m) for k in range(kt)]
                t = self.pe.mm(parts, tok, *fr, *w)
                out = self.ps[:, b, 0:m * n].rearrange("p (a n) -> p a n", a=m)
                self.give(b, *evac(at + g, m, out, t))
            self.done(s, t)
            at += tiles

    def lint(self, name, layer, chunks, x, blocks, evac, *w):
        kt = MATS[name][0] // 128
        cols = MATS[name][2]
        at = 0
        for c in chunks:
            wt, tok, s = self.weight(name, layer, c)
            for m in range(blocks):
                for c0 in range(0, cols, 512):
                    n = min(512, cols - c0)
                    b, fr = self.bank()
                    t = self.pe.mm([(self.ps[:, b, 0:n], x[:, k, m * 128:m * 128 + 128], wt[:, k, c0:c0 + n],
                                     k == 0, k == kt - 1) for k in range(kt)], tok, *fr, *w)
                    self.give(b, *evac(m, at + c0, self.ps[:, b, 0:n], t))
            self.done(s, t)
            at += cols

    def copy(self, out, src, *w):
        self.flip ^= 1
        return self.ac.cp(out, src, *w) if self.flip else self.dv.cp(out, src, *w)

    def stats(self, src, nt, per, n, inv, lhs, rs, sq, eps, *w):
        t = self.ac.act(sq[:, 0:nt, 0:n], src, ACT.Square, *w)
        groups = nt // per
        pb = 512 // n
        for g in range(0, groups, pb):
            m = min(pb, groups - g)
            b, fr = self.bank()
            tm = self.pe.mm([(self.ps[:, b, j * n:(j + 1) * n], lhs, sq[:, (g + j) * per + k, 0:n], k == 0,
                              k == per - 1) for j in range(m) for k in range(per)], t, *fr)
            o = rs[:, g:g + m, 0:n]
            t1 = self.ac.act(o, self.ps[:, b, 0:m * n].rearrange("p (a n) -> p a n", a=m), ACT.Ln, tm,
                             bias=eps, scale=inv)
            self.give(b, t1)
            last = self.ac.act(o, o, ACT.Exp, t1, scale=-0.5)
        return last


def bc(ap, shape):
    return ap.to_broadcast(shape)


class Arena:
    def __init__(self, tensor):
        self.t, self.at, self.top, self.marks = tensor, 0, 0, []

    def __call__(self, *dims):
        n = int(np.prod(dims))
        ap = self.t[:, self.at:self.at + n]
        self.at += n
        assert self.at <= self.t.shape[1], (self.at, self.t.shape)
        self.top = max(self.top, self.at)
        names = "abcd"[:len(dims)]
        if len(dims) == 1:
            return ap
        return ap.rearrange(f"p ({' '.join(names)}) -> p {' '.join(names)}", **{names[i]: dims[i] for i in range(len(dims))})


def first_block(M, A, S):
    pe, dv, ac, po, ps = M.pe, M.dv, M.ac, M.po, M.ps
    C, x = S["c"], S["x"]
    ident = C["ident"]
    ones = C["ones"]
    one = ones[:, 0:1]
    eps = S["eps"]
    tx = S["tx"]

    base = A.at
    ang, kk, r, pos = A(T), A(T), A(T), A(T)
    v0, _ = S["vec1"]
    t = dv.cp(pos, S["pos"], *tx)
    t = dv.ts(ang, pos, v0["inv"], None, ALU.mult, None, t)
    tabs = []
    for tab, shift in ((S["cos"], 0.25), (S["sin"], 0.0)):
        t = dv.ts(kk, ang, 0.15915494309189535, shift, ALU.mult, ALU.add, t)
        t = dv.ts(kk, kk, MAGIC, None, ALU.add, None, t)
        t = dv.ts(kk, kk, MAGIC, None, ALU.subtract, None, t)
        t = dv.stt(r, kk, -TWO_PI_1, ang, ALU.mult, ALU.add, t)
        t = dv.stt(r, kk, -TWO_PI_2, r, ALU.mult, ALU.add, t)
        t = dv.stt(r, kk, -TWO_PI_3, r, ALU.mult, ALU.add, t)
        if shift:
            t = dv.ts(r, r, 1.5707963267948966, None, ALU.add, None, t)
        t = dv.ts(r, r, 3.1415925, -3.1415925, ALU.min, ALU.max, t)
        t = ac.act(tab, r, ACT.Sin, t)
        tabs.append(t)
    A.at = base
    M.barrier()

    for layer in range(2):
        V, tv = S["vec1"] if layer == 0 else S["vec1b"]
        base = A.at
        xn, mixed, gate, y, sq = (A(8, T) for _ in range(5))
        rs = A(8, T)
        keep = A.at

        def normed(src, dst, nt, inv, gain, lhs, w):
            t = M.stats(src, nt, nt, T, inv, lhs, rs, sq, eps, *w)
            t = dv.tt(dst, src, bc(rs[:, 0:1, :], [128, nt, T]), ALU.mult, t)
            return dv.tt(dst, dst, bc(gain.unsqueeze(2), [128, nt, T]), ALU.mult, t)

        txn = normed(x, xn, 8, 1 / 1024, V["n1"], ones, [*tx, *tv])

        def branch_out(yop, ty, wname, gchunk, first):
            def eg(i, m, p, t):
                return [ac.act(gate[:, i:i + m, :], p, ACT.Sigmoid, t)]
            M.lin("win", layer, [gchunk, gchunk + 1], xn, T, eg, txn)
            tg = ac.here()

            def eo(i, m, p, t):
                if first:
                    return [dv.tt(mixed[:, i:i + m, :], p, gate[:, i:i + m, :], ALU.mult, t, tg)]
                t1 = dv.tt(gate[:, i:i + m, :], p, gate[:, i:i + m, :], ALU.mult, t, tg)
                dv.tt(mixed[:, i:i + m, :], mixed[:, i:i + m, :], gate[:, i:i + m, :], ALU.add, t1)
                return [t1]
            M.lin(wname, layer, [0, 1], yop, T, eo, ty)

        def conv(src, dst, nt, wname, w):
            for i in range(nt):
                wv = V[wname]
                t = dv.ts(dst[:, i, :], src[:, i, 0:T], wv[:, 4 * i:4 * i + 1], None, ALU.mult, None, *w)
                for j in range(1, 4):
                    t = dv.stt(dst[:, i, :], src[:, i, j:j + T], wv[:, 4 * i + j:4 * i + j + 1], dst[:, i, :],
                               ALU.mult, ALU.add, t)
            return t

        sm, sp, sa, sb_, sc = A(2, 32), A(2, 24), A(2, 24), A(2, 24), A(2, 24)
        smask = A(48)
        beta, dA, cum = A(2, 8), A(2, 24), A(2, 24)
        tot, etot = A(5, 16), A(5, 16)
        keep = A.at
        M.lint("wsm", layer, [0], xn, 2, lambda m, c0, p, t: [ac.cp(sm[:, m, :], p, t)], txn)
        t = dv.tt(sp, sm[:, :, 0:24], bc(V["bias"].unsqueeze(1), [128, 2, 24]), ALU.add, ac.here())
        ta = ac.act(sa, sp, ACT.Abs, t)
        te = ac.act(sa, sa, ACT.Exp, ta, scale=-1.0)
        tl = ac.act(sb_, sa, ACT.Ln, te, bias=one)
        t = dv.ts(sc, sa, 1 / 3, -0.5, ALU.mult, ALU.add, te)
        t = dv.tt(sc, sc, sa, ALU.mult, t)
        t = dv.stt(sc, sc, 1.0, sa, ALU.add, ALU.mult, t)
        tk = dv.ts(smask.rearrange("p (a b) -> p a b", a=2), sa, 0.01, None, ALU.is_lt, None, te)
        t = dv.pick(sb_.rearrange("p a b -> p (a b)"), smask.bitcast(I32), sc.rearrange("p a b -> p (a b)"), t, tk, tl)
        t = dv.stt(sp, sp, 0.0, sb_, ALU.max, ALU.add, t)
        ta = ac.act(sc[:, 0, :], V["alog"], ACT.Exp, t)
        t = dv.stt(dA, sp, -1.0, bc(sc[:, 0:1, :], [128, 2, 24]), ALU.mult, ALU.mult, t, ta)
        tb = ac.act(beta, sm[:, :, 24:32], ACT.Sigmoid)
        b, fr = M.bank()
        P = ps[:, b, 0:48].rearrange("p (a b) -> p a b", a=2)
        Q = ps[:, b, 64:144].rearrange("p (a b) -> p a b", a=5)
        parts = []
        for c in range(2):
            parts += [(P[:, c, 0:16], C["tri"], dA[:, c, 0:16], True, True),
                      (P[:, c, 16:24], C["btri"], dA[:, c, 16:24], True, True),
                      (Q[:, 2 * c, 0:8], C["cone0"], dA[:, c, 16:24], True, True),
                      (Q[:, 2 * c + 1, 0:8], C["cone1"], dA[:, c, 16:24], True, True)]
        parts += [(Q[:, 4, 0:16], ones, dA[:, 0, 0:16], True, True)]
        tm = pe.mm(parts, t, *fr)
        t1 = ac.cp(cum, P, tm)
        t2 = ac.cp(tot[:, 0:4, 0:8], Q[:, 0:4, 0:8], tm)
        t3 = ac.cp(tot[:, 4, :], Q[:, 4, :], tm)
        t4 = ac.act(etot[:, 0:4, 0:8], Q[:, 0:4, 0:8], ACT.Exp, tm)
        M.give(b, t4)
        ts_ = [t4, tb, t]

        acc = A(16, T)
        z = A(8, T)
        top = A.at
        pad = A(16, T + 3)
        tz = po.fill(pad[:, :, 0:3], 0.0)
        M.lin("win", layer, range(0, 4), xn, T,
              lambda i, m, p, t: [M.copy(pad[:, i:i + m, 3:3 + T], p, t)], txn)
        tp = [tz, ac.here(), dv.here()]
        t = conv(pad, acc, 16, "gw", tp)
        tsl = ac.act(acc, acc, ACT.Silu, t)
        M.lin("win", layer, range(11, 13), xn, T, lambda i, m, p, t: [ac.act(z[:, i:i + m, :], p, ACT.Silu, t)], txn)
        tzz = ac.here()
        A.at = top
        t = M.stats(acc[:, 0:8, :], 8, 1, T, 1.0, ones, rs, sq, eps, tsl)
        tq = dv.stt(acc[:, 0:4, :], acc[:, 0:4, :], 128 ** -0.5, rs[:, 0:4, :], ALU.mult, ALU.mult, t)
        tk = dv.tt(acc[:, 4:8, :], acc[:, 4:8, :], rs[:, 4:8, :], ALU.mult, t)
        qT, kT, vT = acc[:, 0:4, :], acc[:, 4:8, :], acc[:, 8:16, :]
        M.barrier()
        ktok, vtok = A(2, 4, 128), A(2, 8, 128)
        qkT, qg = A(16, 128), A(8, T)
        AT, X, XT = (A(16, 128) for _ in range(3))
        Y = mixed.rearrange("p a (b c) -> p (a b) c", c=128)
        BT = gate.rearrange("p a (b c) -> p (a b) c", c=128)
        u, wT = X, BT
        for c in range(2):
            cs = slice(c * 128, c * 128 + 128)
            b, fr = M.bank()
            t = pe.tr([(ps[:, b, h * 128:h * 128 + 128], kT[:, h, cs]) for h in range(4)], ident, tk, *fr)
            M.give(b, M.copy(ktok[:, c, :, :].rearrange("p a b -> p (a b)"), ps[:, b, :], t))
            for g in range(2):
                b, fr = M.bank()
                t = pe.tr([(ps[:, b, h * 128:h * 128 + 128], vT[:, 4 * g + h, cs]) for h in range(4)], ident, tsl, *fr)
                M.give(b, dv.tt(vtok[:, c, 4 * g:4 * g + 4, :], ps[:, b, :].rearrange("p (a b) -> p a b", a=4),
                                bc(beta[:, c, 4 * g:4 * g + 4].unsqueeze(2), [128, 4, 128]), ALU.mult, t, tb))
        for c in range(2):
            cs = slice(c * 128, c * 128 + 128)
            for g in range(2):
                p0 = c * 8 + 4 * g
                b, fr = M.bank()
                t = pe.mm([(ps[:, b, j * 128:j * 128 + 128], bc(dA[:, c, 16 + 4 * g + j:17 + 4 * g + j], [128, 128]),
                            C["btri"], True, True) for j in range(4)], *ts_, *fr)
                P = ps[:, b, :].rearrange("p (a b) -> p a b", a=4)
                D = Y[:, p0:p0 + 4, :]
                te = ac.act(qg[:, 4 * g:4 * g + 4, cs], P, ACT.Exp, t)
                t1 = dv.tt(D, P, bc(cum[:, c, 16 + 4 * g:20 + 4 * g].unsqueeze(2), [128, 4, 128]), ALU.subtract, t, te)
                M.give(b, te, t1)
                t1 = dv.ts(D, D, 0.0, None, ALU.min, None, t1)
                td = ac.act(D, D, ACT.Exp, t1)
                qv = qT[:, 2 * g:2 * g + 2, cs].unsqueeze(2)
                t1 = dv.tt(qg[:, 4 * g:4 * g + 4, cs].rearrange("p (a r) t -> p a r t", r=2),
                           qg[:, 4 * g:4 * g + 4, cs].rearrange("p (a r) t -> p a r t", r=2),
                           bc(qv, [128, 2, 2, 128]), ALU.mult, te)
                b, fr = M.bank()
                parts = []
                for j in range(2):
                    h = 2 * g + j
                    parts += [(ps[:, b, j * 256:j * 256 + 128], kT[:, h, cs], kT[:, h, cs], True, True),
                              (ps[:, b, j * 256 + 128:j * 256 + 256], kT[:, h, cs], qT[:, h, cs], True, True)]
                t = pe.mm(parts, tq, tk, *fr)
                P = ps[:, b, :].rearrange("p (j w t) -> p j w t", j=2, w=2)
                D4 = D.rearrange("p (a r) t -> p a r t", r=2)
                t1 = dv.tt(AT[:, p0:p0 + 4, :].rearrange("p (a r) t -> p a r t", r=2), D4,
                           bc(P[:, :, 0:1, :], [128, 2, 2, 128]), ALU.mult, td, t)
                t2 = dv.tt(qkT[:, p0:p0 + 4, :].rearrange("p (a r) t -> p a r t", r=2), D4,
                           bc(P[:, :, 1:2, :], [128, 2, 2, 128]), ALU.mult, td, t)
                M.give(b, t1, t2)
                t2 = po.tt(qkT[:, p0:p0 + 4, :], qkT[:, p0:p0 + 4, :], bc(C["btri"].unsqueeze(1), [128, 4, 128]), ALU.mult, t2)
                t1 = dv.tt(AT[:, p0:p0 + 4, :], AT[:, p0:p0 + 4, :], bc(C["bstrict"].unsqueeze(1), [128, 4, 128]), ALU.mult, t1)
                b, fr = M.bank()
                t = pe.tr([(ps[:, b, j * 128:j * 128 + 128], AT[:, p0 + j, :]) for j in range(4)], ident, t1, *fr)
                A4 = BT[:, p0:p0 + 4, :]
                t = dv.tt(A4, ps[:, b, :].rearrange("p (a b) -> p a b", a=4),
                          bc(beta[:, c, 4 * g:4 * g + 4].unsqueeze(2), [128, 4, 128]), ALU.mult, t, tb)
                M.give(b, t)
                b, fr = M.bank()
                t1 = pe.tr([(ps[:, b, j * 128:j * 128 + 128], A4[:, j, :]) for j in range(4)], ident, t, *fr)
                t1 = ac.cp(AT[:, p0:p0 + 4, :], ps[:, b, :].rearrange("p (a b) -> p a b", a=4), t1)
                M.give(b, t1)
                idb = bc(ident.unsqueeze(1), [128, 4, 128])
                t = po.tt(X[:, p0:p0 + 4, :], A4, bc(C["m0"].unsqueeze(1), [128, 4, 128]), ALU.mult, t)
                t = po.tt(X[:, p0:p0 + 4, :], idb, X[:, p0:p0 + 4, :], ALU.subtract, t)
                t = po.tt(XT[:, p0:p0 + 4, :], AT[:, p0:p0 + 4, :], bc(C["t0"].unsqueeze(1), [128, 4, 128]), ALU.mult, t1)
                t = po.tt(XT[:, p0:p0 + 4, :], idb, XT[:, p0:p0 + 4, :], ALU.subtract, t)
        M.barrier()
        tX = [[] for _ in range(4)]
        tB = [[] for _ in range(4)]
        for lev in range(1, 6):
            for q in range(4):
                p0 = 4 * q
                s4 = slice(p0, p0 + 4)
                eng = po
                tb4 = eng.tt(BT[:, s4, :], AT[:, s4, :], bc(C[f"t{lev}"].unsqueeze(1), [128, 4, 128]), ALU.mult, *tB[q])
                b, fr = M.bank()
                t = pe.mm([(ps[:, b, j * 128:j * 128 + 128], BT[:, p0 + j, :], X[:, p0 + j, :], True, True)
                           for j in range(4)], tb4, *tX[q], *fr)
                tB[q] = [t]
                ty = ac.cp(Y[:, s4, :].rearrange("p a b -> p (a b)"), ps[:, b, :], t, *tX[q])
                M.give(b, ty)
                b2, fr2 = M.bank()
                t2 = pe.mm([(ps[:, b2, j * 128:j * 128 + 128], Y[:, p0 + j, :], XT[:, p0 + j, :], True, True)
                            for j in range(4)], ty, *fr2)
                if lev < 5:
                    b1, fr1 = M.bank()
                    t1 = pe.mm([(ps[:, b1, j * 128:j * 128 + 128], XT[:, p0 + j, :], Y[:, p0 + j, :], True, True)
                                for j in range(4)], ty, *fr1)
                    ta = dv.tt(X[:, s4, :], X[:, s4, :], ps[:, b1, :].rearrange("p (a b) -> p a b", a=4), ALU.subtract, t1)
                    M.give(b1, ta)
                    t2 = t1
                tc = dv.tt(XT[:, s4, :], XT[:, s4, :], ps[:, b2, :].rearrange("p (a b) -> p a b", a=4), ALU.subtract, t2)
                M.give(b2, tc)
                tX[q] = [tc, t2]
        M.barrier()
        kd, kbg = AT, Y
        eg = sc[:, :, 0:8]
        eb = sc[:, :, 8:16]
        ed = sc[:, :, 16:24]
        t = ac.act(eg, cum[:, :, 16:24], ACT.Exp)
        teb = dv.tt(eb, eg, beta, ALU.mult, t)
        for c in range(2):
            for half in range(2):
                hp = slice(64 * half, 64 * half + 64)
                t = dv.tt(ed[hp, c, :], tot[hp, 2 * c + half, 0:8], cum[hp, c, 16:24], ALU.subtract)
        ted = ac.act(ed, ed, ACT.Exp, t)
        for c in range(2):
            kv = bc(ktok[:, c, :, :].unsqueeze(2), [128, 4, 2, 128])
            for dst, s, tw, q in ((kbg, eb, teb, dv), (kd, ed, ted, dv)):
                sv = s[:, c, :].rearrange("p (a r) -> p a r", r=2).unsqueeze(3)
                tlast = q.tt(dst[:, 8 * c:8 * c + 8, :].rearrange("p (a r) t -> p a r t", r=2), kv,
                             bc(sv, [128, 4, 2, 128]), ALU.mult, tw)
        for q in range(4):
            c, g = q // 2, q % 2
            b, fr = M.bank()
            t = pe.mm([(ps[:, b, j * 128:j * 128 + 128], XT[:, 4 * q + j, :], vtok[:, c, 4 * g + j, :], True, True)
                       for j in range(4)], *fr)
            M.give(b, ac.cp(u[:, 4 * q:4 * q + 4, :].rearrange("p a b -> p (a b)"), ps[:, b, :], t))
            b, fr = M.bank()
            t = pe.mm([(ps[:, b, j * 128:j * 128 + 128], kbg[:, 4 * q + j, :], XT[:, 4 * q + j, :], True, True)
                       for j in range(4)], tlast, *fr)
            M.give(b, ac.cp(wT[:, 4 * q:4 * q + 4, :].rearrange("p a b -> p (a b)"), ps[:, b, :], t))
        tuw = ac.here()
        ST = XT[:, 0:8, :]
        tS = [[], []]
        o = y
        for n in range(4):
            c, half = n // 2, n % 2
            hp = slice(64 * half, 64 * half + 64)
            cols = slice(64 * n, 64 * n + 64)
            lc = slice(64 * half, 64 * half + 64)
            for g in range(2):
                p0 = 8 * c + 4 * g
                if n:
                    b, fr = M.bank()
                    t = pe.mm([(ps[:, b, j * 128:j * 128 + 128], wT[:, p0 + j, :], ST[:, 4 * g + j, :], True, True)
                               for j in range(4)], *tS[g], tuw, *fr)
                    tv_ = dv.tt(u[hp, p0:p0 + 4, :], u[hp, p0:p0 + 4, :],
                                ps[hp, b, :].rearrange("p (a b) -> p a b", a=4), ALU.subtract, t)
                    M.give(b, tv_)
                else:
                    tv_ = tuw
                b, fr = M.bank()
                parts = []
                for j in range(4):
                    oo = ps[:, b, j * 64:j * 64 + 64]
                    if n:
                        parts.append((oo, ST[:, 4 * g + j, :], qg[:, 4 * g + j, cols], True, False))
                    parts.append((oo, u[hp, p0 + j, :], qkT[hp, p0 + j, lc], n == 0, True))
                t = pe.mm(parts, tv_, *tS[g], *fr)
                M.give(b, ac.cp(o[:, 4 * g:4 * g + 4, cols], ps[:, b, 0:256].rearrange("p (a b) -> p a b", a=4), t))
                to = ac.here()
                if n < 3:
                    b, fr = M.bank()
                    t2 = pe.mm([(ps[:, b, j * 128:j * 128 + 128], kd[hp, p0 + j, :], u[hp, p0 + j, :], True, True)
                                for j in range(4)], tv_, tlast, *fr)
                    P = ps[:, b, :].rearrange("p (a b) -> p a b", a=4)
                    if n:
                        t1 = dv.tt(ST[:, 4 * g:4 * g + 4, :], ST[:, 4 * g:4 * g + 4, :],
                                   bc(etot[:, n, 4 * g:4 * g + 4].unsqueeze(2), [128, 4, 128]), ALU.mult, t)
                        t1 = dv.tt(ST[:, 4 * g:4 * g + 4, :], ST[:, 4 * g:4 * g + 4, :], P, ALU.add, t1, t2)
                    else:
                        t1 = dv.cp(ST[:, 4 * g:4 * g + 4, :], P, t2, tuw, pe.here())
                    M.give(b, t1)
                    tS[g] = [t1]
        t = M.stats(o, 8, 1, T, 1 / 128, ones, rs, sq, eps, to)
        t = dv.tt(o, o, rs, ALU.mult, t)
        ty = dv.stt(o, o, V["gn"], z, ALU.mult, ALU.mult, t, tzz)
        M.barrier()
        A.at = keep
        branch_out(o, ty, "wgo", 17, True)
        M.barrier()

        acc = A(12, T)
        z = A(8, T)
        top = A.at
        pad = A(12, T + 3)
        tz = po.fill(pad[:, :, 0:3], 0.0)
        M.lin("win", layer, range(4, 7), xn, T, lambda i, m, p, t: [M.copy(pad[:, i:i + m, 3:3 + T], p, t)], txn)
        t = conv(pad, acc, 12, "cw", [tz, ac.here(), dv.here()])
        t = dv.tt(acc, acc, bc(V["cb"].unsqueeze(2), [128, 12, T]), ALU.add, t)
        ta = ac.act(acc, acc, ACT.Silu, t)
        M.lin("win", layer, range(9, 11), xn, T, lambda i, m, p, t: [ac.act(z[:, i:i + m, :], p, ACT.Silu, t)], txn)
        M.barrier()
        A.at = top
        Xd, Xs, Bt, Hs = A(2, 1024), A(1024), A(2, 128), A(2, 512)
        CB, L, ytok = A(2, 2, 128), A(16, 128), A(1024)
        tl = ac.act(sc[:, 0, 0:16], cum[:, 0, 0:16], ACT.Identity, scale=-1.0)
        t = dv.tt(sc[:, 0, 0:16], sc[:, 0, 0:16], tot[:, 4, :], ALU.add, tl)
        tdec = ac.act(sc[:, 0, 0:16], sc[:, 0, 0:16], ACT.Exp, t)
        teA = ac.act(sc[:, 1, 0:16], cum[:, 1, 0:16], ACT.Exp)
        tL = []
        for c in range(2):
            cs = slice(c * 128, c * 128 + 128)
            txd = []
            for g in range(2):
                b, fr = M.bank()
                t = pe.tr([(ps[:, b, j * 128:j * 128 + 128], acc[:, 4 * g + j, cs]) for j in range(4)], ident, ta, *fr)
                t = dv.tt(Xd[:, c, 512 * g:512 * g + 512].rearrange("p (h d) -> p h d", d=64),
                          ps[:, b, :].rearrange("p (h d) -> p h d", d=64),
                          bc(sp[:, c, 8 * g:8 * g + 8].unsqueeze(2), [128, 8, 64]), ALU.mult, t)
                M.give(b, t)
                txd.append(t)
            b, fr = M.bank()
            t = pe.mm([(ps[:, b, g * 128:g * 128 + 128], acc[:, 8 + g, cs], acc[:, 10 + g, cs], True, True)
                       for g in range(2)], ta, *fr)
            tcb = dv.tt(CB[:, c, :, :], ps[:, b, 0:256].rearrange("p (a b) -> p a b", a=2),
                        bc(C["tri"].unsqueeze(1), [128, 2, 128]), ALU.mult, t)
            M.give(b, tcb)
            if c == 0:
                b, fr = M.bank()
                t = pe.tr([(ps[:, b, g * 128:g * 128 + 128], acc[:, 8 + g, cs]) for g in range(2)], ident, ta, *fr)
                tbt = ac.cp(Bt.rearrange("p a b -> p (a b)"), ps[:, b, 0:256], t)
                M.give(b, tbt)
                tx_ = dv.tt(Xs.rearrange("p (h d) -> p h d", d=64), Xd[:, 0, :].rearrange("p (h d) -> p h d", d=64),
                            bc(sc[:, 0, 0:16].unsqueeze(2), [128, 16, 64]), ALU.mult, tdec, *txd)
                for g in range(2):
                    b, fr = M.bank()
                    t = pe.mm([(ps[:, b, :], Bt[:, g, :], Xs[:, 512 * g:512 * g + 512], True, True)], tx_, tbt, *fr)
                    th = ac.cp(Hs[:, g, :], ps[:, b, :], t)
                    M.give(b, th)
            te = []
            for q in range(4):
                s4 = slice(4 * q, 4 * q + 4)
                b, fr = M.bank()
                t = pe.mm([(ps[:, b, j * 128:j * 128 + 128], bc(dA[:, c, 4 * q + j:4 * q + j + 1], [128, 128]),
                            C["tri"], True, True) for j in range(4)], *fr)
                t1 = dv.tt(L[:, s4, :], ps[:, b, :].rearrange("p (a b) -> p a b", a=4),
                           bc(cum[:, c, s4].unsqueeze(2), [128, 4, 128]), ALU.subtract, t, *tL)
                M.give(b, t1)
                t1 = dv.ts(L[:, s4, :], L[:, s4, :], 0.0, None, ALU.min, None, t1)
                t1 = ac.act(L[:, s4, :], L[:, s4, :], ACT.Exp, t1)
                te.append(dv.tt(L[:, s4, :], L[:, s4, :], bc(CB[:, c, q // 2:q // 2 + 1, :], [128, 4, 128]), ALU.mult, t1, tcb))
            tyt = []
            for g in range(2):
                b, fr = M.bank()
                t = pe.mm([(ps[:, b, 64 * h:64 * h + 64], L[:, 8 * g + h, :],
                            Xd[:, c, 512 * g + 64 * h:512 * g + 64 * h + 64], True, True) for h in range(8)],
                          *te, *txd, *fr)
                if c == 0:
                    t1 = ac.cp(ytok[:, 512 * g:512 * g + 512], ps[:, b, :], t)
                    M.give(b, t1)
                else:
                    b2, fr2 = M.bank()
                    t2 = pe.mm([(ps[:, b2, :], acc[:, 10 + g, cs], Hs[:, g, :], True, True)], th, *fr2)
                    t1 = dv.tt(ytok[:, 512 * g:512 * g + 512].rearrange("p (h d) -> p h d", d=64),
                               ps[:, b2, :].rearrange("p (h d) -> p h d", d=64),
                               bc(sc[:, 1, 8 * g:8 * g + 8].unsqueeze(2), [128, 8, 64]), ALU.mult, t2, teA, *tyf)
                    M.give(b2, t1)
                    t1 = dv.tt(ytok[:, 512 * g:512 * g + 512], ytok[:, 512 * g:512 * g + 512], ps[:, b, :], ALU.add, t1, t)
                    M.give(b, t1)
                tyt.append(t1)
                tL = [pe.here()]
            tyf = []
            for g in range(2):
                b, fr = M.bank()
                t = pe.tr([(ps[:, b, j * 128:j * 128 + 128], ytok[:, (4 * g + j) * 128:(4 * g + j) * 128 + 128])
                           for j in range(4)], ident, tyt[g], *fr)
                tyf.append(t)
                for j in range(4):
                    i = 4 * g + j
                    t1 = dv.stt(y[:, i, cs], acc[:, i, cs], V["sd"][:, i:i + 1], ps[:, b, j * 128:j * 128 + 128],
                                ALU.mult, ALU.add, t)
                M.give(b, t1)
        t = dv.tt(y, y, z, ALU.mult, t1)
        t = M.stats(y, 8, 4, T, 1 / 512, ones, rs, sq, eps, t)
        for g in range(2):
            t = dv.tt(y[:, 4 * g:4 * g + 4, :], y[:, 4 * g:4 * g + 4, :], bc(rs[:, g:g + 1, :], [128, 4, T]), ALU.mult, t)
        ty = dv.tt(y, y, bc(V["sn"].unsqueeze(2), [128, 8, T]), ALU.mult, t)
        M.barrier()
        A.at = keep
        branch_out(y, ty, "wso", 13, False)
        M.barrier()

        lat = A(8, T)
        M.lin("win", layer, [7, 8], xn, T,
              lambda i, m, p, t: [M.copy(lat[:, i:i + m, :], p, t)], txn)
        tl = [ac.here(), dv.here()]
        qn, kn, kr = A(4, T), A(2, T), A(2, T)
        q12, kT, vt = A(12, T), A(8, T), A(2, 1024)
        Pm, PT, ot = A(8, T), A(8, 2, 128), A(8, 128)
        mx, den = A(16), A(16)
        tq = normed(lat[:, 0:4, :], qn, 4, 1 / 512, V["qn"], ones, tl)
        t = M.stats(lat[:, 4:6, :], 2, 2, T, 1 / 256, ones, rs, sq, eps, tq)
        t = dv.tt(kn, lat[:, 4:6, :], bc(rs[:, 0:1, :], [128, 2, T]), ALU.mult, t)
        tk = dv.tt(kn, kn, bc(V["kn"].unsqueeze(2), [128, 2, T]), ALU.mult, t)
        M.lin("wuq", layer, [0, 1], qn, T, lambda i, m, p, t: [M.copy(q12[:, i:i + m, :], p, t)], tq)
        tqq = [ac.here(), dv.here()]
        M.lin("wuk", layer, [0], kn, T, lambda i, m, p, t: [M.copy(kT[:, i:i + m, :], p, t)], tk)
        M.lint("wuv", layer, [0], kn, 2, lambda m, c0, p, t: [M.copy(vt[:, m, c0:c0 + 512], p, t)], tk)
        tkk = [ac.here(), dv.here()]

        def rope(a, bb, n, w):
            cs_, sn_ = (bc(S[k].unsqueeze(1), [128, n, T]) for k in ("cos", "sin"))
            m1, m2 = sq[:, 0:n, :], sq[:, 4:4 + n, :]
            t1 = dv.tt(m1, bb, sn_, ALU.mult, *w)
            t2 = dv.tt(m2, a, sn_, ALU.mult, *w)
            t3 = dv.tt(a, a, cs_, ALU.mult, t2)
            t4 = dv.tt(bb, bb, cs_, ALU.mult, t1)
            t3 = dv.tt(a, a, m1, ALU.subtract, t3)
            return dv.tt(bb, bb, m2, ALU.add, t4)

        trk = rope(lat[:, 6:7, :], lat[:, 7:8, :], 1, [*tl, pe.here(), dv.here(), *tabs])
        trq = rope(q12[:, 8:10, :], q12[:, 10:12, :], 2, [*tqq, dv.here()])
        M.barrier()
        scale = 192 ** -0.5
        tpp = [[], []]
        for i in range(2):
            nk = 128 * (i + 1)
            qs = slice(i * 128, i * 128 + 128)
            for hp in range(4):
                s = hp % 2
                Pv = Pm[:, 2 * s:2 * s + 2, :]
                b, fr = M.bank()
                parts = []
                for j in range(2):
                    h = hp + 4 * j
                    r = slice(32 * hp, 32 * hp + 32)
                    o_ = ps[:, b, 256 * j:256 * j + nk]
                    parts += [(o_, q12[:, h, qs], kT[:, h, 0:nk], True, False),
                              (o_, q12[r, 8 + h // 4, qs], lat[r, 6, 0:nk], False, False),
                              (o_, q12[r, 10 + h // 4, qs], lat[r, 7, 0:nk], False, True)]
                t = pe.mm(parts, trk, trq, *tkk, *fr)
                P = ps[:, b, :].rearrange("p (a b) -> p a b", a=2)
                dg = slice(128 * i, 128 * i + 128)
                t1 = dv.tt(Pv[:, :, dg], P[:, :, dg], bc(C["causal"].unsqueeze(1), [128, 2, 128]), ALU.add, t, *tpp[s])
                if i:
                    t1 = dv.cp(Pv[:, :, 0:128], P[:, :, 0:128], t, *tpp[s])
                M.give(b, t1)
                k0 = 8 * i + 2 * hp
                t1 = dv.red(mx[:, k0:k0 + 2], Pv[:, :, 0:nk], ALU.max, t1)
                t1 = dv.ts(mx[:, k0:k0 + 2], mx[:, k0:k0 + 2], -scale, None, ALU.mult, None, t1)
                for j in range(2):
                    te = ac.act(Pv[:, j, 0:nk], Pv[:, j, 0:nk], ACT.Exp, t1, bias=mx[:, k0 + j:k0 + j + 1],
                                scale=scale, acc=den[:, k0 + j:k0 + j + 1])
                td = dv.recip(den[:, k0:k0 + 2], den[:, k0:k0 + 2], te)
                b, fr = M.bank()
                t = pe.tr([(ps[:, b, (2 * j + kb) * 128:(2 * j + kb) * 128 + 128], Pv[:, j, kb * 128:kb * 128 + 128])
                           for j in range(2) for kb in range(i + 1)], ident, te, *fr)
                PTv = PT[:, 2 * s:2 * s + 2, :, :]
                t = ac.cp(PTv[:, :, 0:i + 1, :], ps[:, b, :].rearrange("p (a k b) -> p a k b", a=2, k=2)[:, :, 0:i + 1, :],
                          t, *tpp[s])
                M.give(b, t)
                b, fr = M.bank()
                t = pe.mm([(ps[:, b, 128 * j:128 * j + 128], PTv[:, j, kb, :], vt[:, kb, (hp + 4 * j) * 128:(hp + 4 * j) * 128 + 128],
                            kb == 0, kb == i) for j in range(2) for kb in range(i + 1)], t, *fr)
                tpp[s] = [t]
                t = dv.tt(ot[:, hp:hp + 5:4, :], ps[:, b, 0:256].rearrange("p (a b) -> p a b", a=2),
                          bc(den[:, k0:k0 + 2].unsqueeze(2), [128, 2, 128]), ALU.mult, t, td, *(tof if i else []))
                M.give(b, t)
            tof = []
            for g in range(2):
                b, fr = M.bank()
                t1 = pe.tr([(ps[:, b, j * 128:j * 128 + 128], ot[:, 4 * g + j, :]) for j in range(4)], ident, t, *fr)
                tof.append(t1)
                ty = ac.cp(y[:, 4 * g:4 * g + 4, qs], ps[:, b, :].rearrange("p (a b) -> p a b", a=4), t1)
                M.give(b, ty)
        M.barrier()
        A.at = keep
        branch_out(y, ty, "wmo", 15, False)
        tm = dv.here()

        def res(i, m, p, t):
            return [dv.tt(x[:, i:i + m, :], x[:, i:i + m, :], p, ALU.add, t)]
        M.lin("wo", layer, [0, 1], mixed, T, res, tm)
        txn = normed(x, xn, 8, 1 / 1024, V["n2"], ones, [dv.here()])
        M.barrier()
        hid = A(32, T)

        def up(i, m, p, t):
            t1 = ac.act(hid[:, i:i + m, :], p, ACT.Relu, t)
            po.tt(hid[:, i:i + m, :], hid[:, i:i + m, :], hid[:, i:i + m, :], ALU.mult, t1)
            return [t1]
        M.lin("wup", layer, range(8), xn, T, up, txn)
        M.lin("wdn", layer, range(8), hid, T, res, po.here())
        tx = [dv.here()]
        A.at = base
        M.barrier()

    base = A.at
    sq, rs = A(8, T), A(8, T)
    t = M.stats(x, 8, 8, T, 1 / 1024, ones, rs, sq, eps, *tx)
    t = dv.tt(x, x, bc(rs[:, 0:1, :], [128, 8, T]), ALU.mult, t)
    t = dv.tt(x, x, bc(S["vec1"][0]["fn"].unsqueeze(2), [128, 8, T]), ALU.mult, t)
    A.at = base
    M.barrier()
    return t


def second_block(M, A, S, tx0):
    pe, dv, ac, po, ps = M.pe, M.dv, M.ac, M.po, M.ps
    C, x = S["c"], S["x2"]
    ident, ones, eps = C["ident"], C["ones"], S["eps"]
    LAT, CTX = slice(0, 256), slice(256, 512)
    cases = (LAT, CTX)
    sc2 = S["silc"]
    t = ac.act(sc2, S["cvec"], ACT.Silu, *S["tx"])
    tsc = t
    tx = [tx0, *S["tx"]]
    for layer in range(2):
        V, tv = S["vec2"][layer]
        last = layer == 1
        base = A.at
        mod, A1, A2 = A(48, 2), A(8, 2), A(8, 2)
        h = A(8, 512)
        tmp = A(6144)
        sq = tmp[:, 0:4096].rearrange("p (a b) -> p a b", a=8)
        rs = tmp[:, 4096:6144].rearrange("p (a b) -> p a b", a=4)
        keep = A.at

        def em(i, m, p, t):
            return [dv.tt(mod[:, i:i + m, :], p, bc(V["adab"][:, i:i + m].unsqueeze(2), [128, m, 2]), ALU.add, t, *tv)]
        M.lin("ada", layer, range(12), sc2, 2, em, tsc)
        tmod = dv.here()
        for dst, g, off in ((A1, "n1", 8), (A2, "n2", 32)):
            tmod = dv.stt(dst, mod[:, off:off + 8, :], 1.0, bc(V[g].unsqueeze(2), [128, 8, 2]), ALU.add, ALU.mult, tmod)

        def modulated(Am, off, n, w):
            t = M.stats(x[:, :, 0:n], 8, 8, n, 1 / 1024, ones, rs, sq, eps, *w)
            t = dv.tt(h[:, :, 0:n], x[:, :, 0:n], bc(rs[:, 0:1, 0:n], [128, 8, n]), ALU.mult, t)
            for case in range(n // 256):
                hv = h[:, :, cases[case]]
                t1 = dv.tt(hv, hv, bc(Am[:, :, case:case + 1], [128, 8, 256]), ALU.mult, t)
                t1 = dv.tt(hv, hv, bc(mod[:, off:off + 8, case:case + 1], [128, 8, 256]), ALU.add, t1)
            return t1

        def onto_x(goff, n):
            def ev(i, m, p, t):
                for j in range(m):
                    for case in range(n // 256):
                        s = cases[case]
                        t1 = dv.stt(x[:, i + j, s], p[:, j, s], mod[:, goff + i + j, case:case + 1], x[:, i + j, s],
                                    ALU.mult, ALU.add, t)
                return [t1]
            return ev

        th = modulated(A1, 0, 512, [*tx, tmod])
        M.barrier()
        if layer == 0:
            q, k, vt = A(8, 512), A(8, 512), A(4, 1024)
            P4, PT4, ot = A(4, 512), A(4, 512), A(1024)
            den, mx = A(8, 16), A(8, 16)
            M.lin("nqkv", 0, [0, 1], h, 512, lambda i, m, p, t: [M.copy(q[:, i:i + m, :], p, t)], th)
            M.lin("nqkv", 0, [2, 3], h, 512, lambda i, m, p, t: [M.copy(k[:, i:i + m, :], p, t)], th)
            tqk = [ac.here(), dv.here()]
            M.lint("nqkv", 0, [4, 5], h, 4, lambda m, c0, p, t: [M.copy(vt[:, m, c0:c0 + 512], p, t)], th)
            tvv = [ac.here(), dv.here()]
            w = tqk
            for src, gain, f in ((q, "qg", 0.125), (k, "kg", 1.0)):
                for g in range(2):
                    s4 = slice(4 * g, 4 * g + 4)
                    t = M.stats(src[:, s4, :], 4, 1, 512, 1 / 64, C["bd64"], rs, sq, eps, *w)
                    t = dv.tt(src[:, s4, :], src[:, s4, :], rs, ALU.mult, t)
                    w = [t]
                t = dv.ts(src, src, V[gain], f, ALU.mult, ALU.mult, t)
                w = [t]
            M.barrier()
            bias = sq
            oF = h
            tP = [[] for _ in range(4)]
            tbw = [[], []]
            nb = 0
            for i in range(4):
                qs = slice(128 * i, 128 * i + 128)
                lat = i < 2
                ks = slice(0, 512) if lat else CTX
                k0 = 0 if lat else 256
                for hp in range(8):
                    if lat and hp % 4 == 0:
                        bs = nb % 2
                        bv = bias[:, 4 * bs:4 * bs + 4, :].rearrange("p a (b c) -> p (a b) c", c=256)
                        M.dma(bv, M.d["rpb"][i, nb % 2], S["bsem"][bs], [*tbw[bs], pe.here()])
                        nb += 1
                        tbias = (S["bsem"][bs], 16 * ((nb + 1) // 2))
                        if nb == 1:
                            pass
                    tpv = []
                    for j in range(2):
                        hd = 2 * hp + j
                        s = hd % 4
                        r = slice(64 * j, 64 * j + 64)
                        Pv = P4[:, s, :]
                        b, fr = M.bank()
                        t = pe.mm([(ps[:, b, k0:512], q[r, hp, qs], k[r, hp, ks], True, True)], *fr, *w)
                        if lat:
                            t1 = dv.tt(Pv[:, LAT], ps[:, b, LAT], bv[:, hd % 8, :], ALU.add, t, tbias, *tP[s])
                            t2 = ac.cp(Pv[:, CTX], ps[:, b, CTX], t1, *tP[s])
                            M.give(b, t1, t2)
                            if hd % 8 == 7:
                                tbw[bs] = [t1]
                            pin, tw = Pv, [t1, t2]
                        else:
                            pin, tw = ps[:, b, CTX], [t]
                        m_ = mx[:, i, hd:hd + 1]
                        t1 = self_neg_max(dv, m_, pin, tw)
                        te = ac.act(Pv[:, k0:512], pin, ACT.Exp, t1, *tP[s], bias=m_, acc=den[:, i, hd:hd + 1])
                        if not lat:
                            M.give(b, te)
                        b, fr = M.bank()
                        t = pe.tr([(ps[:, b, c:c + 128], Pv[:, c:c + 128]) for c in range(k0, 512, 128)], ident, te, *fr)
                        t = M.copy(PT4[:, s, k0:512], ps[:, b, k0:512], t, *tP[s])
                        M.give(b, t)
                        tpv.append((s, t))
                    td = dv.recip(den[:, i, 2 * hp:2 * hp + 2], den[:, i, 2 * hp:2 * hp + 2], te)
                    b, fr = M.bank()
                    parts = []
                    for j in range(2):
                        hd = 2 * hp + j
                        blocks = range(k0 // 128, 4)
                        parts += [(ps[:, b, 64 * j:64 * j + 64], PT4[:, hd % 4, kb * 128:kb * 128 + 128],
                                   vt[:, kb, 64 * hd:64 * hd + 64], kb == blocks[0], kb == 3) for kb in blocks]
                    t = pe.mm(parts, *[a for _, a in tpv], *tvv, *fr)
                    for s, _ in tpv:
                        tP[s] = [t]
                    t = dv.tt(ot[:, 128 * hp:128 * hp + 128].rearrange("p (a b) -> p a b", a=2),
                              ps[:, b, 0:128].rearrange("p (a b) -> p a b", a=2),
                              bc(den[:, i, 2 * hp:2 * hp + 2].unsqueeze(2), [128, 2, 64]), ALU.mult, t, td,
                              *(tof if i else []))
                    M.give(b, t)
                tof = []
                for g in range(2):
                    b, fr = M.bank()
                    t1 = pe.tr([(ps[:, b, j * 128:j * 128 + 128], ot[:, 512 * g + j * 128:512 * g + j * 128 + 128])
                                for j in range(4)], ident, t, *fr)
                    tof.append(t1)
                    to = ac.cp(oF[:, 4 * g:4 * g + 4, qs], ps[:, b, :].rearrange("p (a b) -> p a b", a=4), t1)
                    M.give(b, to)
            M.barrier()
            M.lin("no", 0, [0, 1], oF, 512, onto_x(16, 512), to)
            n = 512
        else:
            q, g_, vt = A(8, 256), A(8, 256), A(4, 1024)
            B, K = A(8, 512), A(8, 512)
            St, AA = A(16, 128), A(8, 2, 256)
            masks = S["trig"][:, 0:480]
            lb, p0_, mm_ = A(32), A(16), A(16)
            Mu = masks[:, :].bitcast(mybir.dt.uint8).rearrange("p (a b) -> p a b", b=128)
            M.dma(tmp[:, 0:1920], M.d["imask"], S["isem"], M.extra)
            tmask = dv.cp(masks.bitcast(mybir.dt.uint8), tmp[:, 0:1920], (S["isem"], 16))
            hl = V["hl"]
            t = dv.tt(mm_, hl[:, 0:16], hl[:, 16:32], ALU.max, *tv)
            t = dv.tt(lb.rearrange("p (a b) -> p a b", a=2), hl.rearrange("p (a b) -> p a b", a=2),
                      bc(mm_.unsqueeze(1), [128, 2, 16]), ALU.subtract, t)
            t = ac.act(lb, lb, ACT.Exp, t)
            t = dv.tt(mm_, lb[:, 0:16], lb[:, 16:32], ALU.add, t)
            t = dv.recip(mm_, mm_, t)
            t = dv.tt(lb.rearrange("p (a b) -> p a b", a=2), lb.rearrange("p (a b) -> p a b", a=2),
                      bc(mm_.unsqueeze(1), [128, 2, 16]), ALU.mult, t)
            t = dv.tt(mm_, lb[:, 0:16], lb[:, 16:32], ALU.add, t)
            t = dv.tt(mm_, mm_, lb[:, 0:16], ALU.subtract, t)
            tlb = dv.ts(p0_, mm_, -1.0, 1.0, ALU.mult, ALU.add, t)
            LB, OM = mm_, p0_
            M.lin("hin", 0, [0, 1], h, 256, lambda i, m, p, t: [ac.act(q[:, i:i + m, :], p, ACT.Silu, t)], th)
            M.lin("hin", 0, [4, 5], h, 256, lambda i, m, p, t: [ac.act(g_[:, i:i + m, :], p, ACT.Silu, t)], th)
            tqg = ac.here()
            M.lint("hin", 0, [2, 3], h, 4, lambda m, c0, p, t: [M.copy(vt[:, m, c0:c0 + 512], p, t)], th)
            tvv = [ac.here(), dv.here()]
            ta0 = po.fill(AA, 0.0)
            o1 = ones[:, 0:1]
            for dr in range(2):
                E, Qt, Kt = (tmp[:, 2048 * i:2048 * i + 2048] for i in range(3))
                E3, Q3, K3 = (v.rearrange("p (a b) -> p a b", a=8) for v in (E, Qt, Kt))

                def ef(i, m, p, t, dr=dr):
                    t1 = ac.act(B[:, i:i + m, :], p, ACT.Sigmoid, t, tmask)
                    t2 = ac.act(K[:, i:i + m, :], p, ACT.Sigmoid, t, scale=-1.0)
                    for j in range(i, i + m):
                        d = 8 * dr + j
                        dv.ts(B[:, j, :], B[:, j, :], OM[:, d:d + 1], LB[:, d:d + 1], ALU.mult, ALU.add, t1, tlb)
                        dv.ts(K[:, j, :], K[:, j, :], OM[:, d:d + 1], None, ALU.mult, None, t2, tlb)
                    return [t2]
                M.lin("hin", 0, [6 + 2 * dr, 7 + 2 * dr], h, 512, ef, th)
                t = dv.ts(B, B, 1e-19, None, ALU.max, None, dv.here())
                tk = t
                t = ac.act(B, B, ACT.Ln, t)
                rev = slice(None, None, -1)
                for j in range(8):
                    lat, ctx = B[:, j, LAT], B[:, j, CTX]
                    if dr:
                        lat = lat[:, ::-1]
                    else:
                        ctx = ctx[:, ::-1]
                    on = bc(o1, [128, 256])
                    dv.scan(lat, on, lat, t)
                    tsn = dv.scan(ctx, on, ctx, t)
                src, dst = (slice(257, 512), slice(256, 511)) if dr == 0 else (slice(256, 511), slice(257, 512))
                t = ac.act(E3[:, :, 0:255], B[:, :, src], ACT.Exp, tsn)
                tkd = dv.tt(K[:, :, dst], K[:, :, dst], E3[:, :, 0:255], ALU.mult, t, tk)
                kd = K3.rearrange("p a (b c) -> p a b c", b=2)
                for j in range(0, 8, 2):
                    b, fr = M.bank()
                    t = pe.tr([(ps[:, b, (2 * a + c) * 128:(2 * a + c) * 128 + 128],
                                K[:, j + a, 256 + 128 * c:384 + 128 * c]) for a in range(2) for c in range(2)], ident, tkd, *fr)
                    t = M.copy(Kt[:, 256 * j:256 * j + 512], ps[:, b, :], t)
                    M.give(b, t)
                    b, fr = M.bank()
                    t = pe.mm([(ps[:, b, 128 * a:128 * a + 128], kd[:, j + a, c, :],
                                vt[:, 2 + c, 128 * (j + a):128 * (j + a) + 128], c == 0, c == 1)
                               for a in range(2) for c in range(2)], t, *tvv, *fr)
                    tst = ac.cp(St[:, 8 * dr + j:8 * dr + j + 2, :], ps[:, b, 0:256].rearrange("p (a b) -> p a b", a=2), t)
                    M.give(b, tst)
                tuse = [t]
                Bl, Kl = B[:, :, LAT], K[:, :, LAT]
                tA = [ta0]
                for j in range(0, 8, 2):
                    b, fr = M.bank()
                    t = pe.mm([(ps[:, b, (2 * a + c) * 128:(2 * a + c) * 128 + 128], K[:, j + a, 128 * c:128 * c + 128],
                                q[:, j + a, 128 * c:128 * c + 128], True, True) for a in range(2) for c in range(2)],
                              tk, tqg, *fr)
                    Pq = ps[:, b, :].rearrange("p (a c t) -> p a c t", a=2, c=2)
                    for c in range(2):
                        dst_ = AA[:, j:j + 2, c, 128 * c:128 * c + 128]
                        if dr == 0:
                            t1 = dv.pick(dst_, bc(Mu[:, 14:15, :], [128, 2, 128]), Pq[:, :, c, :], t, tmask, ta0)
                        else:
                            t2 = dv.tt(E3[:, j:j + 2, 128 * c:128 * c + 128], Pq[:, :, c, :], bc(ident.unsqueeze(1), [128, 2, 128]), ALU.mult, t, *tuse)
                            t1 = dv.tt(dst_, dst_, E3[:, j:j + 2, 128 * c:128 * c + 128], ALU.add, t2)
                    M.give(b, t1)
                tdd = t1
                for lv in range(8):
                    hf = 1 << lv
                    mid = hf - 1 if dr == 0 else hf
                    nb_ = 256 // (2 * hf)
                    b4 = Bl.rearrange("p a (n r) -> p a n r", r=2 * hf)
                    e4 = E3.rearrange("p a (n r) -> p a n r", r=2 * hf)
                    mb = bc(b4[:, :, :, mid:mid + 1], [128, 8, nb_, hf])
                    left, right = slice(0, hf), slice(hf, 2 * hf)
                    qside, kside = (right, left) if dr == 0 else (left, right)
                    dv.tt(e4[:, :, :, qside], b4[:, :, :, qside], mb, ALU.subtract, tsn, tdd, *tuse)
                    t = dv.tt(e4[:, :, :, kside], mb, b4[:, :, :, kside], ALU.subtract)
                    t = ac.act(E, E, ACT.Exp, t)
                    tq_ = po.tt(Q3, q, E3, ALU.mult, t, tqg, *tuse)
                    tk_ = dv.tt(K3, Kl, E3, ALU.mult, t, tk, *tuse)
                    tdd = tq_
                    tuse = []
                    if lv < 7:
                        mk = bc(Mu[:, 7 * dr + lv:7 * dr + lv + 1, :], [128, 2, 128])
                        for j in range(0, 8, 2):
                            b, fr = M.bank()
                            t = pe.mm([(ps[:, b, (2 * a + c) * 128:(2 * a + c) * 128 + 128], K3[:, j + a, 128 * c:128 * c + 128],
                                        Q3[:, j + a, 128 * c:128 * c + 128], True, True) for a in range(2) for c in range(2)],
                                      tq_, tk_, *fr)
                            Pq = ps[:, b, :].rearrange("p (a c t) -> p a c t", a=2, c=2)
                            for c in range(2):
                                t1 = dv.pick(AA[:, j:j + 2, c, 128 * c:128 * c + 128], mk, Pq[:, :, c, :], t, tmask, ta0)
                            M.give(b, t1)
                    else:
                        sb_, tb_ = (0, 1) if dr == 0 else (1, 0)
                        for j in range(0, 8, 4):
                            b, fr = M.bank()
                            t = pe.mm([(ps[:, b, a * 128:a * 128 + 128], K3[:, j + a, 128 * sb_:128 * sb_ + 128],
                                        Q3[:, j + a, 128 * tb_:128 * tb_ + 128], True, True) for a in range(4)], tq_, tk_, *fr)
                            t1 = dv.cp(AA[:, j:j + 4, sb_, 128 * tb_:128 * tb_ + 128],
                                       ps[:, b, :].rearrange("p (a t) -> p a t", a=4), t, ta0)
                            M.give(b, t1)
                    tuse = [t, tdd]
                t = ac.act(E3, Bl, ACT.Exp, tsn, *tuse, tk_)
                tq_ = dv.tt(Q3, q, E3, ALU.mult, t)
                O = x[:, :, CTX]
                for j in range(0, 8, 2):
                    b, fr = M.bank()
                    parts = []
                    for a in range(2):
                        oo = ps[:, b, 256 * a:256 * a + 256]
                        parts.append((oo, St[:, 8 * dr + j + a, :], Q3[:, j + a, :], True, dr == 0))
                        if dr:
                            parts += [(oo, vt[:, c, 128 * (j + a):128 * (j + a) + 128], AA[:, j + a, c, :], False, c == 1)
                                      for c in range(2)]
                    t = pe.mm(parts, tq_, tst, *([t1] if dr else []), *fr)
                    P = ps[:, b, :].rearrange("p (a b) -> p a b", a=2)
                    if dr == 0:
                        to = dv.cp(O[:, j:j + 2, :], P, t)
                    else:
                        to = dv.tt(O[:, j:j + 2, :], O[:, j:j + 2, :], P, ALU.add, t)
                    M.give(b, to)
                M.barrier()
            t = M.stats(O, 8, 1, 256, 1 / 128, ones, S["rs8"](A, AA), sq, eps, to)
            t = dv.tt(O, O, S["rs8"](A, AA), ALU.mult, t)
            to = dv.stt(O, O, V["hn"], g_, ALU.mult, ALU.mult, t, tqg)
            M.lin("ho", 0, [0, 1], O, 256, onto_x(16, 256), to)
            n = 256
        M.barrier()
        A.at = keep
        th = modulated(A2, 24, n, [dv.here()])
        M.barrier()
        hid = A(22, n)

        def up(i, m, p, t):
            at = 2 * (i // 4) + i % 2
            if i % 4 < 2:
                return [ac.act(hid[:, at:at + m, :], p, ACT.Silu, t)]
            return [dv.tt(hid[:, at:at + m, :], hid[:, at:at + m, :], p, ALU.mult, t, ac.here())]
        M.lin("fi", layer, range(11), h, n, up, th)
        M.lin("fo", layer, range(8), hid, n, onto_x(40, n), dv.here())
        tx = [dv.here()]
        A.at = base
        M.barrier()
    return tx[0]


def self_neg_max(dv, out, src, w):
    return dv(lambda e: e.tensor_reduce(out, src, AX.X, ALU.max, negate=True), w)


def program(nc, d, out):
    with ExitStack() as ctx:
        M = Machine(nc, ctx, d)
        x2 = M.sb("x2", [128, 8, 512])
        cst = M.sb("cst", [128, len(CONSTS), 128])
        o1, n1 = offsets(VEC1)
        o2, n2 = offsets(VEC2)
        v1 = M.sb("v1", [128, 2, n1])
        v2 = M.sb("v2", [128, 2, n2])
        posi = M.sb("posi", [128, T], I32)
        trig = M.sb("trig", [128, 2 * T])
        eps = M.sb("eps", [128, 1])
        cvec, silc = M.sb("cvec", [128, 8, 2]), M.sb("silc", [128, 8, 2])
        arena = M.sb("arena", [128, ARENA])
        A = Arena(arena)
        sx, sv, s2 = M.sem("x"), M.sem("v"), M.sem("v2")
        for o, i in ((x2[:, :, 0:256], d["x"]), (x2[:, :, 256:512], d["ctx"]), (cst[:, :, :], d["cst"]),
                     (posi[:, :], d["pos"]), (cvec[:, :, :], d["c"]), (v1[:, :, :], d["v1"]), (v2[:, :, :], d["v2"])):
            M.dma(o, i, sx)
        te = M.po.fill(eps[:, :], EPS)
        tx = [(sx, 16 * 7), te]
        C = {k: cst[:, i, :] for i, k in enumerate(CONSTS)}
        vec = lambda v, o, l: {k: v[:, l, a:b] for k, (a, b) in o.items()}
        S = {"c": C, "x": x2[:, :, 0:256], "x2": x2[:, :, :], "eps": eps[:, :], "tx": tx, "pos": posi[:, :],
             "cos": trig[:, 0:T], "sin": trig[:, T:2 * T], "trig": trig[:, :], "vec1": (vec(v1, o1, 0), tx), "vec1b": (vec(v1, o1, 1), tx),
             "vec2": [(vec(v2, o2, l), tx) for l in range(2)], "cvec": cvec[:, :, :], "silc": silc[:, :, :],
             "bsem": [M.sem("b0"), M.sem("b1")], "isem": M.sem("im"),
             
             "rs8": lambda A, AA: AA.rearrange("p a b c -> p (a b c)")[:, 0:2048].rearrange("p (a b) -> p a b", a=8)}
        so = M.sem("out")
        t = first_block(M, A, S)
        if STAGE == 2:
            t = second_block(M, A, S, t)
        M.dma(out, x2[:, :, 0:256], so, [t])
        M.sp.items.append((lambda e: e.wait_ge(so, 16), [], False))
        block = ctx.enter_context(nc.Block())

        @block.sync
        def _(e):
            M.sp.play(e)

        @block.tensor
        def _(e):
            M.pe.play(e)

        @block.vector
        def _(e):
            M.dv.play(e)

        @block.scalar
        def _(e):
            M.ac.play(e)

        @block.gpsimd
        def _(e):
            M.po.play(e)
        return A.top


STAGE = 2
ARENA = 33000


def constants():
    i, j = np.meshgrid(np.arange(128), np.arange(128), indexing="ij")
    f = lambda m: m.astype(np.float32)
    same = i // 64 == j // 64
    lev = lambda h: (i // (2 * h) == j // (2 * h)) & (i % (2 * h) < h) & (j % (2 * h) >= h)
    m = {"ident": f(i == j), "ones": f(i == i), "tri": f(i <= j), "bd64": f(same), "btri": f(same & (i <= j)),
         "bstrict": f(same & (i < j)), "cone0": f(i < 64), "cone1": f(i >= 64), "m0": f(lev(1)).T,
         "causal": np.where(j > i, np.float32(NEG), np.float32(0)).astype(np.float32)}
    for n in range(6):
        m[f"t{n}"] = f(lev(1 << n))
    cst = np.stack([m[k] for k in CONSTS], 1)
    ints = [lev(1 << n) for n in range(7)] + [lev(1 << n).T for n in range(7)] + [i == j]
    return np.ascontiguousarray(cst), np.ascontiguousarray(np.stack(ints, 1).astype(np.float32).reshape(128, 1920))


def tiled(name, w):
    k, n, c = MATS[name]
    w = np.asarray(w).reshape(-1, k // 128, 128, n // c, c)
    return np.ascontiguousarray(w.transpose(0, 3, 2, 1, 4)).reshape(-1, n // c, 128, (k // 128) * c)


def cols(v):
    v = np.asarray(v)
    return v.reshape(*v.shape[:-1], -1, 128).swapaxes(-1, -2)


def layout(a):
    d = {}
    win = a["w_in"]
    z, xbc, dt, cq, ckv, kr, qkv, gz, gb, ga, gate = np.split(
        win, np.cumsum([1024, 1536, 16, 512, 256, 64, 2048, 1024, 8, 8]).tolist(), axis=-1)
    r1, r2 = np.tile(kr[..., 0:32], (1, 1, 4)), np.tile(kr[..., 32:64], (1, 1, 4))
    d["win"] = tiled("win", np.concatenate([qkv, xbc, cq, ckv, r1, r2, z, gz, gate], -1))
    d["wsm"] = tiled("wsm", np.concatenate([dt, ga, gb], -1))
    uq = a["mla_w_uq"].reshape(2, 512, 8, 192)
    d["wuq"] = tiled("wuq", np.concatenate([uq[..., 0:128].reshape(2, 512, 1024), uq[..., 128:160].reshape(2, 512, 256),
                                            uq[..., 160:192].reshape(2, 512, 256)], -1))
    ukv = a["mla_w_ukv"].reshape(2, 256, 8, 256)
    d["wuk"] = tiled("wuk", ukv[..., 0:128].reshape(2, 256, 1024))
    d["wuv"] = tiled("wuv", ukv[..., 128:256].reshape(2, 256, 1024))
    for k, n in (("wso", "w_ssd_out"), ("wmo", "w_mla_out"), ("wgo", "w_gdn_out"), ("wo", "w_out"), ("wup", "w_up"),
                 ("wdn", "w_down"), ("ada", "ada_w_2"), ("nqkv", "na_w_qkv_2"), ("no", "na_w_o_2"), ("hin", "hg_w_in_2"),
                 ("ho", "hg_w_o_2"), ("fo", "ffn_w_out_2")):
        d[k] = tiled(k, a[n])
    fi = a["ffn_w_in_2"].reshape(2, 1024, 2, 11, 256)
    d["fi"] = tiled("fi", fi.transpose(0, 1, 3, 2, 4).reshape(2, 1024, 5632))
    d["x"] = np.ascontiguousarray(a["x"][0].T.reshape(8, 128, 256).transpose(1, 0, 2))
    d["ctx"] = np.ascontiguousarray(a["ctx_2"][0].T.reshape(8, 128, 256).transpose(1, 0, 2))
    d["pos"] = np.ascontiguousarray(np.broadcast_to(a["positions"], (128, 256)))
    d["c"] = np.ascontiguousarray(np.stack([cols(a["c_2"][0]), cols(a["c_ctx_2"])], -1))
    rows = lambda v: np.broadcast_to(v[:, None, :], (2, 128, v.shape[-1]))
    taps = lambda w: w.reshape(2, 4, -1, 128).transpose(0, 3, 2, 1).reshape(2, 128, -1)
    inv = (10000.0 ** (-np.arange(0, 64, 2, dtype=np.float32) / np.float32(64))).astype(np.float32)
    fn = np.broadcast_to(cols(a["final_norm_g"])[None], (2, 128, 8))
    v1 = {"n1": cols(a["norm1_g"]), "n2": cols(a["norm2_g"]), "cw": taps(a["ssd_conv_w"]), "cb": cols(a["ssd_conv_b"]),
          "gw": taps(a["gdn_conv_w"]), "qn": cols(a["mla_q_norm_g"]), "kn": cols(a["mla_kv_norm_g"]),
          "sn": cols(a["ssd_norm_g"]), "gn": cols(a["gdn_norm_g"]), "sd": cols(np.repeat(a["ssd_d"], 64, -1)),
          "bias": rows(np.concatenate([a["ssd_dt_bias"], a["gdn_dt_bias"]], -1)),
          "alog": rows(np.concatenate([a["ssd_a_log"], a["gdn_a_log"]], -1)), "fn": fn,
          "inv": np.broadcast_to(np.tile(inv, 4)[None, :, None], (2, 128, 1))}
    d["v1"] = np.ascontiguousarray(np.concatenate([v1[k] for k in VEC1], -1).transpose(1, 0, 2))
    two = lambda g: np.broadcast_to(np.tile(g[0], 2)[None, :, None], (2, 128, 1))
    hl = a["hg_lower_2"].reshape(32, 128).T[None]
    v2 = {"adab": cols(a["ada_b_2"]), "n1": cols(a["norm1_g_2"]), "n2": cols(a["norm2_g_2"]),
          "qg": two(a["na_q_gain_2"]), "kg": two(a["na_k_gain_2"]), "hl": np.broadcast_to(hl, (2, 128, 32)),
          "hn": np.broadcast_to(a["hg_norm_g_2"].reshape(1, 128, 1), (2, 128, 1))}
    d["v2"] = np.ascontiguousarray(np.concatenate([v2[k] for k in VEC2], -1).transpose(1, 0, 2))
    rpb = np.pad(a["na_rpb_2"][0], ((0, 0), (0, 0), (0, 1)), constant_values=NEG)
    qi = np.arange(256)
    r, c = qi // 64, qi % 64
    lo = np.clip(c - 8, 0, 48)[:, None]
    inside = (c[None, :] >= lo) & (c[None, :] < lo + 16)
    ri = r[None, :] - r[:, None] + 7
    ci = np.where(inside, np.clip(c[None, :] - c[:, None] + 15, 0, 30), 31)
    tab = rpb[:, ri, ci]
    d["rpb"] = np.ascontiguousarray(tab.reshape(2, 8, 2, 128, 256).transpose(2, 0, 3, 1, 4))
    d["cst"], d["imask"] = constants()
    return d


def kernel(**inputs):
    import numpy as _np
    import concourse.bacc as _bacc
    from concourse import mybir as _mybir
    from concourse.bass_utils import run_bass_kernel_spmd as _run

    d = layout({k: _np.asarray(v) for k, v in inputs.items()})
    nc = _bacc.Bacc("TRN2", target_bir_lowering=False, num_devices=1)
    arrays, aps = {}, {}
    for name, v in d.items():
        arrays[f"in_{name}"] = v
        aps[name] = nc.dram_tensor(f"in_{name}", v.shape, _mybir.dt.from_np(v.dtype), kind="ExternalInput").ap()
    out = nc.dram_tensor("out_0", (128, 8, 256), F32, kind="ExternalOutput").ap()
    program(nc, aps, out)
    r = _run(nc, [arrays], core_ids=[0])
    y = r.results[0]["out_0"]
    return _np.ascontiguousarray(y.transpose(1, 0, 2).reshape(1024, 256).T)[None]
```

```python
import numpy as np
import concourse.bass as bass
from concourse import mybir
from contextlib import ExitStack

F32 = mybir.dt.float32
F32R = mybir.dt.float32r
AHEAD = 3
POOL_EVERY = 3
I32 = mybir.dt.int32
ALU = mybir.AluOpType
ACT = mybir.ActivationFunctionType
AX = mybir.AxisListType

EPS = 1e-6
T = 256
NEG = -1e30
RAW = 3
HI = 4
SLOT = 1024
MAGIC = 12582912.0
TWO_PI_1 = 6.28125
TWO_PI_2 = 0.0019350051879882812
TWO_PI_3 = 3.019916050356e-07

MATS = {
    "win": (1024, 9728, 128, 1), "wsm": (1024, 32, 32, 1), "wuq": (512, 1536, 256, 1), "wuk": (256, 1024, 512, 1),
    "wuv": (256, 1024, 512, 1), "wso": (1024, 1024, 128, 1), "wmo": (1024, 1024, 128, 1), "wgo": (1024, 1024, 128, 1),
    "wo": (1024, 1024, 128, 1), "wup": (1024, 4096, 128, 1), "wdn": (4096, 1024, 128, 4),
    "ada": (1024, 6144, 128, 1), "nqkv": (1024, 3072, 128, 1), "no": (1024, 1024, 128, 1),
    "hin": (1024, 5120, 128, 1), "ho": (1024, 1024, 128, 1), "fi": (1024, 5632, 128, 1), "fo": (2816, 1024, 128, 3),
}


def spans(name):
    k, _, _, parts = MATS[name]
    kt = k // 128
    most = -(-kt // parts)
    return [(r * most, min(kt, (r + 1) * most)) for r in range(parts)]

CONSTS = ["ident", "ones", "tri", "bd64", "btri", "bstrict", "cone0", "cone1", "m0", "causal",
          "t0", "t1", "t2", "t3", "t4", "t5"]
VEC1 = {"n1": 8, "n2": 8, "cw": 48, "cb": 12, "gw": 64, "qn": 4, "kn": 2, "sn": 8, "gn": 1, "sd": 8,
        "bias": 24, "alog": 24, "fn": 8, "inv": 1}
VEC2 = {"adab": 48, "n1": 8, "n2": 8, "qg": 1, "kg": 1, "hl": 32, "hn": 1}


def offsets(table):
    out, at = {}, 0
    for k, n in table.items():
        out[k] = (at, at + n)
        at += n
    return out, at


class Queue:

    def __init__(self, sem):
        self.sem, self.items, self.n, self.held = sem, [], 0, []

    def __call__(self, fn, waits, signal=True):
        waits = [*self.held, *waits]
        self.held = []
        self.items.append((fn, waits, signal))
        if signal:
            self.n += 1
        return (self.sem, self.n)

    def here(self):
        return (self.sem, self.n)

    def play(self, eng):
        seen = {}
        for fn, waits, signal in self.items:
            for sem, value in waits:
                if value > seen.get(sem.num, 0):
                    eng.wait_ge(sem, value)
                    seen[sem.num] = value
            i = fn(eng)
            if signal:
                i.then_inc(self.sem, 1)


class Elementwise(Queue):
    def tt(self, out, a, b, op, *w):
        return self(lambda e: e.tensor_tensor(out, a, b, op), w)

    def ts(self, out, a, s1, s2, op0, op1, *w):
        if op1 is None:
            return self(lambda e: e.tensor_scalar(out, a, s1, None, op0), w)
        return self(lambda e: e.tensor_scalar(out, a, s1, s2, op0, op1), w)

    def stt(self, out, a, s, b, op0, op1, *w):
        return self(lambda e: e.scalar_tensor_tensor(out=out, in0=a, scalar=s, in1=b, op0=op0, op1=op1), w)

    def cp(self, out, a, *w):
        return self(lambda e: e.tensor_copy(out, a), w)

    def red(self, out, a, op, *w):
        return self(lambda e: e.tensor_reduce(out, a, AX.X, op), w)

    def recip(self, out, a, *w):
        return self(lambda e: e.reciprocal(out, a), w)

    def fill(self, out, v, *w):
        return self(lambda e: e.memset(out, v), w)

    def scan(self, out, a, b, *w):
        return self(lambda e: e.tensor_tensor_scan(out, a, b, 0.0, ALU.mult, ALU.add), w)

    def pick(self, out, mask, data, *w):
        return self(lambda e: e.copy_predicated(out, mask, data), w)


class Scalar(Queue):
    def act(self, out, a, func, *w, bias=None, scale=1.0, acc=None):
        def fn(e):
            kw = {}
            if bias is not None:
                kw["bias"] = bias
            if acc is not None:
                kw["accum_out"] = acc
            return e.activation(out, a, func, scale=scale, **kw)
        return self(fn, w)

    def cp(self, out, a, *w):
        return self(lambda e: e.activation(out, a, ACT.Copy), w)


class Tensor(Queue):
    def mm(self, parts, *w):
        for i, (out, l, r, start, stop) in enumerate(parts):
            t = self(lambda e, o=out, l=l, r=r, s=start, p=stop: e.matmul(o, l, r, start=s, stop=p),
                     w if i == 0 else (), signal=i == len(parts) - 1)
        return t

    def tr(self, parts, ident, *w):
        for i, (out, a) in enumerate(parts):
            t = self(lambda e, o=out, a=a: e.transpose(o, a, ident), w if i == 0 else (),
                     signal=i == len(parts) - 1)
        return t


class Machine:
    def __init__(self, nc, ctx, d, plan):
        self.nc, self.ctx, self.d = nc, ctx, d
        self.plan_known = plan is not None
        self.pe, self.dv, self.ac, self.po = (
            c(self.sem(n)) for c, n in ((Tensor, "pe"), (Elementwise, "dv"), (Scalar, "ac"), (Elementwise, "po")))
        self.sp = Queue(self.sem("sp"))
        self.ps = self.pb("ps", [128, 8, 512])
        self.bfree = [[] for _ in range(8)]
        self.bheld = [False] * 8
        self.bi = 0
        base = (nc.sbuf_base + 31) // 32 * 32
        self.slab = self.sb("slab", [128, ARENA])
        self.ring = self.sb("ring", [128, (2 * RAW + HI) * SLOT])
        self.home = base
        self.names = 0
        self.raw = [self.ring[:, i * SLOT:(i + 1) * SLOT] for i in range(2 * RAW)]
        at = ARENA
        self.low = [self.rounded(at + i * SLOT, SLOT) for i in range(2 * RAW)]
        at += 2 * RAW * SLOT
        self.high = [self.rounded(at + i * SLOT, SLOT) for i in range(HI)]
        self.rsem = [self.sem(f"raw{i}") for i in range(RAW)]
        self.rfree = [[] for _ in range(RAW)]
        self.hfree = [[] for _ in range(HI)]
        self.units = 0
        self.highs = 0
        self.unit = None
        self.fills = []
        self.plan = list(plan or [])
        self.asked = []
        self.ready = []
        self.flip = 0
        self.extra = []

    def sem(self, n):
        return self.ctx.enter_context(self.nc.semaphore("s_" + n))

    def sb(self, n, shape, dt=F32):
        return self.ctx.enter_context(self.nc.sbuf_tensor(n, shape, dt))

    def pb(self, n, shape):
        return self.ctx.enter_context(self.nc.psum_tensor(n, shape, F32))

    def rounded(self, at, n):
        self.names += 1
        t = self.nc.alloc_sbuf_tensor_at(f"r{self.names}", [128, n], F32R, offset=self.home + 4 * at)
        return t[:, 0:n]

    def bank(self):
        b = self.bi
        self.bi = (b + 1) % 8
        assert not self.bheld[b]
        self.bheld[b] = True
        return b, self.bfree[b]

    def give(self, b, *tokens):
        self.bfree[b] = list(tokens)
        self.bheld[b] = False

    def barrier(self):
        now = [q.here() for q in (self.pe, self.dv, self.ac, self.po)]
        for q in (self.pe, self.dv, self.ac, self.po):
            q.held = list(now)
        self.extra = list(now)

    def dma(self, out, src, sem, waits=()):
        self.sp.items.append((lambda e: e.dma_start(out, src).then_inc(sem, 16), list(waits), False))

    def prepare(self):
        name, layer, c = self.plan[len(self.ready)]
        cols = MATS[name][2]
        parts = spans(name)
        lo_, hi_ = parts[c % len(parts)]
        n = (hi_ - lo_) * cols
        if c % 2 == 0:
            s = self.units % RAW
            self.units += 1
            src = self.d[name][layer, c // 2]
            self.unit = (name, layer, c, s, (self.rsem[s], 16 * ((self.units - 1) // RAW + 1)))
            self.dma(self.ring[:, 2 * s * SLOT:2 * s * SLOT + src.shape[1]], src, self.rsem[s], self.rfree[s])
        assert self.unit[:3] == (name, layer, c - c % 2)
        s, got = self.unit[3:]
        i = 2 * s + c % 2
        raw = self.raw[i][:, 0:n]
        kn = lambda v: v.rearrange("p (k n) -> p k n", n=cols)
        if name == "ada":
            self.ready.append((kn(raw), got, s, None))
            return
        h = self.highs % HI
        self.highs += 1
        hi, lo = self.high[h][:, 0:n], self.low[i][:, 0:n]
        t = self.ac.cp(hi, raw, got, *self.hfree[h])
        q = self.po if self.highs % POOL_EVERY == 0 else self.dv
        t = q.tt(lo, raw, hi.bitcast(F32), ALU.subtract, t, got)
        self.ready.append(((kn(hi), kn(lo)), t, s, h))

    def weight(self, name, layer, c):
        i = len(self.asked)
        self.asked.append((name, layer, c))
        if not self.plan_known:
            self.plan.append((name, layer, c))
        while len(self.ready) < min(i + 1 + AHEAD, len(self.plan)):
            self.prepare()
        return self.ready[i]

    def done(self, w, token):
        self.rfree[w[2]] = [token]
        if w[3] is not None:
            self.hfree[w[3]] = [token]

    def split(self, dst, src, *w):
        hi, lo = dst
        t = self.ac.cp(hi, src, *w)
        return self.dv.tt(lo, src, hi.bitcast(F32), ALU.subtract, t, *w)

    def lin(self, name, layer, chunks, x, n, evac, *w):
        cols = MATS[name][2]
        rows = spans(name)
        per = 512 // n
        tiles = [(c, j) for c in chunks for j in range(cols // 128)]
        wt = None
        for g in range(0, len(tiles), per):
            group = tiles[g:g + per]
            b, fr = self.bank()
            for jj, (c, j) in enumerate(group):
                o = self.ps[:, b, jj * n:(jj + 1) * n]
                cs = slice(j * 128, (j + 1) * 128)
                for r, (k0, k1) in enumerate(rows):
                    if j == 0:
                        wt = self.weight(name, layer, c * len(rows) + r)
                    (wh, wl), tok, _, _ = wt
                    t = self.pe.mm([(o, a[:, k - k0, cs], v[:, k, 0:n], k == 0 and i == 0,
                                     k == rows[-1][1] - 1 and i == 2) for k in range(k0, k1)
                                    for i, (a, v) in enumerate(((wh, x[0]), (wh, x[1]), (wl, x[0])))], tok, *fr, *w)
                    if j == cols // 128 - 1:
                        self.done(wt, t)
            out = self.ps[:, b, 0:len(group) * n].rearrange("p (a n) -> p a n", n=n)
            self.give(b, *evac(g, len(group), out, t))

    def fill(self, n):
        for _ in range(n):
            if self.fills:
                self.fills.pop(0)()

    def lint(self, name, layer, chunks, x, blocks, evac, *w):
        k_, _, cols, _ = MATS[name]
        kt = k_ // 128
        at = 0
        for c in chunks:
            wt = self.weight(name, layer, c)
            (wh, wl), tok, _, _ = wt
            for m in range(blocks):
                for c0 in range(0, cols, 512):
                    n = min(512, cols - c0)
                    b, fr = self.bank()
                    parts = []
                    for k in range(kt):
                        for i, (a, v) in enumerate(((x[0], wh), (x[0], wl), (x[1], wh))):
                            parts.append((self.ps[:, b, 0:n], a[:, k, m * 128:m * 128 + 128], v[:, k, c0:c0 + n],
                                          k == 0 and i == 0, k == kt - 1 and i == 2))
                    t = self.pe.mm(parts, tok, *fr, *w)
                    self.give(b, *evac(m, at + c0, self.ps[:, b, 0:n], t))
            self.done(wt, t)
            at += cols

    def copy(self, out, src, *w):
        self.flip ^= 1
        return self.ac.cp(out, src, *w) if self.flip else self.dv.cp(out, src, *w)

    def stats(self, src, nt, per, n, inv, lhs, rs, sq, eps, *w):
        t = self.ac.act(sq[:, 0:nt, 0:n], src, ACT.Square, *w)
        groups = nt // per
        pb = 512 // n
        for g in range(0, groups, pb):
            m = min(pb, groups - g)
            b, fr = self.bank()
            tm = self.pe.mm([(self.ps[:, b, j * n:(j + 1) * n], lhs, sq[:, (g + j) * per + k, 0:n], k == 0,
                              k == per - 1) for j in range(m) for k in range(per)], t, *fr)
            o = rs[:, g:g + m, 0:n]
            t1 = self.ac.act(o, self.ps[:, b, 0:m * n].rearrange("p (a n) -> p a n", a=m), ACT.Ln, tm,
                             bias=eps, scale=inv)
            self.give(b, t1)
            last = self.ac.act(o, o, ACT.Exp, t1, scale=-0.5)
        return last


def bc(ap, shape):
    return ap.to_broadcast(shape)


class Arena:
    def __init__(self, m):
        self.m, self.t, self.at, self.top = m, m.slab, 0, 0

    def pair(self, kt, n):
        out = []
        for _ in range(2):
            ap = self(kt * n)
            out.append(self.m.rounded(self.at - kt * n, kt * n).rearrange("p (k n) -> p k n", k=kt))
        return out

    def __call__(self, *dims):
        n = int(np.prod(dims))
        ap = self.t[:, self.at:self.at + n]
        self.at += n
        assert self.at <= ARENA, self.at
        self.top = max(self.top, self.at)
        names = "abcd"[:len(dims)]
        if len(dims) == 1:
            return ap
        return ap.rearrange(f"p ({' '.join(names)}) -> p {' '.join(names)}", **{names[i]: dims[i] for i in range(len(dims))})


def modulation(M, S):
    t0 = M.ac.act(S["silc"], S["cvec"], ACT.Silu, *S["tx"])

    def piece(layer, g):
        b, fr = M.bank()
        for j in range(2):
            w, tok, s, h = M.weight("ada", layer, 2 * g + j)
            t = M.pe.mm([(M.ps[:, b, 2 * j:2 * j + 2], w[:, k, :], S["silc"][:, k, :], k == 0, k == 7) for k in range(8)],
                        tok, t0, *fr)
            M.done((w, tok, s, h), t)
        t = M.dv.tt(S["mods"][layer][:, 2 * g:2 * g + 2, :], M.ps[:, b, 0:4].rearrange("p (a b) -> p a b", b=2),
                    bc(S["vec2"][layer][0]["adab"][:, 2 * g:2 * g + 2].unsqueeze(2), [128, 2, 2]), ALU.add, t, *S["tx"])
        M.give(b, t)
    M.fills = [lambda l=l, g=g: piece(l, g) for l in range(2) for g in range(24)]


def first_block(M, A, S):
    pe, dv, ac, po, ps = M.pe, M.dv, M.ac, M.po, M.ps
    C, x = S["c"], S["x"]
    ident = C["ident"]
    ones = C["ones"]
    one = ones[:, 0:1]
    eps = S["eps"]
    tx = S["tx"]

    base = A.at
    ang, kk, r, pos = A(T), A(T), A(T), A(T)
    v0, _ = S["vec1"]
    t = dv.cp(pos, S["pos"], *tx)
    t = dv.ts(ang, pos, v0["inv"], None, ALU.mult, None, t)
    tabs = []
    for tab, shift in ((S["cos"], 0.25), (S["sin"], 0.0)):
        t = dv.ts(kk, ang, 0.15915494309189535, shift, ALU.mult, ALU.add, t)
        t = dv.ts(kk, kk, MAGIC, None, ALU.add, None, t)
        t = dv.ts(kk, kk, MAGIC, None, ALU.subtract, None, t)
        t = dv.stt(r, kk, -TWO_PI_1, ang, ALU.mult, ALU.add, t)
        t = dv.stt(r, kk, -TWO_PI_2, r, ALU.mult, ALU.add, t)
        t = dv.stt(r, kk, -TWO_PI_3, r, ALU.mult, ALU.add, t)
        if shift:
            t = dv.ts(r, r, 1.5707963267948966, None, ALU.add, None, t)
        t = dv.ts(r, r, 3.1415925, -3.1415925, ALU.min, ALU.max, t)
        t = ac.act(tab, r, ACT.Sin, t)
        tabs.append(t)
    A.at = base
    M.barrier()

    for layer in range(2):
        V, tv = S["vec1"] if layer == 0 else S["vec1b"]
        base = A.at
        xn = A.pair(8, T)
        mixed, gate, y, sq = (A(8, T) for _ in range(4))
        rs = A(8, T)
        keep = A.at

        def normed(src, dst, nt, inv, gain, lhs, w):
            t = M.stats(src, nt, nt, T, inv, lhs, rs, sq, eps, *w)
            f = sq[:, 0:nt, :]
            t = dv.tt(f, src, bc(rs[:, 0:1, :], [128, nt, T]), ALU.mult, t)
            t = dv.tt(f, f, bc(gain.unsqueeze(2), [128, nt, T]), ALU.mult, t)
            return M.split(dst, f, t)

        txn = normed(x, xn, 8, 1 / 1024, V["n1"], ones, [*tx, *tv])

        def branch_out(yop, ty, wname, gchunk, first):
            def eg(i, m, p, t):
                return [ac.act(gate[:, i:i + m, :], p, ACT.Sigmoid, t)]
            M.lin("win", layer, range(4 * gchunk, 4 * gchunk + 8), xn, T, eg, txn)
            tg = ac.here()

            def eo(i, m, p, t):
                if first:
                    return [dv.tt(mixed[:, i:i + m, :], p, gate[:, i:i + m, :], ALU.mult, t, tg)]
                t1 = dv.tt(gate[:, i:i + m, :], p, gate[:, i:i + m, :], ALU.mult, t, tg)
                dv.tt(mixed[:, i:i + m, :], mixed[:, i:i + m, :], gate[:, i:i + m, :], ALU.add, t1)
                return [t1]
            ys = A.pair(8, T)
            M.lin(wname, layer, range(8), ys, T, eo, M.split(ys, yop, ty))

        def conv(pad, dst, wname, tz, after):
            wv = V[wname]

            def ev(i0, m, p, t):
                tc = ac.cp(pad[:, i0:i0 + m, 3:3 + T], p, t)
                ts = [dv.ts(dst[:, i, :], pad[:, i, 0:T], wv[:, 4 * i:4 * i + 1], None, ALU.mult, None, tc, tz)
                      for i in range(i0, i0 + m)]
                for j in range(1, 4):
                    ts = [dv.stt(dst[:, i, :], pad[:, i, j:j + T], wv[:, 4 * i + j:4 * i + j + 1], dst[:, i, :],
                                 ALU.mult, ALU.add, ts[i - i0]) for i in range(i0, i0 + m)]
                after(i0, m, ts[-1])
                return [tc]
            return ev

        sm, sp, sa, sb_, sc = A(2, 32), A(2, 24), A(2, 24), A(2, 24), A(2, 24)
        smask = A(48)
        beta, dA, cum = A(2, 8), A(2, 24), A(2, 24)
        tot, etot = A(5, 16), A(5, 16)
        keep = A.at
        M.lint("wsm", layer, [0], xn, 2, lambda m, c0, p, t: [ac.cp(sm[:, m, :], p, t)], txn)
        t = dv.tt(sp, sm[:, :, 0:24], bc(V["bias"].unsqueeze(1), [128, 2, 24]), ALU.add, ac.here())
        ta = ac.act(sa, sp, ACT.Abs, t)
        te = ac.act(sa, sa, ACT.Exp, ta, scale=-1.0)
        tl = ac.act(sb_, sa, ACT.Ln, te, bias=one)
        t = dv.ts(sc, sa, 1 / 3, -0.5, ALU.mult, ALU.add, te)
        t = dv.tt(sc, sc, sa, ALU.mult, t)
        t = dv.stt(sc, sc, 1.0, sa, ALU.add, ALU.mult, t)
        tk = dv.ts(smask.rearrange("p (a b) -> p a b", a=2), sa, 0.01, None, ALU.is_lt, None, te)
        t = dv.pick(sb_.rearrange("p a b -> p (a b)"), smask.bitcast(I32), sc.rearrange("p a b -> p (a b)"), t, tk, tl)
        t = dv.stt(sp, sp, 0.0, sb_, ALU.max, ALU.add, t)
        ta = ac.act(sc[:, 0, :], V["alog"], ACT.Exp, t)
        t = dv.stt(dA, sp, -1.0, bc(sc[:, 0:1, :], [128, 2, 24]), ALU.mult, ALU.mult, t, ta)
        tb = ac.act(beta, sm[:, :, 24:32], ACT.Sigmoid)
        b, fr = M.bank()
        P = ps[:, b, 0:48].rearrange("p (a b) -> p a b", a=2)
        Q = ps[:, b, 64:144].rearrange("p (a b) -> p a b", a=5)
        parts = []
        for c in range(2):
            parts += [(P[:, c, 0:16], C["tri"], dA[:, c, 0:16], True, True),
                      (P[:, c, 16:24], C["btri"], dA[:, c, 16:24], True, True),
                      (Q[:, 2 * c, 0:8], C["cone0"], dA[:, c, 16:24], True, True),
                      (Q[:, 2 * c + 1, 0:8], C["cone1"], dA[:, c, 16:24], True, True)]
        parts += [(Q[:, 4, 0:16], ones, dA[:, 0, 0:16], True, True)]
        tm = pe.mm(parts, t, *fr)
        t1 = ac.cp(cum, P, tm)
        t2 = ac.cp(tot[:, 0:4, 0:8], Q[:, 0:4, 0:8], tm)
        t3 = ac.cp(tot[:, 4, :], Q[:, 4, :], tm)
        t4 = ac.act(etot[:, 0:4, 0:8], Q[:, 0:4, 0:8], ACT.Exp, tm)
        M.give(b, t4)
        ts_ = [t4, tb, t]

        acc = A(16, T)
        z = A(8, T)
        top = A.at
        pad = A(16, T + 3)
        tz = po.fill(pad[:, :, 0:3], 0.0)
        M.lin("win", layer, range(0, 16), xn, T, conv(pad, acc, "gw", tz, lambda i, m, t: ac.act(
            acc[:, i:i + m, :], acc[:, i:i + m, :], ACT.Silu, t)), txn)
        tsl = ac.here()
        M.lin("win", layer, range(44, 52), xn, T, lambda i, m, p, t: [ac.act(z[:, i:i + m, :], p, ACT.Silu, t)], txn)
        tzz = ac.here()
        A.at = top
        t = M.stats(acc[:, 0:8, :], 8, 1, T, 1.0, ones, rs, sq, eps, tsl)
        tq = dv.stt(acc[:, 0:4, :], acc[:, 0:4, :], 128 ** -0.5, rs[:, 0:4, :], ALU.mult, ALU.mult, t)
        tk = dv.tt(acc[:, 4:8, :], acc[:, 4:8, :], rs[:, 4:8, :], ALU.mult, t)
        qT, kT, vT = acc[:, 0:4, :], acc[:, 4:8, :], acc[:, 8:16, :]
        M.barrier()
        ktok, vtok = A(2, 4, 128), A(2, 8, 128)
        qkT, qg = A(16, 128), A(8, T)
        AT, X, XT = (A(16, 128) for _ in range(3))
        Y = mixed.rearrange("p a (b c) -> p (a b) c", c=128)
        BT = gate.rearrange("p a (b c) -> p (a b) c", c=128)
        u, wT = X, BT
        for c in range(2):
            cs = slice(c * 128, c * 128 + 128)
            b, fr = M.bank()
            t = pe.tr([(ps[:, b, h * 128:h * 128 + 128], kT[:, h, cs]) for h in range(4)], ident, tk, *fr)
            M.give(b, M.copy(ktok[:, c, :, :].rearrange("p a b -> p (a b)"), ps[:, b, :], t))
            for g in range(2):
                b, fr = M.bank()
                t = pe.tr([(ps[:, b, h * 128:h * 128 + 128], vT[:, 4 * g + h, cs]) for h in range(4)], ident, tsl, *fr)
                M.give(b, dv.tt(vtok[:, c, 4 * g:4 * g + 4, :], ps[:, b, :].rearrange("p (a b) -> p a b", a=4),
                                bc(beta[:, c, 4 * g:4 * g + 4].unsqueeze(2), [128, 4, 128]), ALU.mult, t, tb))
        tat = {}
        for c in range(2):
            cs = slice(c * 128, c * 128 + 128)
            for g in range(2):
                p0 = c * 8 + 4 * g
                b, fr = M.bank()
                t = pe.mm([(ps[:, b, j * 128:j * 128 + 128], bc(dA[:, c, 16 + 4 * g + j:17 + 4 * g + j], [128, 128]),
                            C["btri"], True, True) for j in range(4)], *ts_, *fr)
                P = ps[:, b, :].rearrange("p (a b) -> p a b", a=4)
                D = Y[:, p0:p0 + 4, :]
                te = ac.act(qg[:, 4 * g:4 * g + 4, cs], P, ACT.Exp, t)
                t1 = dv.tt(D, P, bc(cum[:, c, 16 + 4 * g:20 + 4 * g].unsqueeze(2), [128, 4, 128]), ALU.subtract, t, te)
                M.give(b, te, t1)
                t1 = dv.ts(D, D, 0.0, None, ALU.min, None, t1)
                td = ac.act(D, D, ACT.Exp, t1)
                qv = qT[:, 2 * g:2 * g + 2, cs].unsqueeze(2)
                t1 = dv.tt(qg[:, 4 * g:4 * g + 4, cs].rearrange("p (a r) t -> p a r t", r=2),
                           qg[:, 4 * g:4 * g + 4, cs].rearrange("p (a r) t -> p a r t", r=2),
                           bc(qv, [128, 2, 2, 128]), ALU.mult, te)
                b, fr = M.bank()
                parts = []
                for j in range(2):
                    h = 2 * g + j
                    parts += [(ps[:, b, j * 256:j * 256 + 128], kT[:, h, cs], kT[:, h, cs], True, True),
                              (ps[:, b, j * 256 + 128:j * 256 + 256], kT[:, h, cs], qT[:, h, cs], True, True)]
                t = pe.mm(parts, tq, tk, *fr)
                P = ps[:, b, :].rearrange("p (j w t) -> p j w t", j=2, w=2)
                D4 = D.rearrange("p (a r) t -> p a r t", r=2)
                t1 = dv.tt(AT[:, p0:p0 + 4, :].rearrange("p (a r) t -> p a r t", r=2), D4,
                           bc(P[:, :, 0:1, :], [128, 2, 2, 128]), ALU.mult, td, t)
                t2 = dv.tt(qkT[:, p0:p0 + 4, :].rearrange("p (a r) t -> p a r t", r=2), D4,
                           bc(P[:, :, 1:2, :], [128, 2, 2, 128]), ALU.mult, td, t)
                M.give(b, t1, t2)
                t2 = po.tt(qkT[:, p0:p0 + 4, :], qkT[:, p0:p0 + 4, :], bc(C["btri"].unsqueeze(1), [128, 4, 128]), ALU.mult, t2)
                t1 = dv.tt(AT[:, p0:p0 + 4, :], AT[:, p0:p0 + 4, :], bc(C["bstrict"].unsqueeze(1), [128, 4, 128]), ALU.mult, t1)
                tat[c, g] = t1
        order = [(c, g) for c in range(2) for g in range(2)]
        tab = {}
        for c, g in order:
            if True:
                p0 = c * 8 + 4 * g
                t1 = tat[c, g]
                b, fr = M.bank()
                t = pe.tr([(ps[:, b, j * 128:j * 128 + 128], AT[:, p0 + j, :]) for j in range(4)], ident, t1, *fr)
                A4 = BT[:, p0:p0 + 4, :]
                t = dv.tt(A4, ps[:, b, :].rearrange("p (a b) -> p a b", a=4),
                          bc(beta[:, c, 4 * g:4 * g + 4].unsqueeze(2), [128, 4, 128]), ALU.mult, t, tb)
                M.give(b, t)
                tab[c, g] = t
        for c, g in order:
            if True:
                p0 = c * 8 + 4 * g
                t = tab[c, g]
                A4 = BT[:, p0:p0 + 4, :]
                b, fr = M.bank()
                t1 = pe.tr([(ps[:, b, j * 128:j * 128 + 128], A4[:, j, :]) for j in range(4)], ident, t, *fr)
                t1 = ac.cp(AT[:, p0:p0 + 4, :], ps[:, b, :].rearrange("p (a b) -> p a b", a=4), t1)
                M.give(b, t1)
                idb = bc(ident.unsqueeze(1), [128, 4, 128])
                t = po.tt(X[:, p0:p0 + 4, :], A4, bc(C["m0"].unsqueeze(1), [128, 4, 128]), ALU.mult, t)
                t = po.tt(X[:, p0:p0 + 4, :], idb, X[:, p0:p0 + 4, :], ALU.subtract, t)
                t = po.tt(XT[:, p0:p0 + 4, :], AT[:, p0:p0 + 4, :], bc(C["t0"].unsqueeze(1), [128, 4, 128]), ALU.mult, t1)
                t = po.tt(XT[:, p0:p0 + 4, :], idb, XT[:, p0:p0 + 4, :], ALU.subtract, t)
        M.barrier()
        tX = [[] for _ in range(4)]
        tB = [[] for _ in range(4)]
        for lev in range(1, 6):
            for q in range(4):
                p0 = 4 * q
                s4 = slice(p0, p0 + 4)
                eng = po
                tb4 = eng.tt(BT[:, s4, :], AT[:, s4, :], bc(C[f"t{lev}"].unsqueeze(1), [128, 4, 128]), ALU.mult, *tB[q])
                b, fr = M.bank()
                t = pe.mm([(ps[:, b, j * 128:j * 128 + 128], BT[:, p0 + j, :], X[:, p0 + j, :], True, True)
                           for j in range(4)], tb4, *tX[q], *fr)
                tB[q] = [t]
                ty = ac.cp(Y[:, s4, :].rearrange("p a b -> p (a b)"), ps[:, b, :], t, *tX[q])
                M.give(b, ty)
                b2, fr2 = M.bank()
                t2 = pe.mm([(ps[:, b2, j * 128:j * 128 + 128], Y[:, p0 + j, :], XT[:, p0 + j, :], True, True)
                            for j in range(4)], ty, *fr2)
                if lev < 5:
                    b1, fr1 = M.bank()
                    t1 = pe.mm([(ps[:, b1, j * 128:j * 128 + 128], XT[:, p0 + j, :], Y[:, p0 + j, :], True, True)
                                for j in range(4)], ty, *fr1)
                    ta = dv.tt(X[:, s4, :], X[:, s4, :], ps[:, b1, :].rearrange("p (a b) -> p a b", a=4), ALU.subtract, t1)
                    M.give(b1, ta)
                    t2 = t1
                tc = dv.tt(XT[:, s4, :], XT[:, s4, :], ps[:, b2, :].rearrange("p (a b) -> p a b", a=4), ALU.subtract, t2)
                M.give(b2, tc)
                tX[q] = [tc, t2]
                if q == 3:
                    M.fill(1)
        M.barrier()
        kd, kbg = AT, Y
        eg = sc[:, :, 0:8]
        eb = sc[:, :, 8:16]
        ed = sc[:, :, 16:24]
        t = ac.act(eg, cum[:, :, 16:24], ACT.Exp)
        teb = dv.tt(eb, eg, beta, ALU.mult, t)
        for c in range(2):
            for half in range(2):
                hp = slice(64 * half, 64 * half + 64)
                t = dv.tt(ed[hp, c, :], tot[hp, 2 * c + half, 0:8], cum[hp, c, 16:24], ALU.subtract)
        ted = ac.act(ed, ed, ACT.Exp, t)
        for c in range(2):
            kv = bc(ktok[:, c, :, :].unsqueeze(2), [128, 4, 2, 128])
            for dst, s, tw, q in ((kbg, eb, teb, dv), (kd, ed, ted, dv)):
                sv = s[:, c, :].rearrange("p (a r) -> p a r", r=2).unsqueeze(3)
                tlast = q.tt(dst[:, 8 * c:8 * c + 8, :].rearrange("p (a r) t -> p a r t", r=2), kv,
                             bc(sv, [128, 4, 2, 128]), ALU.mult, tw)
        for q in range(4):
            c, g = q // 2, q % 2
            b, fr = M.bank()
            t = pe.mm([(ps[:, b, j * 128:j * 128 + 128], XT[:, 4 * q + j, :], vtok[:, c, 4 * g + j, :], True, True)
                       for j in range(4)], *fr)
            M.give(b, ac.cp(u[:, 4 * q:4 * q + 4, :].rearrange("p a b -> p (a b)"), ps[:, b, :], t))
            b, fr = M.bank()
            t = pe.mm([(ps[:, b, j * 128:j * 128 + 128], kbg[:, 4 * q + j, :], XT[:, 4 * q + j, :], True, True)
                       for j in range(4)], tlast, *fr)
            M.give(b, ac.cp(wT[:, 4 * q:4 * q + 4, :].rearrange("p a b -> p (a b)"), ps[:, b, :], t))
        tuw = ac.here()
        STs = [XT[:, 0:8, :], XT[:, 8:16, :]]
        tS = [[], []]
        tread = [[], []]
        o = y
        for n in range(4):
            c, half = n // 2, n % 2
            hp = slice(64 * half, 64 * half + 64)
            cols = slice(64 * n, 64 * n + 64)
            lc = slice(64 * half, 64 * half + 64)
            ST, SN = STs[n % 2], STs[1 - n % 2]
            tvn = []
            for g in range(2):
                p0 = 8 * c + 4 * g
                if n:
                    b, fr = M.bank()
                    t = pe.mm([(ps[:, b, j * 128:j * 128 + 128], wT[:, p0 + j, :], ST[:, 4 * g + j, :], True, True)
                               for j in range(4)], *tS[g], tuw, *fr)
                    tv_ = dv.tt(u[hp, p0:p0 + 4, :], u[hp, p0:p0 + 4, :],
                                ps[hp, b, :].rearrange("p (a b) -> p a b", a=4), ALU.subtract, t)
                    M.give(b, tv_)
                else:
                    tv_ = tuw
                tvn.append(tv_)
            if n < 3:
                for g in range(2):
                    p0 = 8 * c + 4 * g
                    b, fr = M.bank()
                    t2 = pe.mm([(ps[:, b, j * 128:j * 128 + 128], kd[hp, p0 + j, :], u[hp, p0 + j, :], True, True)
                                for j in range(4)], tvn[g], tlast, *fr)
                    P = ps[:, b, :].rearrange("p (a b) -> p a b", a=4)
                    new = SN[:, 4 * g:4 * g + 4, :]
                    if n:
                        t1 = dv.tt(new, ST[:, 4 * g:4 * g + 4, :],
                                   bc(etot[:, n, 4 * g:4 * g + 4].unsqueeze(2), [128, 4, 128]), ALU.mult, *tS[g], *tread[g])
                        t1 = dv.tt(new, new, P, ALU.add, t1, t2)
                    else:
                        t1 = dv.cp(new, P, t2, tuw)
                    M.give(b, t1)
                    tnew = [*(tnew if g else []), t1]
            M.fill(1)
            for g in range(2):
                p0 = 8 * c + 4 * g
                b, fr = M.bank()
                parts = []
                for j in range(4):
                    oo = ps[:, b, j * 64:j * 64 + 64]
                    if n:
                        parts.append((oo, ST[:, 4 * g + j, :], qg[:, 4 * g + j, cols], True, False))
                    parts.append((oo, u[hp, p0 + j, :], qkT[hp, p0 + j, lc], n == 0, True))
                t = pe.mm(parts, tvn[g], *tS[g], *fr)
                M.give(b, ac.cp(o[:, 4 * g:4 * g + 4, cols], ps[:, b, 0:256].rearrange("p (a b) -> p a b", a=4), t))
                tread[g] = [t]
            to = ac.here()
            if n < 3:
                tS = [[t] for t in tnew]
            M.fill(1)
        t = M.stats(o, 8, 1, T, 1 / 128, ones, rs, sq, eps, to)
        t = dv.tt(o, o, rs, ALU.mult, t)
        ty = dv.stt(o, o, V["gn"], z, ALU.mult, ALU.mult, t, tzz)
        M.barrier()
        A.at = keep
        branch_out(o, ty, "wgo", 17, True)
        M.barrier()
        A.at = keep

        acc = A(12, T)
        z = A(8, T)
        top = A.at
        pad = A(12, T + 3)
        tz = po.fill(pad[:, :, 0:3], 0.0)
        def biased(i0, m, t):
            for i in range(i0, i0 + m):
                ac.act(acc[:, i, :], acc[:, i, :], ACT.Silu, t, bias=V["cb"][:, i:i + 1])
        M.lin("win", layer, range(16, 28), xn, T, conv(pad, acc, "cw", tz, biased), txn)
        ta = ac.here()
        M.lin("win", layer, range(36, 44), xn, T, lambda i, m, p, t: [ac.act(z[:, i:i + m, :], p, ACT.Silu, t)], txn)
        M.barrier()
        A.at = top
        Xd, Xs, Bt, Hs = A(2, 1024), A(1024), A(2, 128), A(2, 512)
        CB, L2, ytok = A(2, 2, 128), A(2, 16, 128), A(1024)
        tl = ac.act(sc[:, 0, 0:16], cum[:, 0, 0:16], ACT.Identity, scale=-1.0)
        t = dv.tt(sc[:, 0, 0:16], sc[:, 0, 0:16], tot[:, 4, :], ALU.add, tl)
        tdec = ac.act(sc[:, 0, 0:16], sc[:, 0, 0:16], ACT.Exp, t)
        teA = ac.act(sc[:, 1, 0:16], cum[:, 1, 0:16], ACT.Exp)
        txs, tcbs, tes = [], [], []
        for c in range(2):
            cs = slice(c * 128, c * 128 + 128)
            txd = []
            for g in range(2):
                b, fr = M.bank()
                t = pe.tr([(ps[:, b, j * 128:j * 128 + 128], acc[:, 4 * g + j, cs]) for j in range(4)], ident, ta, *fr)
                t = dv.tt(Xd[:, c, 512 * g:512 * g + 512].rearrange("p (h d) -> p h d", d=64),
                          ps[:, b, :].rearrange("p (h d) -> p h d", d=64),
                          bc(sp[:, c, 8 * g:8 * g + 8].unsqueeze(2), [128, 8, 64]), ALU.mult, t)
                M.give(b, t)
                txd.append(t)
            b, fr = M.bank()
            t = pe.mm([(ps[:, b, g * 128:g * 128 + 128], acc[:, 8 + g, cs], acc[:, 10 + g, cs], True, True)
                       for g in range(2)], ta, *fr)
            tcb = dv.tt(CB[:, c, :, :], ps[:, b, 0:256].rearrange("p (a b) -> p a b", a=2),
                        bc(C["tri"].unsqueeze(1), [128, 2, 128]), ALU.mult, t)
            M.give(b, tcb)
            txs.append(txd)
            tcbs.append(tcb)
        for c in range(2):
            te = []
            L = L2[:, c, :, :]
            for q in range(4):
                s4 = slice(4 * q, 4 * q + 4)
                b, fr = M.bank()
                t = pe.mm([(ps[:, b, j * 128:j * 128 + 128], bc(dA[:, c, 4 * q + j:4 * q + j + 1], [128, 128]),
                            C["tri"], True, True) for j in range(4)], *fr)
                t1 = dv.tt(L[:, s4, :], ps[:, b, :].rearrange("p (a b) -> p a b", a=4),
                           bc(cum[:, c, s4].unsqueeze(2), [128, 4, 128]), ALU.subtract, t)
                M.give(b, t1)
                t1 = dv.ts(L[:, s4, :], L[:, s4, :], 0.0, None, ALU.min, None, t1)
                t1 = ac.act(L[:, s4, :], L[:, s4, :], ACT.Exp, t1)
                te.append(po.tt(L[:, s4, :], L[:, s4, :], bc(CB[:, c, q // 2:q // 2 + 1, :], [128, 4, 128]), ALU.mult, t1, tcbs[c]))
            tes.append(te)
            M.fill(1)
            if c == 0:
                cs = slice(0, 128)
                b, fr = M.bank()
                t = pe.tr([(ps[:, b, g * 128:g * 128 + 128], acc[:, 8 + g, cs]) for g in range(2)], ident, ta, *fr)
                tbt = ac.cp(Bt.rearrange("p a b -> p (a b)"), ps[:, b, 0:256], t)
                M.give(b, tbt)
                tx_ = dv.tt(Xs.rearrange("p (h d) -> p h d", d=64), Xd[:, 0, :].rearrange("p (h d) -> p h d", d=64),
                            bc(sc[:, 0, 0:16].unsqueeze(2), [128, 16, 64]), ALU.mult, tdec, *txs[0])
                for g in range(2):
                    b, fr = M.bank()
                    t = pe.mm([(ps[:, b, :], Bt[:, g, :], Xs[:, 512 * g:512 * g + 512], True, True)], tx_, tbt, *fr)
                    th = ac.cp(Hs[:, g, :], ps[:, b, :], t)
                    M.give(b, th)
        for c in range(2):
            cs = slice(c * 128, c * 128 + 128)
            L, te, txd = L2[:, c, :, :], tes[c], txs[c]
            tyt = []
            for g in range(2):
                b, fr = M.bank()
                t = pe.mm([(ps[:, b, 64 * h:64 * h + 64], L[:, 8 * g + h, :],
                            Xd[:, c, 512 * g + 64 * h:512 * g + 64 * h + 64], True, True) for h in range(8)],
                          *te[2 * g:2 * g + 2], *txd, *fr)
                if c == 0:
                    t1 = ac.cp(ytok[:, 512 * g:512 * g + 512], ps[:, b, :], t)
                    M.give(b, t1)
                else:
                    b2, fr2 = M.bank()
                    t2 = pe.mm([(ps[:, b2, :], acc[:, 10 + g, cs], Hs[:, g, :], True, True)], th, *fr2)
                    t1 = dv.tt(ytok[:, 512 * g:512 * g + 512].rearrange("p (h d) -> p h d", d=64),
                               ps[:, b2, :].rearrange("p (h d) -> p h d", d=64),
                               bc(sc[:, 1, 8 * g:8 * g + 8].unsqueeze(2), [128, 8, 64]), ALU.mult, t2, teA, *tyf)
                    M.give(b2, t1)
                    t1 = dv.tt(ytok[:, 512 * g:512 * g + 512], ytok[:, 512 * g:512 * g + 512], ps[:, b, :], ALU.add, t1, t)
                    M.give(b, t1)
                tyt.append(t1)
            tyf = []
            M.fill(1)
            for g in range(2):
                b, fr = M.bank()
                t = pe.tr([(ps[:, b, j * 128:j * 128 + 128], ytok[:, (4 * g + j) * 128:(4 * g + j) * 128 + 128])
                           for j in range(4)], ident, tyt[g], *fr)
                tyf.append(t)
                for j in range(4):
                    i = 4 * g + j
                    t1 = dv.stt(y[:, i, cs], acc[:, i, cs], V["sd"][:, i:i + 1], ps[:, b, j * 128:j * 128 + 128],
                                ALU.mult, ALU.add, t)
                M.give(b, t1)
        t = dv.tt(y, y, z, ALU.mult, t1)
        t = M.stats(y, 8, 4, T, 1 / 512, ones, rs, sq, eps, t)
        for g in range(2):
            t = dv.tt(y[:, 4 * g:4 * g + 4, :], y[:, 4 * g:4 * g + 4, :], bc(rs[:, g:g + 1, :], [128, 4, T]), ALU.mult, t)
        ty = dv.tt(y, y, bc(V["sn"].unsqueeze(2), [128, 8, T]), ALU.mult, t)
        M.barrier()
        A.at = keep
        branch_out(y, ty, "wso", 13, False)
        M.barrier()
        A.at = keep

        lat = A(8, T)
        M.lin("win", layer, range(28, 36), xn, T,
              lambda i, m, p, t: [M.copy(lat[:, i:i + m, :], p, t)], txn)
        tl = [ac.here(), dv.here()]
        qn, kn = A.pair(4, T), A.pair(2, T)
        q12, kT, vt = A(12, T), A(8, T), A(2, 1024)
        Pm, PT, ot = A(8, T), A(8, 2, 128), A(8, 128)
        mx, den = A(16), A(16)
        tq = normed(lat[:, 0:4, :], qn, 4, 1 / 512, V["qn"], ones, tl)
        t = M.stats(lat[:, 4:6, :], 2, 2, T, 1 / 256, ones, rs, sq, eps, tq)
        f = sq[:, 0:2, :]
        t = dv.tt(f, lat[:, 4:6, :], bc(rs[:, 0:1, :], [128, 2, T]), ALU.mult, t)
        t = dv.tt(f, f, bc(V["kn"].unsqueeze(2), [128, 2, T]), ALU.mult, t)
        tk = M.split(kn, f, t)
        M.lin("wuq", layer, range(6), qn, T, lambda i, m, p, t: [M.copy(q12[:, i:i + m, :], p, t)], tq)
        tqq = [ac.here(), dv.here()]
        M.lin("wuk", layer, range(2), kn, T, lambda i, m, p, t: [M.copy(kT[:, i:i + m, :], p, t)], tk)
        M.lint("wuv", layer, range(2), kn, 2, lambda m, c0, p, t: [M.copy(vt[:, m, c0:c0 + 512], p, t)], tk)
        tkk = [ac.here(), dv.here()]

        def rope(a, bb, n, w):
            cs_, sn_ = (bc(S[k].unsqueeze(1), [128, n, T]) for k in ("cos", "sin"))
            m1, m2 = sq[:, 0:n, :], sq[:, 4:4 + n, :]
            t1 = dv.tt(m1, bb, sn_, ALU.mult, *w)
            t2 = dv.tt(m2, a, sn_, ALU.mult, *w)
            t3 = dv.tt(a, a, cs_, ALU.mult, t2)
            t4 = dv.tt(bb, bb, cs_, ALU.mult, t1)
            t3 = dv.tt(a, a, m1, ALU.subtract, t3)
            return dv.tt(bb, bb, m2, ALU.add, t4)

        trk = rope(lat[:, 6:7, :], lat[:, 7:8, :], 1, [*tl, pe.here(), dv.here(), *tabs])
        trq = rope(q12[:, 8:10, :], q12[:, 10:12, :], 2, [*tqq, dv.here()])
        M.barrier()
        scale = 192 ** -0.5
        tpf, ttf = [[], []], [[], []]
        tof = []
        got = {}

        def scores(i, hp):
            nk = 128 * (i + 1)
            qs = slice(i * 128, i * 128 + 128)
            s = hp % 2
            Pv = Pm[:, 2 * s:2 * s + 2, :]
            b, fr = M.bank()
            parts = []
            for j in range(2):
                h = hp + 4 * j
                r = slice(32 * hp, 32 * hp + 32)
                o_ = ps[:, b, 256 * j:256 * j + nk]
                parts += [(o_, q12[:, h, qs], kT[:, h, 0:nk], True, False),
                          (o_, q12[r, 8 + h // 4, qs], lat[r, 6, 0:nk], False, False),
                          (o_, q12[r, 10 + h // 4, qs], lat[r, 7, 0:nk], False, True)]
            t = pe.mm(parts, trk, trq, *tkk, *fr)
            P = ps[:, b, :].rearrange("p (a b) -> p a b", a=2)
            dg = slice(128 * i, 128 * i + 128)
            t1 = [dv.tt(Pv[:, :, dg], P[:, :, dg], bc(C["causal"].unsqueeze(1), [128, 2, 128]), ALU.add, t, *tpf[s])]
            if i:
                t1.append(dv.cp(Pv[:, :, 0:128], P[:, :, 0:128], t, *tpf[s]))
            M.give(b, *t1)
            k0 = 8 * i + 2 * hp
            t1 = dv.red(mx[:, k0:k0 + 2], Pv[:, :, 0:nk], ALU.max, *t1)
            t1 = dv.ts(mx[:, k0:k0 + 2], mx[:, k0:k0 + 2], -scale, None, ALU.mult, None, t1)
            for j in range(2):
                te = ac.act(Pv[:, j, 0:nk], Pv[:, j, 0:nk], ACT.Exp, t1, bias=mx[:, k0 + j:k0 + j + 1],
                            scale=scale, acc=den[:, k0 + j:k0 + j + 1])
            got["e", i, hp] = te

        def turned(i, hp):
            s = hp % 2
            Pv = Pm[:, 2 * s:2 * s + 2, :]
            b, fr = M.bank()
            t = pe.tr([(ps[:, b, (2 * j + kb) * 128:(2 * j + kb) * 128 + 128], Pv[:, j, kb * 128:kb * 128 + 128])
                       for j in range(2) for kb in range(i + 1)], ident, got["e", i, hp], *fr)
            tpf[s] = [t]
            PTv = PT[:, 2 * s:2 * s + 2, :, :]
            t = ac.cp(PTv[:, :, 0:i + 1, :], ps[:, b, :].rearrange("p (a k b) -> p a k b", a=2, k=2)[:, :, 0:i + 1, :],
                      t, *ttf[s])
            M.give(b, t)
            got["p", i, hp] = t

        def mixed_values(i, hp):
            s = hp % 2
            qs = slice(i * 128, i * 128 + 128)
            k0 = 8 * i + 2 * hp
            td = dv.recip(den[:, k0:k0 + 2], den[:, k0:k0 + 2], got["e", i, hp])
            PTv = PT[:, 2 * s:2 * s + 2, :, :]
            b, fr = M.bank()
            t = pe.mm([(ps[:, b, 128 * j:128 * j + 128], PTv[:, j, kb, :], vt[:, kb, (hp + 4 * j) * 128:(hp + 4 * j) * 128 + 128],
                        kb == 0, kb == i) for j in range(2) for kb in range(i + 1)], got["p", i, hp], *fr)
            ttf[s] = [t]
            t = dv.tt(ot[:, hp:hp + 5:4, :], ps[:, b, 0:256].rearrange("p (a b) -> p a b", a=2),
                      bc(den[:, k0:k0 + 2].unsqueeze(2), [128, 2, 128]), ALU.mult, t, td, *(tof if i else []))
            M.give(b, t)
            if hp == 3:
                for g in range(2):
                    b, fr = M.bank()
                    t1 = pe.tr([(ps[:, b, j * 128:j * 128 + 128], ot[:, 4 * g + j, :]) for j in range(4)], ident, t, *fr)
                    tof.append(t1)
                    M.give(b, ac.cp(y[:, 4 * g:4 * g + 4, qs], ps[:, b, :].rearrange("p (a b) -> p a b", a=4), t1))

        steps = [(i, hp) for i in range(2) for hp in range(4)]
        for n in range(len(steps) + 2):
            if n < len(steps):
                scores(*steps[n])
            if 1 <= n <= len(steps):
                turned(*steps[n - 1])
            if n >= 2:
                mixed_values(*steps[n - 2])
            M.fill(1 if n % 2 else 0)
        ty = ac.here()
        M.barrier()
        A.at = keep
        branch_out(y, ty, "wmo", 15, False)
        tm = dv.here()

        def res(i, m, p, t):
            return [dv.tt(x[:, i:i + m, :], x[:, i:i + m, :], p, ALU.add, t)]
        ms = A.pair(8, T)
        M.lin("wo", layer, range(8), ms, T, res, M.split(ms, mixed, tm))
        txn = normed(x, xn, 8, 1 / 1024, V["n2"], ones, [dv.here()])
        M.barrier()
        A.at = keep
        hid = A.pair(32, T)
        tmp = [A(2, T) for _ in range(3)]
        free = [[] for _ in range(3)]

        def up(i, m, p, t):
            s = (i // 2) % 3
            f = tmp[s]
            t1 = ac.act(f, p, ACT.Relu, t, *free[s])
            t2 = dv.tt(f, f, f, ALU.mult, t1)
            free[s] = [M.split([v[:, i:i + 2, :] for v in hid], f, t2)]
            return [t1]
        M.lin("wup", layer, range(32), xn, T, up, txn)
        M.lin("wdn", layer, range(8), hid, T, res, dv.here())
        tx = [dv.here()]
        A.at = base
        M.barrier()

    base = A.at
    sq, rs = A(8, T), A(8, T)
    t = M.stats(x, 8, 8, T, 1 / 1024, ones, rs, sq, eps, *tx)
    t = dv.tt(x, x, bc(rs[:, 0:1, :], [128, 8, T]), ALU.mult, t)
    t = dv.tt(x, x, bc(S["vec1"][0]["fn"].unsqueeze(2), [128, 8, T]), ALU.mult, t)
    A.at = base
    M.barrier()
    return t


def second_block(M, A, S, tx0):
    pe, dv, ac, po, ps = M.pe, M.dv, M.ac, M.po, M.ps
    C, x = S["c"], S["x2"]
    ident, ones, eps = C["ident"], C["ones"], S["eps"]
    LAT, CTX = slice(0, 256), slice(256, 512)
    cases = (LAT, CTX)
    tx = [tx0, *S["tx"]]
    for layer in range(2):
        V, tv = S["vec2"][layer]
        last = layer == 1
        base = A.at
        mod, A1, A2 = S["mods"][layer], A(8, 2), A(8, 2)
        h = A.pair(8, 512)
        early = A.at
        tmp = A(6144)
        sq = tmp[:, 0:4096].rearrange("p (a b) -> p a b", a=8)
        rs = tmp[:, 4096:6144].rearrange("p (a b) -> p a b", a=4)
        keep = A.at

        M.fill(1000)
        tmod = dv.here()
        for dst, g, off in ((A1, "n1", 8), (A2, "n2", 32)):
            tmod = dv.stt(dst, mod[:, off:off + 8, :], 1.0, bc(V[g].unsqueeze(2), [128, 8, 2]), ALU.add, ALU.mult, tmod)

        def modulated(Am, off, n, w):
            t = M.stats(x[:, :, 0:n], 8, 8, n, 1 / 1024, ones, rs, sq, eps, *w)
            t = dv.tt(sq[:, :, 0:n], x[:, :, 0:n], bc(rs[:, 0:1, 0:n], [128, 8, n]), ALU.mult, t)
            for case in range(n // 256):
                hv = sq[:, :, cases[case]]
                t1 = dv.tt(hv, hv, bc(Am[:, :, case:case + 1], [128, 8, 256]), ALU.mult, t)
                t1 = dv.tt(hv, hv, bc(mod[:, off:off + 8, case:case + 1], [128, 8, 256]), ALU.add, t1)
            return M.split([v[:, :, 0:n] for v in h], sq[:, :, 0:n], t1)

        def onto_x(goff, n):
            def ev(i, m, p, t):
                for j in range(m):
                    for case in range(n // 256):
                        s = cases[case]
                        t1 = dv.stt(x[:, i + j, s], p[:, j, s], mod[:, goff + i + j, case:case + 1], x[:, i + j, s],
                                    ALU.mult, ALU.add, t)
                return [t1]
            return ev

        th = modulated(A1, 0, 512, [*tx, tmod])
        M.barrier()
        if layer == 0:
            q, k, vt = A(8, 512), A(8, 512), A(4, 1024)
            P4, PT4, ot = A(4, 512), A(4, 512), A(1024)
            den, mx = A(8, 16), A(8, 16)
            M.lin("nqkv", 0, range(8), h, 512, lambda i, m, p, t: [M.copy(q[:, i:i + m, :], p, t)], th)
            M.lin("nqkv", 0, range(8, 16), h, 512, lambda i, m, p, t: [M.copy(k[:, i:i + m, :], p, t)], th)
            tqk = [ac.here(), dv.here()]
            M.lint("nqkv", 0, range(16, 24), h, 4, lambda m, c0, p, t: [M.copy(vt[:, m, c0:c0 + 128], p, t)], th)
            tvv = [ac.here(), dv.here()]
            w = tqk
            for src, gain, f in ((q, "qg", 0.125), (k, "kg", 1.0)):
                for g in range(2):
                    s4 = slice(4 * g, 4 * g + 4)
                    t = M.stats(src[:, s4, :], 4, 1, 512, 1 / 64, C["bd64"], rs, sq, eps, *w)
                    t = dv.tt(src[:, s4, :], src[:, s4, :], rs, ALU.mult, t)
                    w = [t]
                t = dv.ts(src, src, V[gain], f, ALU.mult, ALU.mult, t)
                w = [t]
            M.barrier()
            bias = sq
            oF = h
            tpf, ttf = [[] for _ in range(4)], [[] for _ in range(4)]
            tbw = [[], []]
            bt = {}
            tof, got = [], {}

            def scores(i, hp):
                qs = slice(128 * i, 128 * i + 128)
                lat = i < 2
                ks = slice(0, 512) if lat else CTX
                k0 = 0 if lat else 256
                bs = (hp // 4) % 2
                bv = bias[:, 4 * bs:4 * bs + 4, :].rearrange("p a (b c) -> p (a b) c", c=256)
                if lat and hp % 4 == 0:
                    M.dma(bv, M.d["rpb"][i, bs], S["bsem"][bs], [*tbw[bs], first])
                    bt[bs] = (S["bsem"][bs], 16 * (i + 1))
                banks = []
                for j in range(2):
                    r = slice(64 * j, 64 * j + 64)
                    b, fr = M.bank()
                    banks.append((b, pe.mm([(ps[:, b, k0:512], q[r, hp, qs], k[r, hp, ks], True, True)], *fr, *w)))
                for j in range(2):
                    b, t = banks[j]
                    hd = 2 * hp + j
                    s = hd % 4
                    Pv = P4[:, s, :]
                    if lat:
                        t1 = dv.tt(Pv[:, LAT], ps[:, b, LAT], bv[:, hd % 8, :], ALU.add, t, bt[bs], *tpf[s])
                        t2 = ac.cp(Pv[:, CTX], ps[:, b, CTX], t1, *tpf[s])
                        M.give(b, t1, t2)
                        if hd % 8 == 7:
                            tbw[bs] = [t1]
                        pin, tw = Pv, [t1, t2]
                    else:
                        pin, tw = ps[:, b, CTX], [t]
                    m_ = mx[:, i, hd:hd + 1]
                    t1 = self_neg_max(dv, m_, pin, tw)
                    te = ac.act(Pv[:, k0:512], pin, ACT.Exp, t1, *tpf[s], bias=m_, acc=den[:, i, hd:hd + 1])
                    if not lat:
                        M.give(b, te)
                    got["e", i, hd] = te

            def turned(i, hp):
                k0 = 0 if i < 2 else 256
                for j in range(2):
                    hd = 2 * hp + j
                    s = hd % 4
                    b, fr = M.bank()
                    t = pe.tr([(ps[:, b, c:c + 128], P4[:, s, c:c + 128]) for c in range(k0, 512, 128)], ident,
                              got["e", i, hd], *fr)
                    tpf[s] = [t]
                    t = M.copy(PT4[:, s, k0:512], ps[:, b, k0:512], t, *ttf[s])
                    M.give(b, t)
                    got["p", i, hd] = t

            def mixed_values(i, hp):
                k0 = 0 if i < 2 else 256
                blocks = range(k0 // 128, 4)
                te = [got["e", i, 2 * hp + j] for j in range(2)]
                td = dv.recip(den[:, i, 2 * hp:2 * hp + 2], den[:, i, 2 * hp:2 * hp + 2], *te)
                b, fr = M.bank()
                parts = []
                for j in range(2):
                    hd = 2 * hp + j
                    parts += [(ps[:, b, 64 * j:64 * j + 64], PT4[:, hd % 4, kb * 128:kb * 128 + 128],
                               vt[:, kb, 64 * hd:64 * hd + 64], kb == blocks[0], kb == 3) for kb in blocks]
                t = pe.mm(parts, *[got["p", i, 2 * hp + j] for j in range(2)], *tvv, *fr)
                for j in range(2):
                    ttf[(2 * hp + j) % 4] = [t]
                t = dv.tt(ot[:, 128 * hp:128 * hp + 128].rearrange("p (a b) -> p a b", a=2),
                          ps[:, b, 0:128].rearrange("p (a b) -> p a b", a=2),
                          bc(den[:, i, 2 * hp:2 * hp + 2].unsqueeze(2), [128, 2, 64]), ALU.mult, t, td, *tof)
                M.give(b, t)
                if hp == 7:
                    for g in range(2):
                        b, fr = M.bank()
                        t1 = pe.tr([(ps[:, b, j * 128:j * 128 + 128], ot[:, 512 * g + j * 128:512 * g + j * 128 + 128])
                                    for j in range(4)], ident, t, *fr)
                        tof.append(t1)
                        M.give(b, M.split([v[:, 4 * g:4 * g + 4, 128 * i:128 * i + 128] for v in oF],
                                          ps[:, b, :].rearrange("p (a b) -> p a b", a=4), t1))

            first = pe.here()
            steps = [(i, hp) for i in range(4) for hp in range(8)]
            for n in range(len(steps) + 2):
                if n < len(steps):
                    scores(*steps[n])
                if 1 <= n <= len(steps):
                    turned(*steps[n - 1])
                if n >= 2:
                    mixed_values(*steps[n - 2])
            to = dv.here()
            M.barrier()
            M.lin("no", 0, range(8), oF, 512, onto_x(16, 512), to)
            n = 512
        else:
            q, vt = A(8, 256), A(4, 1024)
            B, K = A(8, 512), A(8, 512)
            St, AA = A(8, 128), A(8, 2, 256)
            masks = S["trig"][:, 0:480]
            lb, p0_, mm_ = A(32), A(16), A(16)
            Mu = masks[:, :].bitcast(mybir.dt.uint8).rearrange("p (a b) -> p a b", b=128)
            M.dma(tmp[:, 0:1920], M.d["imask"], S["isem"], M.extra)
            tmask = dv.cp(masks.bitcast(mybir.dt.uint8), tmp[:, 0:1920], (S["isem"], 16))
            hl = V["hl"]
            t = dv.tt(mm_, hl[:, 0:16], hl[:, 16:32], ALU.max, *tv)
            t = dv.tt(lb.rearrange("p (a b) -> p a b", a=2), hl.rearrange("p (a b) -> p a b", a=2),
                      bc(mm_.unsqueeze(1), [128, 2, 16]), ALU.subtract, t)
            t = ac.act(lb, lb, ACT.Exp, t)
            t = dv.tt(mm_, lb[:, 0:16], lb[:, 16:32], ALU.add, t)
            t = dv.recip(mm_, mm_, t)
            t = dv.tt(lb.rearrange("p (a b) -> p a b", a=2), lb.rearrange("p (a b) -> p a b", a=2),
                      bc(mm_.unsqueeze(1), [128, 2, 16]), ALU.mult, t)
            t = dv.tt(mm_, lb[:, 0:16], lb[:, 16:32], ALU.add, t)
            t = dv.tt(mm_, mm_, lb[:, 0:16], ALU.subtract, t)
            tlb = dv.ts(p0_, mm_, -1.0, 1.0, ALU.mult, ALU.add, t)
            LB, OM = mm_, p0_
            M.lin("hin", 0, range(8), h, 256, lambda i, m, p, t: [ac.act(q[:, i:i + m, :], p, ACT.Silu, t)], th)
            tqg = ac.here()
            M.lint("hin", 0, range(8, 16), h, 4, lambda m, c0, p, t: [M.copy(vt[:, m, c0:c0 + 128], p, t)], th)
            tvv = [ac.here(), dv.here()]
            ta0 = po.fill(AA, 0.0)
            o1 = ones[:, 0:1]
            for dr in range(2):
                E, Qt, Kt = (tmp[:, 2048 * i:2048 * i + 2048] for i in range(3))
                E3, Q3, K3 = (v.rearrange("p (a b) -> p a b", a=8) for v in (E, Qt, Kt))

                def ef(i, m, p, t, dr=dr):
                    t1 = ac.act(B[:, i:i + m, :], p, ACT.Sigmoid, t, tmask)
                    t2 = ac.act(K[:, i:i + m, :], p, ACT.Sigmoid, t, scale=-1.0)
                    for j in range(i, i + m):
                        d = 8 * dr + j
                        dv.ts(B[:, j, :], B[:, j, :], OM[:, d:d + 1], LB[:, d:d + 1], ALU.mult, ALU.add, t1, tlb)
                        dv.ts(K[:, j, :], K[:, j, :], OM[:, d:d + 1], None, ALU.mult, None, t2, tlb)
                    return [t2]
                M.lin("hin", 0, range(24 + 8 * dr, 32 + 8 * dr), h, 512, ef, th)
                t = dv.ts(B, B, 1e-19, None, ALU.max, None, dv.here())
                tk = t
                t = ac.act(B, B, ACT.Ln, t)
                rev = slice(None, None, -1)
                for j in range(8):
                    lat, ctx = B[:, j, LAT], B[:, j, CTX]
                    if dr:
                        lat = lat[:, ::-1]
                    else:
                        ctx = ctx[:, ::-1]
                    on = bc(o1, [128, 256])
                    dv.scan(lat, on, lat, t)
                    tsn = dv.scan(ctx, on, ctx, t)
                src, dst = (slice(257, 512), slice(256, 511)) if dr == 0 else (slice(256, 511), slice(257, 512))
                t = ac.act(E3[:, :, 0:255], B[:, :, src], ACT.Exp, tsn)
                tkd = dv.tt(K[:, :, dst], K[:, :, dst], E3[:, :, 0:255], ALU.mult, t, tk)
                kd = K3.rearrange("p a (b c) -> p a b c", b=2)
                for j in range(0, 8, 2):
                    b, fr = M.bank()
                    t = pe.tr([(ps[:, b, (2 * a + c) * 128:(2 * a + c) * 128 + 128],
                                K[:, j + a, 256 + 128 * c:384 + 128 * c]) for a in range(2) for c in range(2)], ident, tkd, *fr)
                    t = M.copy(Kt[:, 256 * j:256 * j + 512], ps[:, b, :], t)
                    M.give(b, t)
                    b, fr = M.bank()
                    t = pe.mm([(ps[:, b, 128 * a:128 * a + 128], kd[:, j + a, c, :],
                                vt[:, 2 + c, 128 * (j + a):128 * (j + a) + 128], c == 0, c == 1)
                               for a in range(2) for c in range(2)], t, *tvv, *fr)
                    tst = ac.cp(St[:, j:j + 2, :], ps[:, b, 0:256].rearrange("p (a b) -> p a b", a=2), t)
                    M.give(b, tst)
                tuse = [t]
                Bl, Kl = B[:, :, LAT], K[:, :, LAT]
                tA = [ta0]
                for j in range(0, 8, 2):
                    b, fr = M.bank()
                    t = pe.mm([(ps[:, b, (2 * a + c) * 128:(2 * a + c) * 128 + 128], K[:, j + a, 128 * c:128 * c + 128],
                                q[:, j + a, 128 * c:128 * c + 128], True, True) for a in range(2) for c in range(2)],
                              tk, tqg, *fr)
                    Pq = ps[:, b, :].rearrange("p (a c t) -> p a c t", a=2, c=2)
                    for c in range(2):
                        dst_ = AA[:, j:j + 2, c, 128 * c:128 * c + 128]
                        if dr == 0:
                            t1 = dv.pick(dst_, bc(Mu[:, 14:15, :], [128, 2, 128]), Pq[:, :, c, :], t, tmask, ta0)
                        else:
                            t2 = dv.tt(E3[:, j:j + 2, 128 * c:128 * c + 128], Pq[:, :, c, :], bc(ident.unsqueeze(1), [128, 2, 128]), ALU.mult, t, *tuse)
                            t1 = dv.tt(dst_, dst_, E3[:, j:j + 2, 128 * c:128 * c + 128], ALU.add, t2)
                    M.give(b, t1)
                tdd = t1
                for lv in range(8):
                    hf = 1 << lv
                    mid = hf - 1 if dr == 0 else hf
                    nb_ = 256 // (2 * hf)
                    b4 = Bl.rearrange("p a (n r) -> p a n r", r=2 * hf)
                    e4 = E3.rearrange("p a (n r) -> p a n r", r=2 * hf)
                    mb = bc(b4[:, :, :, mid:mid + 1], [128, 8, nb_, hf])
                    left, right = slice(0, hf), slice(hf, 2 * hf)
                    qside, kside = (right, left) if dr == 0 else (left, right)
                    dv.tt(e4[:, :, :, qside], b4[:, :, :, qside], mb, ALU.subtract, tsn, tdd, *tuse)
                    t = dv.tt(e4[:, :, :, kside], mb, b4[:, :, :, kside], ALU.subtract)
                    t = ac.act(E, E, ACT.Exp, t)
                    tq_ = po.tt(Q3, q, E3, ALU.mult, t, tqg, *tuse)
                    tk_ = dv.tt(K3, Kl, E3, ALU.mult, t, tk, *tuse)
                    tdd = tq_
                    tuse = []
                    if lv < 7:
                        mk = bc(Mu[:, 7 * dr + lv:7 * dr + lv + 1, :], [128, 2, 128])
                        for j in range(0, 8, 2):
                            b, fr = M.bank()
                            t = pe.mm([(ps[:, b, (2 * a + c) * 128:(2 * a + c) * 128 + 128], K3[:, j + a, 128 * c:128 * c + 128],
                                        Q3[:, j + a, 128 * c:128 * c + 128], True, True) for a in range(2) for c in range(2)],
                                      tq_, tk_, *fr)
                            Pq = ps[:, b, :].rearrange("p (a c t) -> p a c t", a=2, c=2)
                            for c in range(2):
                                t1 = dv.pick(AA[:, j:j + 2, c, 128 * c:128 * c + 128], mk, Pq[:, :, c, :], t, tmask, ta0)
                            M.give(b, t1)
                    else:
                        sb_, tb_ = (0, 1) if dr == 0 else (1, 0)
                        for j in range(0, 8, 4):
                            b, fr = M.bank()
                            t = pe.mm([(ps[:, b, a * 128:a * 128 + 128], K3[:, j + a, 128 * sb_:128 * sb_ + 128],
                                        Q3[:, j + a, 128 * tb_:128 * tb_ + 128], True, True) for a in range(4)], tq_, tk_, *fr)
                            t1 = dv.cp(AA[:, j:j + 4, sb_, 128 * tb_:128 * tb_ + 128],
                                       ps[:, b, :].rearrange("p (a t) -> p a t", a=4), t, ta0)
                            M.give(b, t1)
                    tuse = [t, tdd]
                t = ac.act(E3, Bl, ACT.Exp, tsn, *tuse, tk_)
                tq_ = dv.tt(Q3, q, E3, ALU.mult, t)
                O = x[:, :, CTX]
                for j in range(0, 8, 2):
                    b, fr = M.bank()
                    parts = []
                    for a in range(2):
                        oo = ps[:, b, 256 * a:256 * a + 256]
                        parts.append((oo, St[:, j + a, :], Q3[:, j + a, :], True, dr == 0))
                        if dr:
                            parts += [(oo, vt[:, c, 128 * (j + a):128 * (j + a) + 128], AA[:, j + a, c, :], False, c == 1)
                                      for c in range(2)]
                    t = pe.mm(parts, tq_, tst, *([t1] if dr else []), *fr)
                    P = ps[:, b, :].rearrange("p (a b) -> p a b", a=2)
                    if dr == 0:
                        to = dv.cp(O[:, j:j + 2, :], P, t)
                    else:
                        to = dv.tt(O[:, j:j + 2, :], O[:, j:j + 2, :], P, ALU.add, t)
                    M.give(b, to)
                M.barrier()
            g_ = B.rearrange("p a b -> p (a b)")[:, 0:2048].rearrange("p (a b) -> p a b", a=8)
            M.lin("hin", 0, range(16, 24), h, 256, lambda i, m, p, t: [ac.act(g_[:, i:i + m, :], p, ACT.Silu, t)], th)
            tqg = ac.here()
            t = M.stats(O, 8, 1, 256, 1 / 128, ones, S["rs8"](A, AA), sq, eps, to)
            t = dv.tt(O, O, S["rs8"](A, AA), ALU.mult, t)
            to = dv.stt(O, O, V["hn"], g_, ALU.mult, ALU.mult, t, tqg)
            M.barrier()
            os_ = [v[:, :, 0:256] for v in h]
            M.lin("ho", 0, range(8), os_, 256, onto_x(16, 256), M.split(os_, O, to))
            n = 256
        M.barrier()
        A.at = keep
        th = modulated(A2, 24, n, [dv.here()])
        M.barrier()
        A.at = early
        hid = A.pair(22, n)
        per = 512 // n
        tmp2 = [A(per, n) for _ in range(3 * (2 // per))]
        free = [[] for _ in tmp2]
        ta_ = [None] * len(tmp2)

        def up(i, m, p, t):
            c, r = i // 4, i % 4
            s = (c * (2 // per) + (r % 2) // per) % len(tmp2)
            f = tmp2[s]
            if r < 2:
                ta_[s] = ac.act(f, p, ACT.Silu, t, *free[s])
                return [ta_[s]]
            at = 2 * c + r % 2
            t1 = dv.tt(f, f, p, ALU.mult, t, ta_[s])
            free[s] = [M.split([v[:, at:at + m, :] for v in hid], f, t1)]
            return [t1]
        M.lin("fi", layer, range(44), h, n, up, th)
        M.lin("fo", layer, range(8), hid, n, onto_x(40, n), dv.here())
        tx = [dv.here()]
        A.at = base
        M.barrier()
    return tx[0]


def self_neg_max(dv, out, src, w):
    return dv(lambda e: e.tensor_reduce(out, src, AX.X, ALU.max, negate=True), w)


def program(nc, d, out, plan=None):
    with ExitStack() as ctx:
        M = Machine(nc, ctx, d, plan)
        x2 = M.sb("x2", [128, 8, 512])
        cst = M.sb("cst", [128, len(CONSTS), 128])
        o1, n1 = offsets(VEC1)
        o2, n2 = offsets(VEC2)
        v1 = M.sb("v1", [128, 2, n1])
        v2 = M.sb("v2", [128, 2, n2])
        posi = M.sb("posi", [128, T], I32)
        trig = M.sb("trig", [128, 2 * T])
        eps = M.sb("eps", [128, 1])
        cvec, silc = M.sb("cvec", [128, 8, 2]), M.sb("silc", [128, 8, 2])
        A = Arena(M)
        mods = M.sb("mods", [128, 2, 48, 2])
        sx, sv, s2 = M.sem("x"), M.sem("v"), M.sem("v2")
        for o, i in ((x2[:, :, 0:256], d["x"]), (x2[:, :, 256:512], d["ctx"]), (cst[:, :, :], d["cst"]),
                     (posi[:, :], d["pos"]), (cvec[:, :, :], d["c"]), (v1[:, :, :], d["v1"]), (v2[:, :, :], d["v2"])):
            M.dma(o, i, sx)
        te = M.po.fill(eps[:, :], EPS)
        tx = [(sx, 16 * 7), te]
        C = {k: cst[:, i, :] for i, k in enumerate(CONSTS)}
        vec = lambda v, o, l: {k: v[:, l, a:b] for k, (a, b) in o.items()}
        S = {"c": C, "x": x2[:, :, 0:256], "x2": x2[:, :, :], "eps": eps[:, :], "tx": tx, "pos": posi[:, :],
             "cos": trig[:, 0:T], "sin": trig[:, T:2 * T], "trig": trig[:, :], "vec1": (vec(v1, o1, 0), tx), "vec1b": (vec(v1, o1, 1), tx),
             "vec2": [(vec(v2, o2, l), tx) for l in range(2)], "cvec": cvec[:, :, :], "silc": silc[:, :, :], "mods": [mods[:, l, :, :] for l in range(2)],
             "bsem": [M.sem("b0"), M.sem("b1")], "isem": M.sem("im"),
             
             "rs8": lambda A, AA: AA.rearrange("p a b c -> p (a b c)")[:, 0:2048].rearrange("p (a b) -> p a b", a=8)}
        so = M.sem("out")
        modulation(M, S)
        t = first_block(M, A, S)
        if STAGE == 2:
            t = second_block(M, A, S, t)
        if plan is None:
            return M.asked
        M.dma(out, x2[:, :, 0:256], so, [t])
        M.sp.items.append((lambda e: e.wait_ge(so, 16), [], False))
        block = ctx.enter_context(nc.Block())

        @block.sync
        def _(e):
            M.sp.play(e)

        @block.tensor
        def _(e):
            M.pe.play(e)

        @block.vector
        def _(e):
            M.dv.play(e)

        @block.scalar
        def _(e):
            M.ac.play(e)

        @block.gpsimd
        def _(e):
            M.po.play(e)
        return A.top


STAGE = 2
ARENA = 34688


def constants():
    i, j = np.meshgrid(np.arange(128), np.arange(128), indexing="ij")
    f = lambda m: m.astype(np.float32)
    same = i // 64 == j // 64
    lev = lambda h: (i // (2 * h) == j // (2 * h)) & (i % (2 * h) < h) & (j % (2 * h) >= h)
    m = {"ident": f(i == j), "ones": f(i == i), "tri": f(i <= j), "bd64": f(same), "btri": f(same & (i <= j)),
         "bstrict": f(same & (i < j)), "cone0": f(i < 64), "cone1": f(i >= 64), "m0": f(lev(1)).T,
         "causal": np.where(j > i, np.float32(NEG), np.float32(0)).astype(np.float32)}
    for n in range(6):
        m[f"t{n}"] = f(lev(1 << n))
    cst = np.stack([m[k] for k in CONSTS], 1)
    ints = [lev(1 << n) for n in range(7)] + [lev(1 << n).T for n in range(7)] + [i == j]
    return np.ascontiguousarray(cst), np.ascontiguousarray(np.stack(ints, 1).astype(np.float32).reshape(128, 1920))


def tiled(name, w):
    k, n, c, parts = MATS[name]
    w = np.asarray(w).reshape(-1, k // 128, 128, n // c, c).transpose(0, 3, 2, 1, 4)
    most = -(-(k // 128) // parts)
    w = np.pad(w, ((0, 0), (0, 0), (0, 0), (0, most * parts - k // 128), (0, 0)))
    w = w.reshape(w.shape[0], n // c, 128, parts, most * c).transpose(0, 1, 3, 2, 4).reshape(w.shape[0], -1, 128, most * c)
    if w.shape[1] > 1:
        w = w.reshape(w.shape[0], -1, 2, 128, most * c).transpose(0, 1, 3, 2, 4)
    return np.ascontiguousarray(w).reshape(w.shape[0], w.shape[1], 128, -1)


def cols(v):
    v = np.asarray(v)
    return v.reshape(*v.shape[:-1], -1, 128).swapaxes(-1, -2)


def layout(a):
    d = {}
    win = a["w_in"]
    z, xbc, dt, cq, ckv, kr, qkv, gz, gb, ga, gate = np.split(
        win, np.cumsum([1024, 1536, 16, 512, 256, 64, 2048, 1024, 8, 8]).tolist(), axis=-1)
    r1, r2 = np.tile(kr[..., 0:32], (1, 1, 4)), np.tile(kr[..., 32:64], (1, 1, 4))
    d["win"] = tiled("win", np.concatenate([qkv, xbc, cq, ckv, r1, r2, z, gz, gate], -1))
    d["wsm"] = tiled("wsm", np.concatenate([dt, ga, gb], -1))
    uq = a["mla_w_uq"].reshape(2, 512, 8, 192)
    d["wuq"] = tiled("wuq", np.concatenate([uq[..., 0:128].reshape(2, 512, 1024), uq[..., 128:160].reshape(2, 512, 256),
                                            uq[..., 160:192].reshape(2, 512, 256)], -1))
    ukv = a["mla_w_ukv"].reshape(2, 256, 8, 256)
    d["wuk"] = tiled("wuk", ukv[..., 0:128].reshape(2, 256, 1024))
    d["wuv"] = tiled("wuv", ukv[..., 128:256].reshape(2, 256, 1024))
    for k, n in (("wso", "w_ssd_out"), ("wmo", "w_mla_out"), ("wgo", "w_gdn_out"), ("wo", "w_out"), ("wup", "w_up"),
                 ("wdn", "w_down"), ("ada", "ada_w_2"), ("nqkv", "na_w_qkv_2"), ("no", "na_w_o_2"), ("hin", "hg_w_in_2"),
                 ("ho", "hg_w_o_2"), ("fo", "ffn_w_out_2")):
        d[k] = tiled(k, a[n])
    fi = a["ffn_w_in_2"].reshape(2, 1024, 2, 11, 256)
    d["fi"] = tiled("fi", fi.transpose(0, 1, 3, 2, 4).reshape(2, 1024, 5632))
    d["x"] = np.ascontiguousarray(a["x"][0].T.reshape(8, 128, 256).transpose(1, 0, 2))
    d["ctx"] = np.ascontiguousarray(a["ctx_2"][0].T.reshape(8, 128, 256).transpose(1, 0, 2))
    d["pos"] = np.ascontiguousarray(np.broadcast_to(a["positions"], (128, 256)))
    d["c"] = np.ascontiguousarray(np.stack([cols(a["c_2"][0]), cols(a["c_ctx_2"])], -1))
    rows = lambda v: np.broadcast_to(v[:, None, :], (2, 128, v.shape[-1]))
    taps = lambda w: w.reshape(2, 4, -1, 128).transpose(0, 3, 2, 1).reshape(2, 128, -1)
    inv = (10000.0 ** (-np.arange(0, 64, 2, dtype=np.float32) / np.float32(64))).astype(np.float32)
    fn = np.broadcast_to(cols(a["final_norm_g"])[None], (2, 128, 8))
    v1 = {"n1": cols(a["norm1_g"]), "n2": cols(a["norm2_g"]), "cw": taps(a["ssd_conv_w"]), "cb": cols(a["ssd_conv_b"]),
          "gw": taps(a["gdn_conv_w"]), "qn": cols(a["mla_q_norm_g"]), "kn": cols(a["mla_kv_norm_g"]),
          "sn": cols(a["ssd_norm_g"]), "gn": cols(a["gdn_norm_g"]), "sd": cols(np.repeat(a["ssd_d"], 64, -1)),
          "bias": rows(np.concatenate([a["ssd_dt_bias"], a["gdn_dt_bias"]], -1)),
          "alog": rows(np.concatenate([a["ssd_a_log"], a["gdn_a_log"]], -1)), "fn": fn,
          "inv": np.broadcast_to(np.tile(inv, 4)[None, :, None], (2, 128, 1))}
    d["v1"] = np.ascontiguousarray(np.concatenate([v1[k] for k in VEC1], -1).transpose(1, 0, 2))
    two = lambda g: np.broadcast_to(np.tile(g[0], 2)[None, :, None], (2, 128, 1))
    hl = a["hg_lower_2"].reshape(32, 128).T[None]
    v2 = {"adab": cols(a["ada_b_2"]), "n1": cols(a["norm1_g_2"]), "n2": cols(a["norm2_g_2"]),
          "qg": two(a["na_q_gain_2"]), "kg": two(a["na_k_gain_2"]), "hl": np.broadcast_to(hl, (2, 128, 32)),
          "hn": np.broadcast_to(a["hg_norm_g_2"].reshape(1, 128, 1), (2, 128, 1))}
    d["v2"] = np.ascontiguousarray(np.concatenate([v2[k] for k in VEC2], -1).transpose(1, 0, 2))
    rpb = np.pad(a["na_rpb_2"][0], ((0, 0), (0, 0), (0, 1)), constant_values=NEG)
    qi = np.arange(256)
    r, c = qi // 64, qi % 64
    lo = np.clip(c - 8, 0, 48)[:, None]
    inside = (c[None, :] >= lo) & (c[None, :] < lo + 16)
    ri = r[None, :] - r[:, None] + 7
    ci = np.where(inside, np.clip(c[None, :] - c[:, None] + 15, 0, 30), 31)
    tab = rpb[:, ri, ci]
    d["rpb"] = np.ascontiguousarray(tab.reshape(2, 8, 2, 128, 256).transpose(2, 0, 3, 1, 4))
    d["cst"], d["imask"] = constants()
    return d


def kernel(**inputs):
    import numpy as _np
    import concourse.bacc as _bacc
    from concourse import mybir as _mybir
    from concourse.bass_utils import run_bass_kernel_spmd as _run

    d = layout({k: _np.asarray(v) for k, v in inputs.items()})
    nc = _bacc.Bacc("TRN2", target_bir_lowering=False, num_devices=1)
    arrays, aps = {}, {}
    for name, v in d.items():
        arrays[f"in_{name}"] = v
        aps[name] = nc.dram_tensor(f"in_{name}", v.shape, _mybir.dt.from_np(v.dtype), kind="ExternalInput").ap()
    out = nc.dram_tensor("out_0", (128, 8, 256), F32, kind="ExternalOutput").ap()
    order = program(_bacc.Bacc("TRN2", target_bir_lowering=False, num_devices=1), aps, out)
    program(nc, aps, out, order)
    r = _run(nc, [arrays], core_ids=[0])
    y = r.results[0]["out_0"]
    return _np.ascontiguousarray(y.transpose(1, 0, 2).reshape(1024, 256).T)[None]
```

```python
import numpy as np
import concourse.bass as bass
from concourse import mybir
from contextlib import ExitStack

F32 = mybir.dt.float32
F32R = mybir.dt.float32r
AHEAD = 2
POOL_EVERY = 3
I32 = mybir.dt.int32
ALU = mybir.AluOpType
ACT = mybir.ActivationFunctionType
AX = mybir.AxisListType

EPS = 1e-6
T = 256
NEG = -1e30
RAW = 3
HI = 4
SLOT = 1024
MAGIC = 12582912.0
TWO_PI_1 = 6.28125
TWO_PI_2 = 0.0019350051879882812
TWO_PI_3 = 3.019916050356e-07

MATS = {
    "win": (1024, 9728, 128, 1), "wsm": (1024, 32, 32, 1), "wuq": (512, 1536, 256, 1), "wuk": (256, 1024, 512, 1),
    "wuv": (256, 1024, 512, 1), "wso": (1024, 1024, 128, 1), "wmo": (1024, 1024, 128, 1), "wgo": (1024, 1024, 128, 1),
    "wo": (1024, 1024, 128, 1), "wup": (1024, 4096, 128, 1), "wdn": (4096, 1024, 128, 4),
    "ada": (1024, 6144, 128, 1), "nqkv": (1024, 3072, 128, 1), "no": (1024, 1024, 128, 1),
    "hin": (1024, 5120, 128, 1), "ho": (1024, 1024, 128, 1), "fi": (1024, 5632, 128, 1), "fo": (2816, 1024, 128, 3),
}


def spans(name):
    k, _, _, parts = MATS[name]
    kt = k // 128
    most = -(-kt // parts)
    return [(r * most, min(kt, (r + 1) * most)) for r in range(parts)]

CONSTS = ["ident", "ones", "tri", "bd64", "btri", "bstrict", "cone0", "cone1", "m0", "causal",
          "t0", "t1", "t2", "t3", "t4", "t5"]
VEC1 = {"n1": 8, "n2": 8, "cw": 48, "cb": 12, "gw": 64, "qn": 4, "kn": 2, "sn": 8, "gn": 1, "sd": 8,
        "bias": 24, "alog": 24, "fn": 8, "inv": 1}
VEC2 = {"adab": 48, "n1": 8, "n2": 8, "qg": 1, "kg": 1, "hl": 32, "hn": 1}


def offsets(table):
    out, at = {}, 0
    for k, n in table.items():
        out[k] = (at, at + n)
        at += n
    return out, at


class Queue:

    def __init__(self, sem):
        self.sem, self.items, self.n, self.held = sem, [], 0, []

    def __call__(self, fn, waits, signal=True):
        waits = [*self.held, *waits]
        self.held = []
        self.items.append((fn, waits, signal))
        if signal:
            self.n += 1
        return (self.sem, self.n)

    def here(self):
        return (self.sem, self.n)

    def play(self, eng):
        seen = {}
        for fn, waits, signal in self.items:
            for sem, value in waits:
                if value > seen.get(sem.num, 0):
                    eng.wait_ge(sem, value)
                    seen[sem.num] = value
            i = fn(eng)
            if signal:
                i.then_inc(self.sem, 1)


class Elementwise(Queue):
    def tt(self, out, a, b, op, *w):
        return self(lambda e: e.tensor_tensor(out, a, b, op), w)

    def ts(self, out, a, s1, s2, op0, op1, *w):
        if op1 is None:
            return self(lambda e: e.tensor_scalar(out, a, s1, None, op0), w)
        return self(lambda e: e.tensor_scalar(out, a, s1, s2, op0, op1), w)

    def stt(self, out, a, s, b, op0, op1, *w):
        return self(lambda e: e.scalar_tensor_tensor(out=out, in0=a, scalar=s, in1=b, op0=op0, op1=op1), w)

    def cp(self, out, a, *w):
        return self(lambda e: e.tensor_copy(out, a), w)

    def red(self, out, a, op, *w):
        return self(lambda e: e.tensor_reduce(out, a, AX.X, op), w)

    def recip(self, out, a, *w):
        return self(lambda e: e.reciprocal(out, a), w)

    def fill(self, out, v, *w):
        return self(lambda e: e.memset(out, v), w)

    def scan(self, out, a, b, *w):
        return self(lambda e: e.tensor_tensor_scan(out, a, b, 0.0, ALU.mult, ALU.add), w)

    def pick(self, out, mask, data, *w):
        return self(lambda e: e.copy_predicated(out, mask, data), w)


class Scalar(Queue):
    def act(self, out, a, func, *w, bias=None, scale=1.0, acc=None):
        def fn(e):
            kw = {}
            if bias is not None:
                kw["bias"] = bias
            if acc is not None:
                kw["accum_out"] = acc
            return e.activation(out, a, func, scale=scale, **kw)
        return self(fn, w)

    def cp(self, out, a, *w):
        return self(lambda e: e.activation(out, a, ACT.Copy), w)


class Tensor(Queue):
    def mm(self, parts, *w):
        for i, (out, l, r, start, stop) in enumerate(parts):
            t = self(lambda e, o=out, l=l, r=r, s=start, p=stop: e.matmul(o, l, r, start=s, stop=p),
                     w if i == 0 else (), signal=i == len(parts) - 1)
        return t

    def tr(self, parts, ident, *w):
        for i, (out, a) in enumerate(parts):
            t = self(lambda e, o=out, a=a: e.transpose(o, a, ident), w if i == 0 else (),
                     signal=i == len(parts) - 1)
        return t


class Machine:
    def __init__(self, nc, ctx, d, plan):
        self.nc, self.ctx, self.d = nc, ctx, d
        self.plan_known = plan is not None
        self.pe, self.dv, self.ac, self.po = (
            c(self.sem(n)) for c, n in ((Tensor, "pe"), (Elementwise, "dv"), (Scalar, "ac"), (Elementwise, "po")))
        self.sp = Queue(self.sem("sp"))
        self.ps = self.pb("ps", [128, 8, 512])
        self.bfree = [[] for _ in range(8)]
        self.bheld = [False] * 8
        self.bi = 0
        base = (nc.sbuf_base + 31) // 32 * 32
        self.slab = self.sb("slab", [128, ARENA])
        self.ring = self.sb("ring", [128, (2 * RAW + HI) * SLOT])
        self.home = base
        self.names = 0
        self.raw = [self.ring[:, i * SLOT:(i + 1) * SLOT] for i in range(2 * RAW)]
        self.raw2 = [self.ring[:, 2 * i * SLOT:2 * (i + 1) * SLOT].rearrange("p (c k n) -> p k c n", c=2, k=8) for i in range(RAW)]
        at = ARENA
        at += 2 * RAW * SLOT
        self.lows2 = [self.rounded(ARENA + 2 * i * SLOT, 2 * SLOT) for i in range(RAW)]
        self.highs2 = [self.rounded(at + 2 * i * SLOT, 2 * SLOT) for i in range(HI // 2)]
        half = lambda v: [a[:, i * SLOT:(i + 1) * SLOT] for a in v for i in range(2)]
        self.low, self.high = half(self.lows2), half(self.highs2)
        self.rsem = [self.sem(f"raw{i}") for i in range(RAW)]
        self.rfree = [[] for _ in range(RAW)]
        self.hfree = [[] for _ in range(HI)]
        self.units = 0
        self.highs = 0
        self.plan, self.starts, self.unit_of = [], [], []
        for chunk in plan or []:
            self.planned(chunk)
        self.asked = []
        self.ready = []
        self.flip = 0
        self.extra = []

    def sem(self, n):
        return self.ctx.enter_context(self.nc.semaphore("s_" + n))

    def sb(self, n, shape, dt=F32):
        return self.ctx.enter_context(self.nc.sbuf_tensor(n, shape, dt))

    def pb(self, n, shape):
        return self.ctx.enter_context(self.nc.psum_tensor(n, shape, F32))

    def rounded(self, at, n):
        self.names += 1
        t = self.nc.alloc_sbuf_tensor_at(f"r{self.names}", [128, n], F32R, offset=self.home + 4 * at)
        return t[:, 0:n]

    def bank(self):
        b = self.bi
        while self.bheld[b]:
            b = (b + 1) % 8
        self.bi = (b + 1) % 8
        assert not self.bheld[b]
        self.bheld[b] = True
        return b, self.bfree[b]

    def give(self, b, *tokens):
        self.bfree[b] = list(tokens)
        self.bheld[b] = False

    def barrier(self):
        now = [q.here() for q in (self.pe, self.dv, self.ac, self.po)]
        for q in (self.pe, self.dv, self.ac, self.po):
            q.held = list(now)
        self.extra = list(now)

    def dma(self, out, src, sem, waits=()):
        self.sp.items.append((lambda e: e.dma_start(out, src).then_inc(sem, 16), list(waits), False))

    def planned(self, chunk):
        if chunk[2] % 2 == 0:
            self.starts.append(len(self.plan))
        else:
            assert self.plan[-1] == (*chunk[:2], chunk[2] - 1)
        self.unit_of.append(len(self.starts) - 1)
        self.plan.append(chunk)

    def fetch(self):
        name, layer, c = self.plan[self.starts[self.units]]
        s = self.units % RAW
        src = self.d[name][layer, c // 2]
        at = 2 * s * SLOT
        self.dma(self.ring[:, at:at + src.shape[1]], src, self.rsem[s], self.rfree[s])
        self.units += 1

    def prepare(self):
        p = len(self.ready)
        name, layer, c = self.plan[p]
        while self.units <= self.unit_of[p]:
            self.fetch()
        cols = MATS[name][2]
        parts = spans(name)
        lo_, hi_ = parts[c % len(parts)]
        n = (hi_ - lo_) * cols
        u = self.unit_of[p]
        s, got = u % RAW, (self.rsem[u % RAW], 16 * (u // RAW + 1))
        i = 2 * s + c % 2
        raw = self.raw[i][:, 0:n]
        kn = lambda v: v.rearrange("p (k n) -> p k n", n=cols)
        if name == "ada":
            self.ready.append((kn(raw), got, s, None))
            return
        h = 2 * (u % 2) + c % 2
        self.highs += 1
        hi, lo = self.high[h][:, 0:n], self.low[i][:, 0:n]
        t = self.ac.cp(hi, raw, got, *self.hfree[h])
        q = self.po if self.highs % POOL_EVERY == 0 else self.dv
        t = q.tt(lo, raw, hi.bitcast(F32), ALU.subtract, t, got)
        self.ready.append(((kn(hi), kn(lo)), t, s, h))

    def weight(self, name, layer, c):
        i = len(self.asked)
        self.asked.append((name, layer, c))
        if not self.plan_known:
            self.planned((name, layer, c))
        while c % 2 == 0 and self.units < min(self.unit_of[i] + RAW, len(self.starts)):
            self.fetch()
        while len(self.ready) < min(i + 1 + AHEAD, len(self.plan)):
            self.prepare()
        return self.ready[i]

    def done(self, w, token):
        self.rfree[w[2]] = [token]
        if w[3] is not None:
            self.hfree[w[3]] = [token]

    def splits(self, dst, src, ws):
        out = []
        for i in range(0, src.shape[1], 2):
            t = self.split([v[:, i:i + 2, 0:src.shape[2]] for v in dst], src[:, i:i + 2, :], *ws)
            out += [t, t]
        return out

    def scaled(self, src, dst, n, gain, shift, rs, sq, *w):
        out = []
        for i in range(src.shape[1]):
            for c in range(0, n, 256):
                cs = slice(c, c + 256)
                f, hi, lo = sq[:, i, cs], dst[0][:, i, cs], dst[1][:, i, cs]
                t = self.dv.stt(f, src[:, i, cs], gain(i, c // 256), rs[:, 0, cs], ALU.mult, ALU.mult, *w)
                if shift is None:
                    t = self.split((hi, lo), f, t)
                else:
                    t = self.ac.act(hi, f, ACT.Identity, t, bias=shift(i, c // 256))
                    t = self.dv.stt(lo, f, shift(i, c // 256), hi.bitcast(F32), ALU.add, ALU.subtract, t)
            out.append(t)
        return out

    def split(self, dst, src, *w):
        hi, lo = dst
        t = self.ac.cp(hi, src, *w)
        return self.dv.tt(lo, src, hi.bitcast(F32), ALU.subtract, t, *w)

    def lin(self, *args):
        for _ in self.lins(*args):
            pass

    def lins(self, name, layer, chunks, x, n, evac, w):
        cols = MATS[name][2]
        rows = spans(name)
        per = 512 // n
        tiles = [(c, j) for c in chunks for j in range(cols // 128)]
        wt = None
        for g in range(0, len(tiles), per):
            group = tiles[g:g + per]
            b, fr = self.bank()
            for jj, (c, j) in enumerate(group):
                o = self.ps[:, b, jj * n:(jj + 1) * n]
                cs = slice(j * 128, (j + 1) * 128)
                for r, (k0, k1) in enumerate(rows):
                    if j == 0:
                        wt = self.weight(name, layer, c * len(rows) + r)
                    (wh, wl), tok, _, _ = wt
                    parts = [(o, a[:, k - k0, cs], v[:, k, 0:n], k == 0 and i == 0,
                              k == rows[-1][1] - 1 and i == 2) for k in range(k0, k1)
                             for i, (a, v) in enumerate(((wh, x[0]), (wh, x[1]), (wl, x[0])))]
                    if g + jj == 0:
                        for k in range(k0, k1):
                            t = self.pe.mm(parts[3 * (k - k0):3 * (k - k0) + 3], tok, *fr, w[k])
                    else:
                        t = self.pe.mm(parts, tok, *fr)
                    if j == cols // 128 - 1:
                        self.done(wt, t)
            out = self.ps[:, b, 0:len(group) * n].rearrange("p (a n) -> p a n", n=n)
            self.give(b, *evac(g, len(group), out, t))
            if (tiles[g][0] * len(rows) // 2) != (((tiles[g + per][0]) * len(rows)) // 2 if g + per < len(tiles) else -1):
                yield

    def fill(self, *jobs):
        for job in jobs:
            next(job, None)

    def finish(self, job):
        for _ in job:
            pass

    def lint(self, name, layer, chunks, x, blocks, evac, *w):
        k_, _, cols, _ = MATS[name]
        kt = k_ // 128
        at = 0
        both = 2 if cols == 128 else 1
        for c in range(chunks[0], chunks[-1] + 1, both):
            ws = [self.weight(name, layer, c + i) for i in range(both)]
            toks = [v[1] for v in ws]
            (wh, wl), _, unit, h = ws[0]
            if both == 2:
                pair = lambda v: v.rearrange("p (c k n) -> p k c n", c=2, k=kt)
                wh, wl = pair(self.highs2[h // 2]), pair(self.lows2[unit])
            for m in range(blocks):
                for c0 in range(0, both * cols, 512):
                    n = min(512, both * cols - c0)
                    b, fr = self.bank()
                    parts = []
                    o = self.ps[:, b, 0:n]
                    for k in range(kt):
                        for i, (a, v) in enumerate(((x[0], wh), (x[0], wl), (x[1], wh))):
                            v = v[:, k, :, :] if both == 2 else v[:, k, c0:c0 + n]
                            parts.append((o, a[:, k, m * 128:m * 128 + 128], v, k == 0 and i == 0, k == kt - 1 and i == 2))
                    t = self.pe.mm(parts, *toks, *fr, *w)
                    self.give(b, *evac(m, at + c0, o, t))
            for v in ws:
                self.done(v, t)
            at += both * cols

    def copy(self, out, src, *w):
        self.flip ^= 1
        return self.ac.cp(out, src, *w) if self.flip else self.dv.cp(out, src, *w)

    def stats(self, src, nt, per, n, inv, lhs, rs, sq, eps, *w):
        t = self.ac.act(sq[:, 0:nt, 0:n], src, ACT.Square, *w)
        groups = nt // per
        pb = 512 // n
        for g in range(0, groups, pb):
            m = min(pb, groups - g)
            b, fr = self.bank()
            tm = self.pe.mm([(self.ps[:, b, j * n:(j + 1) * n], lhs, sq[:, (g + j) * per + k, 0:n], k == 0,
                              k == per - 1) for j in range(m) for k in range(per)], t, *fr)
            o = rs[:, g:g + m, 0:n]
            t1 = self.ac.act(o, self.ps[:, b, 0:m * n].rearrange("p (a n) -> p a n", a=m), ACT.Ln, tm,
                             bias=eps, scale=inv)
            self.give(b, t1)
        o = rs[:, 0:groups, 0:n]
        return self.ac.act(o, o, ACT.Exp, t1, scale=-0.5)


class Power:

    def __init__(self, m, ones, sq, n, nt):
        self.m, self.ones, self.sq, self.n, self.nt, self.left = m, ones, sq, n, nt, None
        self.b, self.free = m.bank()
        self.o = m.ps[:, self.b, 0:n]
        self.places, self.summed = sq.shape[1], []

    def add(self, i, src, *w):
        p = i % self.places
        t = self.m.ac.act(self.sq[:, p:p + 2, 0:self.n], src, ACT.Square, *w, *self.summed)
        if self.left is not None:
            self.summed = [self.sum()]
        self.left = (i, t)

    def sum(self):
        i, t = self.left
        return self.m.pe.mm([(self.o, self.ones, self.sq[:, i % self.places + k, 0:self.n], i + k == 0, i + k == self.nt - 1)
                             for k in range(2)], t, *self.free)

    def root(self, rs, inv, eps):
        t = self.m.ac.act(rs, self.o, ACT.Ln, self.sum(), bias=eps, scale=inv)
        self.m.give(self.b, t)
        return self.m.ac.act(rs, rs, ACT.Exp, t, scale=-0.5)


def bc(ap, shape):
    return ap.to_broadcast(shape)


class Arena:
    def __init__(self, m):
        self.m, self.t, self.at, self.top = m, m.slab, 0, 0

    def pair(self, kt, n):
        out = []
        for _ in range(2):
            ap = self(kt * n)
            out.append(self.m.rounded(self.at - kt * n, kt * n).rearrange("p (k n) -> p k n", k=kt))
        return out

    def __call__(self, *dims):
        n = int(np.prod(dims))
        ap = self.t[:, self.at:self.at + n]
        self.at += n
        assert self.at <= ARENA, self.at
        self.top = max(self.top, self.at)
        names = "abcd"[:len(dims)]
        if len(dims) == 1:
            return ap
        return ap.rearrange(f"p ({' '.join(names)}) -> p {' '.join(names)}", **{names[i]: dims[i] for i in range(len(dims))})


def modulation(M, S):
    t0 = M.ac.act(S["silc"], S["cvec"], ACT.Silu, *S["tx"])

    turned = [[], []]

    def turn(layer, g, t):
        b, fr = M.bank()
        row = S["row"][g % 2]
        t = M.pe.tr([(M.ps[:, b, 2 * j:2 * j + 2], row[:, 128 * j:128 * j + 128]) for j in range(2)], S["c"]["ident"][0:2, 0:2], t, *fr)
        turned[g % 2] = [t]
        t = M.dv.tt(S["mods"][layer][:, 2 * g:2 * g + 2, :], M.ps[:, b, 0:4].rearrange("p (a b) -> p a b", b=2),
                    bc(S["vec2"][layer][0]["adab"][:, 2 * g:2 * g + 2].unsqueeze(2), [128, 2, 2]), ALU.add, t, *S["tx"])
        M.give(b, t)

    def pieces(layer):
        before = None
        for g in range(24):
            ws = [M.weight("ada", layer, 2 * g + j) for j in range(2)]
            w = M.raw2[ws[0][2]]
            b, fr = M.bank()
            t = M.pe.mm([(M.ps[0:2, b, 0:256], S["silc"][:, k, :], w[:, k, :, :], k == 0, k == 7) for k in range(8)],
                        ws[0][1], t0, *fr)
            for v in ws:
                M.done(v, t)
            t = M.ac.cp(S["row"][g % 2], M.ps[0:2, b, 0:256], t, *turned[g % 2])
            M.give(b, t)
            if before is not None:
                turn(layer, g - 1, before)
            before = t
            yield
        turn(layer, 23, before)
        yield
    S["ada"] = [pieces(0), pieces(1)]


def first_block(M, A, S):
    pe, dv, ac, po, ps = M.pe, M.dv, M.ac, M.po, M.ps
    C, x = S["c"], S["x"]
    ident = C["ident"]
    ones = C["ones"]
    one = ones[:, 0:1]
    eps = S["eps"]
    tx = S["tx"]

    power = None
    for layer in range(2):
        V, tv = S["vec1"] if layer == 0 else S["vec1b"]
        base = A.at
        xn = A.pair(8, T)
        mixed, gate, y, sq = (A(8, T) for _ in range(4))
        rs = A(8, T)
        keep = A.at

        ada = S["ada"][0]

        def normed(src, dst, inv, gain, sq, rs, power, *w):
            if power is None:
                power = Power(M, ones, sq, T, src.shape[1])
                for i in range(0, src.shape[1], 2):
                    power.add(i, src[:, i:i + 2, :], *w)
            t = power.root(rs[:, 0, :], inv, eps)
            return M.scaled(src, dst, T, lambda i, c: gain[:, i:i + 1], None, rs, sq, t)

        txn = normed(x, xn, 1 / 1024, V["n1"], sq, rs, power, *tx, *tv)
        M.fill(ada, ada)

        if layer == 0:
            ang, kk, r, pos = (y[:, i, :] for i in range(4))
            v0, _ = S["vec1"]
            t = dv.cp(pos, S["pos"], *tx)
            t = dv.ts(ang, pos, v0["inv"], None, ALU.mult, None, t)
            tabs = []
            for tab, shift in ((S["cos"], 0.25), (S["sin"], 0.0)):
                t = dv.ts(kk, ang, 0.15915494309189535, shift, ALU.mult, ALU.add, t)
                t = dv.ts(kk, kk, MAGIC, None, ALU.add, None, t)
                t = dv.ts(kk, kk, MAGIC, None, ALU.subtract, None, t)
                t = dv.stt(r, kk, -TWO_PI_1, ang, ALU.mult, ALU.add, t)
                t = dv.stt(r, kk, -TWO_PI_2, r, ALU.mult, ALU.add, t)
                t = dv.stt(r, kk, -TWO_PI_3, r, ALU.mult, ALU.add, t)
                if shift:
                    t = dv.ts(r, r, 1.5707963267948966, None, ALU.add, None, t)
                t = dv.ts(r, r, 3.1415925, -3.1415925, ALU.min, ALU.max, t)
                t = ac.act(tab, r, ACT.Sin, t)
                tabs.append(t)

        def gates(chunk, dst, tokens):
            def eg(i, m, p, t):
                tokens[:] = [ac.act(dst[:, i:i + m, :], p, ACT.Sigmoid, t)]
                return tokens
            return M.lins("win", layer, range(4 * chunk, 4 * chunk + 8), xn, T, eg, txn)

        def silus(chunk, dst, tokens):
            def ez(i, m, p, t):
                tokens[:] = [ac.act(dst[:, i:i + m, :], p, ACT.Silu, t)]
                return tokens
            return M.lins("win", layer, range(chunk, chunk + 8), xn, T, ez, txn)

        def branch_out(yop, ty, wname, gate, tg, first, ms=None):
            ts = []

            def eo(i, m, p, t):
                if first:
                    return [dv.tt(mixed[:, i:i + m, :], p, gate[:, i:i + m, :], ALU.mult, t, *tg)]
                t1 = dv.tt(gate[:, i:i + m, :], p, gate[:, i:i + m, :], ALU.mult, t, *tg)
                t2 = dv.tt(mixed[:, i:i + m, :], mixed[:, i:i + m, :], gate[:, i:i + m, :], ALU.add, t1)
                if ms is not None:
                    t2 = M.split([v[:, i:i + m, :] for v in ms], mixed[:, i:i + m, :], t2)
                    ts.extend([t2] * m)
                return [t1]
            ys = A.pair(8, T)
            M.lin(wname, layer, range(8), ys, T, eo, M.splits(ys, yop, [ty]))
            return ts

        def conv(pad, dst, wname, tz, after):
            wv = V[wname]

            def ev(i0, m, p, t):
                tc = ac.cp(pad[:, i0:i0 + m, 3:3 + T], p, t)
                ts = [dv.ts(dst[:, i, :], pad[:, i, 0:T], wv[:, 4 * i:4 * i + 1], None, ALU.mult, None, tc, tz)
                      for i in range(i0, i0 + m)]
                for j in range(1, 4):
                    ts = [dv.stt(dst[:, i, :], pad[:, i, j:j + T], wv[:, 4 * i + j:4 * i + j + 1], dst[:, i, :],
                                 ALU.mult, ALU.add, ts[i - i0]) for i in range(i0, i0 + m)]
                after(i0, m, ts[-1])
                return [tc]
            return ev

        sm, sp, sa, sb_, sc = A(2, 32), A(2, 24), A(2, 24), A(2, 24), A(2, 24)
        smask = A(48)
        beta, dA, cum = A(2, 8), A(2, 24), A(2, 24)
        tot, etot = A(5, 16), A(5, 16)
        keep = A.at
        acc = A(16, T)
        z = A(8, T)
        top = A.at
        pad = A(16, T + 3)
        tz = po.fill(pad[:, :, 0:3], 0.0, txn[-1])
        tsl = []
        def silu(i, m, t):
            tsl[:] = [ac.act(acc[:, i:i + m, :], acc[:, i:i + m, :], ACT.Silu, t)]
        job = M.lins("win", layer, range(0, 16), xn, T, conv(pad, acc, "gw", tz, silu), txn)
        M.lint("wsm", layer, [0], xn, 2, lambda m, c0, p, t: [ac.cp(sm[:, m, :], p, t)], txn[-1])
        t = dv.tt(sp, sm[:, :, 0:24], bc(V["bias"].unsqueeze(1), [128, 2, 24]), ALU.add, ac.here())
        ta = ac.act(sa, sp, ACT.Abs, t)
        te = ac.act(sa, sa, ACT.Exp, ta, scale=-1.0)
        tl = ac.act(sb_, sa, ACT.Ln, te, bias=one)
        M.fill(job)
        t = dv.ts(sc, sa, 1 / 3, -0.5, ALU.mult, ALU.add, te)
        t = dv.tt(sc, sc, sa, ALU.mult, t)
        t = dv.stt(sc, sc, 1.0, sa, ALU.add, ALU.mult, t)
        tk = dv.ts(smask.rearrange("p (a b) -> p a b", a=2), sa, 0.01, None, ALU.is_lt, None, te)
        t = dv.pick(sb_.rearrange("p a b -> p (a b)"), smask.bitcast(I32), sc.rearrange("p a b -> p (a b)"), t, tk, tl)
        t = dv.stt(sp, sp, 0.0, sb_, ALU.max, ALU.add, t)
        ta = ac.act(sc[:, 0, :], V["alog"], ACT.Exp, t)
        t = dv.stt(dA, sp, -1.0, bc(sc[:, 0:1, :], [128, 2, 24]), ALU.mult, ALU.mult, t, ta)
        M.fill(job)
        tb = ac.act(beta, sm[:, :, 24:32], ACT.Sigmoid)
        b, fr = M.bank()
        P = ps[:, b, 0:48].rearrange("p (a b) -> p a b", a=2)
        Q = ps[:, b, 64:144].rearrange("p (a b) -> p a b", a=5)
        parts = []
        for c in range(2):
            parts += [(P[:, c, 0:16], C["tri"], dA[:, c, 0:16], True, True),
                      (P[:, c, 16:24], C["btri"], dA[:, c, 16:24], True, True),
                      (Q[:, 2 * c, 0:8], C["cone0"], dA[:, c, 16:24], True, True),
                      (Q[:, 2 * c + 1, 0:8], C["cone1"], dA[:, c, 16:24], True, True)]
        parts += [(Q[:, 4, 0:16], ones, dA[:, 0, 0:16], True, True)]
        tm = pe.mm(parts, t, *fr)
        t1 = ac.cp(cum, P, tm)
        t2 = ac.cp(tot[:, 0:4, 0:8], Q[:, 0:4, 0:8], tm)
        t3 = ac.cp(tot[:, 4, :], Q[:, 4, :], tm)
        t4 = ac.act(etot[:, 0:4, 0:8], Q[:, 0:4, 0:8], ACT.Exp, tm)
        M.give(b, t4)
        ts_ = [t4, tb, t]

        M.fill(*[job] * 2)
        tqk = list(tsl)
        M.fill(*[job] * 2)
        t = M.stats(acc[:, 0:8, :], 8, 1, T, 1.0, ones, rs, sq, eps, *tqk)
        tq = dv.stt(acc[:, 0:4, :], acc[:, 0:4, :], 128 ** -0.5, rs[:, 0:4, :], ALU.mult, ALU.mult, t)
        tk = dv.tt(acc[:, 4:8, :], acc[:, 4:8, :], rs[:, 4:8, :], ALU.mult, t)
        M.finish(job)
        A.at = top
        tsl, tzz = tsl[0], []
        zjob = silus(44, z, tzz)
        M.fill(zjob)
        qT, kT, vT = acc[:, 0:4, :], acc[:, 4:8, :], acc[:, 8:16, :]
        M.barrier()
        ktok, vtok = A(2, 4, 128), A(2, 8, 128)
        qkT, qg = A(16, 128), A(8, T)
        AT, X, XT = (A(16, 128) for _ in range(3))
        Y = mixed.rearrange("p a (b c) -> p (a b) c", c=128)
        BT = gate.rearrange("p a (b c) -> p (a b) c", c=128)
        u, wT = X, BT
        for c in range(2):
            cs = slice(c * 128, c * 128 + 128)
            b, fr = M.bank()
            t = pe.tr([(ps[:, b, h * 128:h * 128 + 128], kT[:, h, cs]) for h in range(4)], ident, tk, *fr)
            M.give(b, M.copy(ktok[:, c, :, :].rearrange("p a b -> p (a b)"), ps[:, b, :], t))
            for g in range(2):
                b, fr = M.bank()
                t = pe.tr([(ps[:, b, h * 128:h * 128 + 128], vT[:, 4 * g + h, cs]) for h in range(4)], ident, tsl, *fr)
                M.give(b, dv.tt(vtok[:, c, 4 * g:4 * g + 4, :], ps[:, b, :].rearrange("p (a b) -> p a b", a=4),
                                bc(beta[:, c, 4 * g:4 * g + 4].unsqueeze(2), [128, 4, 128]), ALU.mult, t, tb))
        tat = {}
        for c in range(2):
            cs = slice(c * 128, c * 128 + 128)
            for g in range(2):
                p0 = c * 8 + 4 * g
                b, fr = M.bank()
                t = pe.mm([(ps[:, b, j * 128:j * 128 + 128], bc(dA[:, c, 16 + 4 * g + j:17 + 4 * g + j], [128, 128]),
                            C["btri"], True, True) for j in range(4)], *ts_, *fr)
                P = ps[:, b, :].rearrange("p (a b) -> p a b", a=4)
                D = Y[:, p0:p0 + 4, :]
                te = ac.act(qg[:, 4 * g:4 * g + 4, cs], P, ACT.Exp, t)
                t1 = dv.tt(D, P, bc(cum[:, c, 16 + 4 * g:20 + 4 * g].unsqueeze(2), [128, 4, 128]), ALU.subtract, t, te)
                M.give(b, te, t1)
                t1 = dv.ts(D, D, 0.0, None, ALU.min, None, t1)
                td = ac.act(D, D, ACT.Exp, t1)
                qv = qT[:, 2 * g:2 * g + 2, cs].unsqueeze(2)
                t1 = dv.tt(qg[:, 4 * g:4 * g + 4, cs].rearrange("p (a r) t -> p a r t", r=2),
                           qg[:, 4 * g:4 * g + 4, cs].rearrange("p (a r) t -> p a r t", r=2),
                           bc(qv, [128, 2, 2, 128]), ALU.mult, te)
                b, fr = M.bank()
                parts = []
                for j in range(2):
                    h = 2 * g + j
                    parts += [(ps[:, b, j * 256:j * 256 + 128], kT[:, h, cs], kT[:, h, cs], True, True),
                              (ps[:, b, j * 256 + 128:j * 256 + 256], kT[:, h, cs], qT[:, h, cs], True, True)]
                t = pe.mm(parts, tq, tk, *fr)
                P = ps[:, b, :].rearrange("p (j w t) -> p j w t", j=2, w=2)
                D4 = D.rearrange("p (a r) t -> p a r t", r=2)
                t1 = dv.tt(AT[:, p0:p0 + 4, :].rearrange("p (a r) t -> p a r t", r=2), D4,
                           bc(P[:, :, 0:1, :], [128, 2, 2, 128]), ALU.mult, td, t)
                t2 = dv.tt(qkT[:, p0:p0 + 4, :].rearrange("p (a r) t -> p a r t", r=2), D4,
                           bc(P[:, :, 1:2, :], [128, 2, 2, 128]), ALU.mult, td, t)
                M.give(b, t1, t2)
                t2 = po.tt(qkT[:, p0:p0 + 4, :], qkT[:, p0:p0 + 4, :], bc(C["btri"].unsqueeze(1), [128, 4, 128]), ALU.mult, t2)
                t1 = dv.tt(AT[:, p0:p0 + 4, :], AT[:, p0:p0 + 4, :], bc(C["bstrict"].unsqueeze(1), [128, 4, 128]), ALU.mult, t1)
                tat[c, g] = t1
                if c + g < 2:
                    M.fill(zjob)
        order = [(c, g) for c in range(2) for g in range(2)]
        tab = {}
        for c, g in order:
            if True:
                p0 = c * 8 + 4 * g
                t1 = tat[c, g]
                b, fr = M.bank()
                t = pe.tr([(ps[:, b, j * 128:j * 128 + 128], AT[:, p0 + j, :]) for j in range(4)], ident, t1, *fr)
                A4 = BT[:, p0:p0 + 4, :]
                t = dv.tt(A4, ps[:, b, :].rearrange("p (a b) -> p a b", a=4),
                          bc(beta[:, c, 4 * g:4 * g + 4].unsqueeze(2), [128, 4, 128]), ALU.mult, t, tb)
                M.give(b, t)
                tab[c, g] = t
        for c, g in order:
            if True:
                p0 = c * 8 + 4 * g
                t = tab[c, g]
                A4 = BT[:, p0:p0 + 4, :]
                b, fr = M.bank()
                t1 = pe.tr([(ps[:, b, j * 128:j * 128 + 128], A4[:, j, :]) for j in range(4)], ident, t, *fr)
                t1 = ac.cp(AT[:, p0:p0 + 4, :], ps[:, b, :].rearrange("p (a b) -> p a b", a=4), t1)
                M.give(b, t1)
                idb = bc(ident.unsqueeze(1), [128, 4, 128])
                t = po.tt(X[:, p0:p0 + 4, :], A4, bc(C["m0"].unsqueeze(1), [128, 4, 128]), ALU.mult, t)
                t = po.tt(X[:, p0:p0 + 4, :], idb, X[:, p0:p0 + 4, :], ALU.subtract, t)
                t = dv.tt(XT[:, p0:p0 + 4, :], AT[:, p0:p0 + 4, :], bc(C["t0"].unsqueeze(1), [128, 4, 128]), ALU.mult, t1)
                t = dv.tt(XT[:, p0:p0 + 4, :], idb, XT[:, p0:p0 + 4, :], ALU.subtract, t)
        M.finish(zjob)
        M.barrier()
        tX = [[] for _ in range(4)]
        tB = [[] for _ in range(4)]
        tyy = [None] * 4

        def below(lev, q):
            p0 = 4 * q
            s4 = slice(p0, p0 + 4)
            tb4 = po.tt(BT[:, s4, :], AT[:, s4, :], bc(C[f"t{lev}"].unsqueeze(1), [128, 4, 128]), ALU.mult, *tB[q])
            b, fr = M.bank()
            t = pe.mm([(ps[:, b, j * 128:j * 128 + 128], BT[:, p0 + j, :], X[:, p0 + j, :], True, True)
                       for j in range(4)], tb4, *tX[q], *fr)
            tB[q] = [t]
            tyy[q] = ac.cp(Y[:, s4, :].rearrange("p a b -> p (a b)"), ps[:, b, :], t, *tX[q])
            M.give(b, tyy[q])

        def joined(lev, q):
            p0 = 4 * q
            s4 = slice(p0, p0 + 4)
            b2, fr2 = M.bank()
            t2 = pe.mm([(ps[:, b2, j * 128:j * 128 + 128], Y[:, p0 + j, :], XT[:, p0 + j, :], True, True)
                        for j in range(4)], tyy[q], *fr2)
            if lev < 5:
                b1, fr1 = M.bank()
                t1 = pe.mm([(ps[:, b1, j * 128:j * 128 + 128], XT[:, p0 + j, :], Y[:, p0 + j, :], True, True)
                            for j in range(4)], tyy[q], *fr1)
                ta = dv.tt(X[:, s4, :], X[:, s4, :], ps[:, b1, :].rearrange("p (a b) -> p a b", a=4), ALU.subtract, t1)
                M.give(b1, ta)
                t2 = t1
            tc = dv.tt(XT[:, s4, :], XT[:, s4, :], ps[:, b2, :].rearrange("p (a b) -> p a b", a=4), ALU.subtract, t2)
            M.give(b2, tc)
            tX[q] = [tc, t2]

        levels = [(lev, q) for lev in range(1, 6) for q in range(4)]
        below(*levels[0])
        for i, at_ in enumerate(levels):
            if i + 1 < len(levels):
                below(*levels[i + 1])
            joined(*at_)
        M.barrier()
        kd, kbg = AT, Y
        eg = sc[:, :, 0:8]
        eb = sc[:, :, 8:16]
        ed = sc[:, :, 16:24]
        t = ac.act(eg, cum[:, :, 16:24], ACT.Exp)
        teb = dv.tt(eb, eg, beta, ALU.mult, t)
        for c in range(2):
            for half in range(2):
                hp = slice(64 * half, 64 * half + 64)
                t = dv.tt(ed[hp, c, :], tot[hp, 2 * c + half, 0:8], cum[hp, c, 16:24], ALU.subtract)
        ted = ac.act(ed, ed, ACT.Exp, t)
        for c in range(2):
            kv = bc(ktok[:, c, :, :].unsqueeze(2), [128, 4, 2, 128])
            for dst, s, tw, q in ((kbg, eb, teb, dv), (kd, ed, ted, dv)):
                sv = s[:, c, :].rearrange("p (a r) -> p a r", r=2).unsqueeze(3)
                tlast = q.tt(dst[:, 8 * c:8 * c + 8, :].rearrange("p (a r) t -> p a r t", r=2), kv,
                             bc(sv, [128, 4, 2, 128]), ALU.mult, tw)
        for q in range(4):
            c, g = q // 2, q % 2
            b, fr = M.bank()
            t = pe.mm([(ps[:, b, j * 128:j * 128 + 128], XT[:, 4 * q + j, :], vtok[:, c, 4 * g + j, :], True, True)
                       for j in range(4)], *fr)
            M.give(b, ac.cp(u[:, 4 * q:4 * q + 4, :].rearrange("p a b -> p (a b)"), ps[:, b, :], t))
            b, fr = M.bank()
            t = pe.mm([(ps[:, b, j * 128:j * 128 + 128], kbg[:, 4 * q + j, :], XT[:, 4 * q + j, :], True, True)
                       for j in range(4)], tlast, *fr)
            M.give(b, ac.cp(wT[:, 4 * q:4 * q + 4, :].rearrange("p a b -> p (a b)"), ps[:, b, :], t))
        tuw = ac.here()
        STs = [XT[:, 0:8, :], XT[:, 8:16, :]]
        tS = [[], []]
        tread = [[], []]
        o = y
        gate1, z2 = acc[:, 8:16, :], acc[:, 0:8, :]
        tg1, tz2 = [], []
        work = iter([*[silus(36, z2, tz2)] * 4, *[gates(17, gate1, tg1)] * 4])
        for n in range(4):
            c, half = n // 2, n % 2
            hp = slice(64 * half, 64 * half + 64)
            cols = slice(64 * n, 64 * n + 64)
            lc = slice(64 * half, 64 * half + 64)
            ST, SN = STs[n % 2], STs[1 - n % 2]
            tvn = []
            for g in range(2):
                p0 = 8 * c + 4 * g
                if n:
                    b, fr = M.bank()
                    t = pe.mm([(ps[:, b, j * 128:j * 128 + 128], wT[:, p0 + j, :], ST[:, 4 * g + j, :], True, True)
                               for j in range(4)], *tS[g], tuw, *fr)
                    tv_ = dv.tt(u[hp, p0:p0 + 4, :], u[hp, p0:p0 + 4, :],
                                ps[hp, b, :].rearrange("p (a b) -> p a b", a=4), ALU.subtract, t)
                    M.give(b, tv_)
                else:
                    tv_ = tuw
                tvn.append(tv_)
            if n < 3:
                for g in range(2):
                    p0 = 8 * c + 4 * g
                    b, fr = M.bank()
                    t2 = pe.mm([(ps[:, b, j * 128:j * 128 + 128], kd[hp, p0 + j, :], u[hp, p0 + j, :], True, True)
                                for j in range(4)], tvn[g], tlast, *fr)
                    P = ps[:, b, :].rearrange("p (a b) -> p a b", a=4)
                    new = SN[:, 4 * g:4 * g + 4, :]
                    if n:
                        t1 = dv.tt(new, ST[:, 4 * g:4 * g + 4, :],
                                   bc(etot[:, n, 4 * g:4 * g + 4].unsqueeze(2), [128, 4, 128]), ALU.mult, *tS[g], *tread[g])
                        t1 = dv.tt(new, new, P, ALU.add, t1, t2)
                    else:
                        t1 = dv.cp(new, P, t2, tuw)
                    M.give(b, t1)
                    tnew = [*(tnew if g else []), t1]
            if n < 3:
                M.fill(next(work), ada)
            for g in range(2):
                p0 = 8 * c + 4 * g
                b, fr = M.bank()
                parts = []
                for j in range(4):
                    oo = ps[:, b, j * 64:j * 64 + 64]
                    if n:
                        parts.append((oo, ST[:, 4 * g + j, :], qg[:, 4 * g + j, cols], True, False))
                    parts.append((oo, u[hp, p0 + j, :], qkT[hp, p0 + j, lc], n == 0, True))
                t = pe.mm(parts, tvn[g], *tS[g], *fr)
                M.give(b, ac.cp(o[:, 4 * g:4 * g + 4, cols], ps[:, b, 0:256].rearrange("p (a b) -> p a b", a=4), t))
                tread[g] = [t]
            to = ac.here()
            if n < 3:
                tS = [[t] for t in tnew]
                M.fill(next(work))
        M.fill(next(work))
        tys = []
        for g in range(2):
            s4 = slice(4 * g, 4 * g + 4)
            t = M.stats(o[:, s4, :], 4, 1, T, 1 / 128, ones, rs[:, s4, :], sq[:, s4, :], eps, to)
            M.fill(next(work) if g == 0 else ada)
            for i in range(4 * g, 4 * g + 4, 2):
                t1 = dv.tt(o[:, i:i + 2, :], o[:, i:i + 2, :], rs[:, i:i + 2, :], ALU.mult, t)
                ty = dv.stt(o[:, i:i + 2, :], o[:, i:i + 2, :], V["gn"], z[:, i:i + 2, :], ALU.mult, ALU.mult, t1, *tzz)
        M.barrier()
        A.at = top
        branch_out(o, ty, "wgo", gate1, tg1, True)
        M.barrier()
        A.at = keep

        z = A(8, T)
        acc = A(12, T)
        top = A.at
        pad = A(12, T + 3)
        tz = po.fill(pad[:, :, 0:3], 0.0)
        tcv = []
        def biased(i0, m, t):
            for i in range(i0, i0 + m):
                tcv[:] = [ac.act(acc[:, i, :], acc[:, i, :], ACT.Silu, t, bias=V["cb"][:, i:i + 1])]
        M.lin("win", layer, range(16, 28), xn, T, conv(pad, acc, "cw", tz, biased), txn)
        lat = M.slab[:, ARENA - 8 * T:ARENA].rearrange("p (a b) -> p a b", a=8)
        tlat, tg2 = [], []
        def elat(i, m, p, t):
            tlat[:] = [ac.cp(lat[:, i:i + m, :], p, t)]
            return tlat
        latjob = M.lins("win", layer, range(28, 36), xn, T, elat, txn)
        ta = tcv[0]
        M.fill(latjob)
        M.barrier()
        A.at = top
        gjob = gates(13, gate, tg2)
        Xd, Xs, Bt, Hs = A(2, 1024), A(1024), A(2, 128), A(2, 512)
        CB, L2, ytok = A(2, 2, 128), A(2, 16, 128), A(1024)
        tl = ac.act(sc[:, 0, 0:16], cum[:, 0, 0:16], ACT.Identity, scale=-1.0)
        t = dv.tt(sc[:, 0, 0:16], sc[:, 0, 0:16], tot[:, 4, :], ALU.add, tl)
        tdec = ac.act(sc[:, 0, 0:16], sc[:, 0, 0:16], ACT.Exp, t)
        teA = ac.act(sc[:, 1, 0:16], cum[:, 1, 0:16], ACT.Exp)
        txs, tcbs, tes = [], [], []
        for c in range(2):
            cs = slice(c * 128, c * 128 + 128)
            txd = []
            for g in range(2):
                b, fr = M.bank()
                t = pe.tr([(ps[:, b, j * 128:j * 128 + 128], acc[:, 4 * g + j, cs]) for j in range(4)], ident, ta, *fr)
                t = dv.tt(Xd[:, c, 512 * g:512 * g + 512].rearrange("p (h d) -> p h d", d=64),
                          ps[:, b, :].rearrange("p (h d) -> p h d", d=64),
                          bc(sp[:, c, 8 * g:8 * g + 8].unsqueeze(2), [128, 8, 64]), ALU.mult, t)
                M.give(b, t)
                txd.append(t)
            b, fr = M.bank()
            t = pe.mm([(ps[:, b, g * 128:g * 128 + 128], acc[:, 8 + g, cs], acc[:, 10 + g, cs], True, True)
                       for g in range(2)], ta, *fr)
            tcb = dv.tt(CB[:, c, :, :], ps[:, b, 0:256].rearrange("p (a b) -> p a b", a=2),
                        bc(C["tri"].unsqueeze(1), [128, 2, 128]), ALU.mult, t)
            M.give(b, tcb)
            txs.append(txd)
            tcbs.append(tcb)
        for c in range(2):
            te = []
            L = L2[:, c, :, :]
            for q in range(4):
                s4 = slice(4 * q, 4 * q + 4)
                b, fr = M.bank()
                t = pe.mm([(ps[:, b, j * 128:j * 128 + 128], bc(dA[:, c, 4 * q + j:4 * q + j + 1], [128, 128]),
                            C["tri"], True, True) for j in range(4)], *fr)
                t1 = dv.tt(L[:, s4, :], ps[:, b, :].rearrange("p (a b) -> p a b", a=4),
                           bc(cum[:, c, s4].unsqueeze(2), [128, 4, 128]), ALU.subtract, t)
                M.give(b, t1)
                t1 = dv.ts(L[:, s4, :], L[:, s4, :], 0.0, None, ALU.min, None, t1)
                t1 = ac.act(L[:, s4, :], L[:, s4, :], ACT.Exp, t1)
                te.append(po.tt(L[:, s4, :], L[:, s4, :], bc(CB[:, c, q // 2:q // 2 + 1, :], [128, 4, 128]), ALU.mult, t1, tcbs[c]))
                if c == 0 or q < 2:
                    M.fill(latjob if c == 0 else gjob)
            tes.append(te)
            if c == 0:
                cs = slice(0, 128)
                b, fr = M.bank()
                t = pe.tr([(ps[:, b, g * 128:g * 128 + 128], acc[:, 8 + g, cs]) for g in range(2)], ident, ta, *fr)
                tbt = ac.cp(Bt.rearrange("p a b -> p (a b)"), ps[:, b, 0:256], t)
                M.give(b, tbt)
                tx_ = dv.tt(Xs.rearrange("p (h d) -> p h d", d=64), Xd[:, 0, :].rearrange("p (h d) -> p h d", d=64),
                            bc(sc[:, 0, 0:16].unsqueeze(2), [128, 16, 64]), ALU.mult, tdec, *txs[0])
                for g in range(2):
                    b, fr = M.bank()
                    t = pe.mm([(ps[:, b, :], Bt[:, g, :], Xs[:, 512 * g:512 * g + 512], True, True)], tx_, tbt, *fr)
                    th = ac.cp(Hs[:, g, :], ps[:, b, :], t)
                    M.give(b, th)
        for c in range(2):
            cs = slice(c * 128, c * 128 + 128)
            L, te, txd = L2[:, c, :, :], tes[c], txs[c]
            tyt = []
            for g in range(2):
                b, fr = M.bank()
                t = pe.mm([(ps[:, b, 64 * h:64 * h + 64], L[:, 8 * g + h, :],
                            Xd[:, c, 512 * g + 64 * h:512 * g + 64 * h + 64], True, True) for h in range(8)],
                          *te[2 * g:2 * g + 2], *txd, *fr)
                if c == 0:
                    t1 = ac.cp(ytok[:, 512 * g:512 * g + 512], ps[:, b, :], t)
                    M.give(b, t1)
                else:
                    b2, fr2 = M.bank()
                    t2 = pe.mm([(ps[:, b2, :], acc[:, 10 + g, cs], Hs[:, g, :], True, True)], th, *fr2)
                    t1 = dv.tt(ytok[:, 512 * g:512 * g + 512].rearrange("p (h d) -> p h d", d=64),
                               ps[:, b2, :].rearrange("p (h d) -> p h d", d=64),
                               bc(sc[:, 1, 8 * g:8 * g + 8].unsqueeze(2), [128, 8, 64]), ALU.mult, t2, teA, *tyf)
                    M.give(b2, t1)
                    t1 = dv.tt(ytok[:, 512 * g:512 * g + 512], ytok[:, 512 * g:512 * g + 512], ps[:, b, :], ALU.add, t1, t)
                    M.give(b, t1)
                tyt.append(t1)
            tyf = []
            M.fill(ada)
            for g in range(2):
                b, fr = M.bank()
                t = pe.tr([(ps[:, b, j * 128:j * 128 + 128], ytok[:, (4 * g + j) * 128:(4 * g + j) * 128 + 128])
                           for j in range(4)], ident, tyt[g], *fr)
                tyf.append(t)
                for j in range(4):
                    i = 4 * g + j
                    t1 = dv.stt(y[:, i, cs], acc[:, i, cs], V["sd"][:, i:i + 1], ps[:, b, j * 128:j * 128 + 128],
                                ALU.mult, ALU.add, t)
                M.give(b, t1)
        for g in range(2):
            s4 = slice(4 * g, 4 * g + 4)
            t = dv.tt(y[:, s4, :], y[:, s4, :], z[:, s4, :], ALU.mult, t1)
            M.fill(gjob)
            t = M.stats(y[:, s4, :], 4, 4, T, 1 / 512, ones, rs[:, g:g + 1, :], sq[:, s4, :], eps, t)
            for i in range(4 * g, 4 * g + 4):
                ty = dv.stt(y[:, i, :], y[:, i, :], V["sn"][:, i:i + 1], rs[:, g, :], ALU.mult, ALU.mult, t)
        M.barrier()
        A.at = keep
        M.finish(latjob)
        M.finish(gjob)
        branch_out(y, ty, "wso", gate, tg2, False)
        M.barrier()
        A.at = keep

        tl = tlat
        tg3 = []
        gjob = gates(15, gate, tg3)
        qn, kn = A.pair(4, T), A.pair(2, T)
        q12, kT, vt = A(12, T), A(8, T), A(2, 1024)
        Pm, PT, ot = A(8, T), A(8, 2, 128), A(8, 128)
        mx, den = A(16), A(16)
        tq = normed(lat[:, 0:4, :], qn, 1 / 512, V["qn"], sq, rs, None, *tl)
        tk = normed(lat[:, 4:6, :], kn, 1 / 256, V["kn"], sq[:, 4:6, :], rs[:, 1:2, :], None, *tl)
        M.fill(gjob)
        M.lin("wuq", layer, range(6), qn, T, lambda i, m, p, t: [M.copy(q12[:, i:i + m, :], p, t)], tq)
        tqq = [ac.here(), dv.here()]
        M.lin("wuk", layer, range(2), kn, T, lambda i, m, p, t: [M.copy(kT[:, i:i + m, :], p, t)], tk)
        M.lint("wuv", layer, range(2), kn, 2, lambda m, c0, p, t: [M.copy(vt[:, m, c0:c0 + 512], p, t)], tk[-1])
        tkk = [ac.here(), dv.here()]

        def rope(a, bb, n, w):
            cs_, sn_ = (bc(S[k].unsqueeze(1), [128, n, T]) for k in ("cos", "sin"))
            m1, m2 = sq[:, 0:n, :], sq[:, 4:4 + n, :]
            t1 = dv.tt(m1, bb, sn_, ALU.mult, *w)
            t2 = dv.tt(m2, a, sn_, ALU.mult, *w)
            t3 = dv.tt(a, a, cs_, ALU.mult, t2)
            t4 = dv.tt(bb, bb, cs_, ALU.mult, t1)
            t3 = dv.tt(a, a, m1, ALU.subtract, t3)
            return dv.tt(bb, bb, m2, ALU.add, t4)

        trk = rope(lat[:, 6:7, :], lat[:, 7:8, :], 1, [*tl, pe.here(), dv.here(), *tabs])
        trq = rope(q12[:, 8:10, :], q12[:, 10:12, :], 2, [*tqq, dv.here()])
        M.fill(gjob)
        M.barrier()
        scale = 192 ** -0.5
        tpf, ttf = [[], []], [[], []]
        tof = []
        got = {}

        def scores(i, hp):
            nk = 128 * (i + 1)
            qs = slice(i * 128, i * 128 + 128)
            s = hp % 2
            Pv = Pm[:, 2 * s:2 * s + 2, :]
            b, fr = M.bank()
            parts = []
            for j in range(2):
                h = hp + 4 * j
                r = slice(32 * hp, 32 * hp + 32)
                o_ = ps[:, b, 256 * j:256 * j + nk]
                parts += [(o_, q12[:, h, qs], kT[:, h, 0:nk], True, False),
                          (o_, q12[r, 8 + h // 4, qs], lat[r, 6, 0:nk], False, False),
                          (o_, q12[r, 10 + h // 4, qs], lat[r, 7, 0:nk], False, True)]
            t = pe.mm(parts, trk, trq, *tkk, *fr)
            P = ps[:, b, :].rearrange("p (a b) -> p a b", a=2)
            dg = slice(128 * i, 128 * i + 128)
            t1 = [dv.tt(Pv[:, :, dg], P[:, :, dg], bc(C["causal"].unsqueeze(1), [128, 2, 128]), ALU.add, t, *tpf[s])]
            if i:
                t1.append(dv.cp(Pv[:, :, 0:128], P[:, :, 0:128], t, *tpf[s]))
            M.give(b, *t1)
            k0 = 8 * i + 2 * hp
            t1 = dv.red(mx[:, k0:k0 + 2], Pv[:, :, 0:nk], ALU.max, *t1)
            t1 = dv.ts(mx[:, k0:k0 + 2], mx[:, k0:k0 + 2], -scale, None, ALU.mult, None, t1)
            for j in range(2):
                te = ac.act(Pv[:, j, 0:nk], Pv[:, j, 0:nk], ACT.Exp, t1, bias=mx[:, k0 + j:k0 + j + 1],
                            scale=scale, acc=den[:, k0 + j:k0 + j + 1])
            got["e", i, hp] = te

        def turned(i, hp):
            s = hp % 2
            Pv = Pm[:, 2 * s:2 * s + 2, :]
            b, fr = M.bank()
            t = pe.tr([(ps[:, b, (2 * j + kb) * 128:(2 * j + kb) * 128 + 128], Pv[:, j, kb * 128:kb * 128 + 128])
                       for j in range(2) for kb in range(i + 1)], ident, got["e", i, hp], *fr)
            tpf[s] = [t]
            PTv = PT[:, 2 * s:2 * s + 2, :, :]
            t = ac.cp(PTv[:, :, 0:i + 1, :], ps[:, b, :].rearrange("p (a k b) -> p a k b", a=2, k=2)[:, :, 0:i + 1, :],
                      t, *ttf[s])
            M.give(b, t)
            got["p", i, hp] = t

        def mixed_values(i, hp):
            s = hp % 2
            qs = slice(i * 128, i * 128 + 128)
            k0 = 8 * i + 2 * hp
            td = dv.recip(den[:, k0:k0 + 2], den[:, k0:k0 + 2], got["e", i, hp])
            PTv = PT[:, 2 * s:2 * s + 2, :, :]
            b, fr = M.bank()
            t = pe.mm([(ps[:, b, 128 * j:128 * j + 128], PTv[:, j, kb, :], vt[:, kb, (hp + 4 * j) * 128:(hp + 4 * j) * 128 + 128],
                        kb == 0, kb == i) for j in range(2) for kb in range(i + 1)], got["p", i, hp], *fr)
            ttf[s] = [t]
            t = dv.tt(ot[:, hp:hp + 5:4, :], ps[:, b, 0:256].rearrange("p (a b) -> p a b", a=2),
                      bc(den[:, k0:k0 + 2].unsqueeze(2), [128, 2, 128]), ALU.mult, t, td, *(tof if i else []))
            M.give(b, t)
            if hp == 3:
                for g in range(2):
                    b, fr = M.bank()
                    t1 = pe.tr([(ps[:, b, j * 128:j * 128 + 128], ot[:, 4 * g + j, :]) for j in range(4)], ident, t, *fr)
                    tof.append(t1)
                    M.give(b, ac.cp(y[:, 4 * g:4 * g + 4, qs], ps[:, b, :].rearrange("p (a b) -> p a b", a=4), t1))

        steps = [(i, hp) for i in range(2) for hp in range(4)]
        for n in range(len(steps) + 2):
            if n < len(steps):
                scores(*steps[n])
            if 1 <= n <= len(steps):
                turned(*steps[n - 1])
            if n >= 2:
                mixed_values(*steps[n - 2])
            M.fill(gjob if n % 4 == 2 else ada)
        M.finish(gjob)
        ty = ac.here()
        M.barrier()
        A.at = keep
        ms = A.pair(8, T)
        tm = branch_out(y, ty, "wmo", gate, tg3, False, ms)

        def res(i, m, p, t):
            t = dv.tt(x[:, i:i + m, :], x[:, i:i + m, :], p, ALU.add, t)
            power.add(i, x[:, i:i + m, :], t)
            return [t]
        power = Power(M, ones, sq, T, 8)
        M.lin("wo", layer, range(8), ms, T, res, tm)
        txn = normed(x, xn, 1 / 1024, V["n2"], sq, rs, power)
        M.fill(ada, ada)
        A.at = keep
        hid = A.pair(32, T)
        thid = []
        tmp = [A(2, T) for _ in range(3)]
        free = [[] for _ in range(3)]

        def up(i, m, p, t):
            s = (i // 2) % 3
            f = tmp[s]
            t1 = ac.act(f, p, ACT.Relu, t, *free[s])
            t2 = dv.tt(f, f, f, ALU.mult, t1, txn[-1])
            free[s] = [M.split([v[:, i:i + 2, :] for v in hid], f, t2)]
            thid.extend(free[s] * 2)
            return [t1]
        M.lin("wup", layer, range(32), xn, T, up, txn)
        power = Power(M, ones, sq, T, 8)
        M.lin("wdn", layer, range(8), hid, T, res, thid)
        tx = [dv.here()]
        A.at = base

    t = power.root(rs[:, 0, :], 1 / 1024, eps)
    for i in range(0, 8, 2):
        for j in range(i, i + 2):
            t1 = dv.stt(x[:, j, :], x[:, j, :], S["vec1"][0]["fn"][:, j:j + 1], rs[:, 0, :], ALU.mult, ALU.mult, t)
    t = t1
    A.at = base
    M.barrier()
    return t


def second_block(M, A, S, tx0):
    pe, dv, ac, po, ps = M.pe, M.dv, M.ac, M.po, M.ps
    C, x = S["c"], S["x2"]
    ident, ones, eps = C["ident"], C["ones"], S["eps"]
    LAT, CTX = slice(0, 256), slice(256, 512)
    cases = (LAT, CTX)
    tx = [tx0, *S["tx"], S["tctx"]]
    power = None
    for layer in range(2):
        V, tv = S["vec2"][layer]
        last = layer == 1
        base = A.at
        mod, A1, A2 = S["mods"][layer], A(8, 2), A(8, 2)
        h = A.pair(8, 512)
        early = A.at
        tmp = A(6144)
        sq = tmp[:, 0:4096].rearrange("p (a b) -> p a b", a=8)
        rs = tmp[:, 4096:6144].rearrange("p (a b) -> p a b", a=4)
        keep = A.at

        M.finish(S["ada"][layer])
        tmod = dv.here()
        for dst, g, off in ((A1, "n1", 8), (A2, "n2", 32)):
            tmod = dv.stt(dst, mod[:, off:off + 8, :], 1.0, bc(V[g].unsqueeze(2), [128, 8, 2]), ALU.add, ALU.mult, tmod, *tx)

        def modulated(Am, off, n, power, *w, jobs):
            if power is None:
                power = Power(M, ones, sq, n, 8)
                for i in range(0, 8, 2):
                    power.add(i, x[:, i:i + 2, 0:n], *w)
            t = power.root(rs[:, 0, 0:n], 1 / 1024, eps)
            M.fill(*jobs)
            return M.scaled(x[:, :, 0:n], h, n, lambda i, c: Am[:, i, c:c + 1], lambda i, c: mod[:, off + i, c:c + 1],
                            rs, sq, t, tmod)

        def onto_x(goff, n, power=None):
            def ev(i, m, p, t):
                for j in range(m):
                    for case in range(n // 256):
                        s = cases[case]
                        t1 = dv.stt(x[:, i + j, s], p[:, j, s], mod[:, goff + i + j, case:case + 1], x[:, i + j, s],
                                    ALU.mult, ALU.add, t)
                if power is not None:
                    if (i + m) % 2 == 0:
                        power.add(i + m - 2, x[:, i + m - 2:i + m, 0:n], t1)
                return [t1]
            return ev

        th = modulated(A1, 0, 512, power, *tx, jobs=[S["ada"][1]] * 3)
        if layer == 0:
            q, k, vt = A(8, 512), A(8, 512), A(4, 1024)
            P4, PT4, ot = A(4, 512), A(4, 512), A(1024)
            den, mx = A(8, 16), A(8, 16)
            M.lin("nqkv", 0, range(8), h, 512, lambda i, m, p, t: [M.copy(q[:, i:i + m, :], p, t)], th)
            M.lin("nqkv", 0, range(8, 16), h, 512, lambda i, m, p, t: [M.copy(k[:, i:i + m, :], p, t)], th)
            tqk = [ac.here(), dv.here()]
            M.lint("nqkv", 0, range(16, 24), h, 4, lambda m, c0, p, t: [M.copy(vt[:, m, c0:c0 + 256], p, t)], th[-1])
            tvv = [ac.here(), dv.here()]
            w = tqk
            for src, gain, f in ((q, "qg", 0.125), (k, "kg", 1.0)):
                for g in range(2):
                    s4 = slice(4 * g, 4 * g + 4)
                    t = M.stats(src[:, s4, :], 4, 1, 512, 1 / 64, C["bd64"], rs, sq, eps, *w)
                    t = dv.tt(src[:, s4, :], src[:, s4, :], rs, ALU.mult, t)
                    w = [t]
                    M.fill(*[S["ada"][1]] * 2)
                t = dv.ts(src, src, V[gain], f, ALU.mult, ALU.mult, t)
                w = [t]
            M.barrier()
            bias = sq
            oF = h
            tpf, ttf = [[] for _ in range(4)], [[] for _ in range(4)]
            tbw = [[], []]
            bt = {}
            tof, got = [], {}

            def scores(i, hp):
                qs = slice(128 * i, 128 * i + 128)
                lat = i < 2
                ks = slice(0, 512) if lat else CTX
                k0 = 0 if lat else 256
                bs = (hp // 4) % 2
                bv = bias[:, 4 * bs:4 * bs + 4, :].rearrange("p a (b c) -> p (a b) c", c=256)
                if lat and hp % 4 == 0:
                    M.dma(bv, M.d["rpb"][i, bs], S["bsem"][bs], [*tbw[bs], first])
                    bt[bs] = (S["bsem"][bs], 16 * (i + 1))
                banks = []
                for j in range(2):
                    r = slice(64 * j, 64 * j + 64)
                    b, fr = M.bank()
                    banks.append((b, pe.mm([(ps[:, b, k0:512], q[r, hp, qs], k[r, hp, ks], True, True)], *fr, *w)))
                for j in range(2):
                    b, t = banks[j]
                    hd = 2 * hp + j
                    s = hd % 4
                    Pv = P4[:, s, :]
                    if lat:
                        t1 = dv.tt(Pv[:, LAT], ps[:, b, LAT], bv[:, hd % 8, :], ALU.add, t, bt[bs], *tpf[s])
                        t2 = ac.cp(Pv[:, CTX], ps[:, b, CTX], t1, *tpf[s])
                        M.give(b, t1, t2)
                        if hd % 8 == 7:
                            tbw[bs] = [t1]
                        pin, tw = Pv, [t1, t2]
                    else:
                        pin, tw = ps[:, b, CTX], [t]
                    m_ = mx[:, i, hd:hd + 1]
                    t1 = self_neg_max(dv, m_, pin, tw)
                    te = ac.act(Pv[:, k0:512], pin, ACT.Exp, t1, *tpf[s], bias=m_, acc=den[:, i, hd:hd + 1])
                    if not lat:
                        M.give(b, te)
                    got["e", i, hd] = te

            def turned(i, hp):
                k0 = 0 if i < 2 else 256
                for j in range(2):
                    hd = 2 * hp + j
                    s = hd % 4
                    b, fr = M.bank()
                    t = pe.tr([(ps[:, b, c:c + 128], P4[:, s, c:c + 128]) for c in range(k0, 512, 128)], ident,
                              got["e", i, hd], *fr)
                    tpf[s] = [t]
                    t = M.copy(PT4[:, s, k0:512], ps[:, b, k0:512], t, *ttf[s])
                    M.give(b, t)
                    got["p", i, hd] = t

            def mixed_values(i, hp):
                k0 = 0 if i < 2 else 256
                blocks = range(k0 // 128, 4)
                te = [got["e", i, 2 * hp + j] for j in range(2)]
                td = dv.recip(den[:, i, 2 * hp:2 * hp + 2], den[:, i, 2 * hp:2 * hp + 2], *te)
                b, fr = M.bank()
                parts = []
                for j in range(2):
                    hd = 2 * hp + j
                    parts += [(ps[:, b, 64 * j:64 * j + 64], PT4[:, hd % 4, kb * 128:kb * 128 + 128],
                               vt[:, kb, 64 * hd:64 * hd + 64], kb == blocks[0], kb == 3) for kb in blocks]
                t = pe.mm(parts, *[got["p", i, 2 * hp + j] for j in range(2)], *tvv, *fr)
                for j in range(2):
                    ttf[(2 * hp + j) % 4] = [t]
                t = dv.tt(ot[:, 128 * hp:128 * hp + 128].rearrange("p (a b) -> p a b", a=2),
                          ps[:, b, 0:128].rearrange("p (a b) -> p a b", a=2),
                          bc(den[:, i, 2 * hp:2 * hp + 2].unsqueeze(2), [128, 2, 64]), ALU.mult, t, td, *tof)
                M.give(b, t)
                if hp == 7:
                    for g in range(2):
                        b, fr = M.bank()
                        t1 = pe.tr([(ps[:, b, j * 128:j * 128 + 128], ot[:, 512 * g + j * 128:512 * g + j * 128 + 128])
                                    for j in range(4)], ident, t, *fr)
                        tof.append(t1)
                        M.give(b, M.split([v[:, 4 * g:4 * g + 4, 128 * i:128 * i + 128] for v in oF],
                                          ps[:, b, :].rearrange("p (a b) -> p a b", a=4), t1))

            first = pe.here()
            steps = [(i, hp) for i in range(4) for hp in range(8)]
            for n in range(len(steps) + 2):
                if n < len(steps):
                    scores(*steps[n])
                if 1 <= n <= len(steps):
                    turned(*steps[n - 1])
                if n >= 2:
                    mixed_values(*steps[n - 2])
                if n % 4 == 1 and n < 30:
                    M.fill(S["ada"][1])
            to = dv.here()
            M.barrier()
            power = Power(M, ones, sq, 512, 8)
            M.lin("no", 0, range(8), oF, 512, onto_x(16, 512, power), [to] * 8)
            n = 512
        else:
            q, vt = A(8, 256), A(4, 1024)
            B, K = A(8, 512), A(8, 512)
            St, AA = A(8, 128), A(8, 2, 256)
            masks = S["trig"][:, 0:480]
            lb, p0_, mm_ = A(32), A(16), A(16)
            g_ = M.slab[:, early - 8192:early - 4096].rearrange("p (a b) -> p a b", a=8)[:, :, CTX]
            tgg = []
            def eg(i, m, p, t):
                tgg[:] = [ac.act(g_[:, i:i + m, :], p, ACT.Silu, t)]
                return tgg
            gjob = M.lins("hin", 0, range(16, 24), h, 256, eg, th)
            sets = [[tmp[:, 1024 * (3 * i + j):1024 * (3 * i + j + 1)].rearrange("p (a b) -> p a b", a=4) for j in range(3)]
                    for i in range(2)]
            Mu = masks[:, :].bitcast(mybir.dt.uint8).rearrange("p (a b) -> p a b", b=128)
            M.dma(tmp[:, 0:1920], M.d["imask"], S["isem"], [th[-1]])
            tmask = dv.cp(masks.bitcast(mybir.dt.uint8), tmp[:, 0:1920], (S["isem"], 16), th[-1])
            hl = V["hl"]
            t = dv.tt(mm_, hl[:, 0:16], hl[:, 16:32], ALU.max, *tv, th[-1])
            t = dv.tt(lb.rearrange("p (a b) -> p a b", a=2), hl.rearrange("p (a b) -> p a b", a=2),
                      bc(mm_.unsqueeze(1), [128, 2, 16]), ALU.subtract, t)
            t = ac.act(lb, lb, ACT.Exp, t)
            t = dv.tt(mm_, lb[:, 0:16], lb[:, 16:32], ALU.add, t)
            t = dv.recip(mm_, mm_, t)
            t = dv.tt(lb.rearrange("p (a b) -> p a b", a=2), lb.rearrange("p (a b) -> p a b", a=2),
                      bc(mm_.unsqueeze(1), [128, 2, 16]), ALU.mult, t)
            t = dv.tt(mm_, lb[:, 0:16], lb[:, 16:32], ALU.add, t)
            t = dv.tt(mm_, mm_, lb[:, 0:16], ALU.subtract, t)
            tlb = dv.ts(p0_, mm_, -1.0, 1.0, ALU.mult, ALU.add, t)
            LB, OM = mm_, p0_
            M.lin("hin", 0, range(8), h, 256, lambda i, m, p, t: [ac.act(q[:, i:i + m, :], p, ACT.Silu, t)], th)
            tqg = ac.here()
            M.lint("hin", 0, range(8, 16), h, 4, lambda m, c0, p, t: [M.copy(vt[:, m, c0:c0 + 256], p, t)], th[-1])
            tvv = [ac.here(), dv.here()]
            ta0 = po.fill(AA, 0.0, th[-1])
            tAA = [[ta0] for _ in range(4)]
            tz = po.fill(tmp[:, 1920:6144], 0.0, th[-1])
            o1 = ones[:, 0:1]
            for dr in range(2):
                E, Qt, Kt = (tmp[:, 2048 * i:2048 * i + 2048] for i in range(3))
                E3, Q3, K3 = (v.rearrange("p (a b) -> p a b", a=8) for v in (E, Qt, Kt))

                def ef(i, m, p, t, dr=dr):
                    t1 = ac.act(B[:, i:i + m, :], p, ACT.Sigmoid, t, tmask)
                    t2 = ac.act(K[:, i:i + m, :], p, ACT.Sigmoid, t, scale=-1.0)
                    for j in range(i, i + m):
                        d = 8 * dr + j
                        dv.ts(B[:, j, :], B[:, j, :], OM[:, d:d + 1], LB[:, d:d + 1], ALU.mult, ALU.add, t1, tlb)
                        tef.append(dv.ts(K[:, j, :], K[:, j, :], OM[:, d:d + 1], None, ALU.mult, None, t2, tlb))
                    return [t2]
                tef = []
                job = M.lins("hin", 0, range(24 + 8 * dr, 32 + 8 * dr), h, 512, ef, th)
                rev = slice(None, None, -1)

                def sums(j0):
                    s4 = slice(j0, j0 + 4)
                    t = dv.ts(B[:, s4, :], B[:, s4, :], 1e-19, None, ALU.max, None, tef[-1])
                    t = ac.act(B[:, s4, :], B[:, s4, :], ACT.Ln, t)
                    for j in range(j0, j0 + 4):
                        lat, ctx = B[:, j, LAT], B[:, j, CTX]
                        if dr:
                            lat = lat[:, ::-1]
                        else:
                            ctx = ctx[:, ::-1]
                        on = bc(o1, [128, 256])
                        dv.scan(lat, on, lat, t)
                        tsn = dv.scan(ctx, on, ctx, t)
                    return tsn
                M.fill(*[job] * 3)
                sums(0)
                M.finish(job)
                if dr:
                    M.fill(gjob)
                tk = tef[-1]
                tsn = sums(4)
                src, dst = (slice(257, 512), slice(256, 511)) if dr == 0 else (slice(256, 511), slice(257, 512))
                t = ac.act(E3[:, :, 0:255], B[:, :, src], ACT.Exp, tsn)
                tkd = dv.tt(K[:, :, dst], K[:, :, dst], E3[:, :, 0:255], ALU.mult, t, tk)
                kd = K3.rearrange("p a (b c) -> p a b c", b=2)
                for j in range(0, 8, 2):
                    b, fr = M.bank()
                    t = pe.tr([(ps[:, b, (2 * a + c) * 128:(2 * a + c) * 128 + 128],
                                K[:, j + a, 256 + 128 * c:384 + 128 * c]) for a in range(2) for c in range(2)], ident, tkd, *fr)
                    t = M.copy(Kt[:, 256 * j:256 * j + 512], ps[:, b, :], t)
                    M.give(b, t)
                    b, fr = M.bank()
                    t = pe.mm([(ps[:, b, 128 * a:128 * a + 128], kd[:, j + a, c, :],
                                vt[:, 2 + c, 128 * (j + a):128 * (j + a) + 128], c == 0, c == 1)
                               for a in range(2) for c in range(2)], t, *tvv, *fr)
                    tst = ac.cp(St[:, j:j + 2, :], ps[:, b, 0:256].rearrange("p (a b) -> p a b", a=2), t)
                    M.give(b, tst)
                Bl, Kl = B[:, :, LAT], K[:, :, LAT]
                use = [[t, tsn, tkd], [t, tsn, tkd]]
                for j in range(0, 8, 2):
                    b, fr = M.bank()
                    t = pe.mm([(ps[:, b, (2 * a + c) * 128:(2 * a + c) * 128 + 128], K[:, j + a, 128 * c:128 * c + 128],
                                q[:, j + a, 128 * c:128 * c + 128], True, True) for a in range(2) for c in range(2)],
                              tk, tqg, *fr)
                    Pq = ps[:, b, :].rearrange("p (a c t) -> p a c t", a=2, c=2)
                    for c in range(2):
                        dst_ = AA[:, j:j + 2, c, 128 * c:128 * c + 128]
                        if dr == 0:
                            t1 = dv.pick(dst_, bc(Mu[:, 14:15, :], [128, 2, 128]), Pq[:, :, c, :], t, tmask, *tAA[j // 2])
                        else:
                            own = sets[j // 4][0][:, j % 4:j % 4 + 2, 128 * c:128 * c + 128]
                            t2 = dv.tt(own, Pq[:, :, c, :], bc(ident.unsqueeze(1), [128, 2, 128]), ALU.mult, t, *use[j // 4])
                            t1 = dv.tt(dst_, dst_, own, ALU.add, t2, *tAA[j // 2])
                    M.give(b, t1)
                    tAA[j // 2] = [t1]
                    use[j // 4].append(t1)
                td, tq2, tk2, prod = [None, None], [None, None], [None, None], {}

                def sides(v, hf):
                    v = v.rearrange("p a (n r) -> p a n r", r=2 * hf)
                    left, right = v[:, :, :, 0:hf], v[:, :, :, hf:2 * hf]
                    return (right, left) if dr == 0 else (left, right)

                def decays(lv, i):
                    hf = 1 << lv
                    mid = hf - 1 if dr == 0 else hf
                    Bh, E3 = Bl[:, 4 * i:4 * i + 4, :], sets[i][0]
                    mb = bc(Bh.rearrange("p a (n r) -> p a n r", r=2 * hf)[:, :, :, mid:mid + 1], [128, 4, 256 // (2 * hf), hf])
                    (eq, ek), (bq, bk) = sides(E3, hf), sides(Bh, hf)
                    free = use[i] if tq2[i] is None else [tq2[i], tk2[i]]
                    dv.tt(eq, bq, mb, ALU.subtract, tsn, *free)
                    t = dv.tt(ek, mb, bk, ALU.subtract)
                    td[i] = ac.act(E3, E3, ACT.Exp, t)

                def scaled(lv, i):
                    hf = 1 << lv
                    E3, Q3, K3 = sets[i]
                    (eq, ek), (qq, _), (_, kk) = sides(E3, hf), sides(Q3, hf), sides(K3, hf)
                    tq2[i] = po.tt(qq, sides(q[:, 4 * i:4 * i + 4, :], hf)[0], eq, ALU.mult, td[i], tqg, tz, *use[i])
                    tk2[i] = (po if lv % 2 else dv).tt(kk, sides(Kl[:, 4 * i:4 * i + 4, :], hf)[1], ek, ALU.mult, td[i], tk, tz, *use[i])

                def between(lv, i):
                    _, Q3, K3 = sets[i]
                    prod[lv, i] = []
                    if lv < 7:
                        for j in range(0, 4, 2):
                            b, fr = M.bank()
                            t = pe.mm([(ps[:, b, (2 * a + c) * 128:(2 * a + c) * 128 + 128], K3[:, j + a, 128 * c:128 * c + 128],
                                        Q3[:, j + a, 128 * c:128 * c + 128], True, True) for a in range(2) for c in range(2)],
                                      tq2[i], tk2[i], *fr)
                            prod[lv, i].append((b, t))
                    else:
                        sb_, tb_ = (0, 1) if dr == 0 else (1, 0)
                        b, fr = M.bank()
                        t = pe.mm([(ps[:, b, a * 128:a * 128 + 128], K3[:, a, 128 * sb_:128 * sb_ + 128],
                                    Q3[:, a, 128 * tb_:128 * tb_ + 128], True, True) for a in range(4)], tq2[i], tk2[i], *fr)
                        prod[lv, i].append((b, t))
                    use[i] = [t, tq2[i], tk2[i]]

                def placed(lv, i):
                    last_ = None
                    for n_, (b, t) in enumerate(prod[lv, i]):
                        j = 4 * i + 2 * n_
                        if lv < 7:
                            mk = bc(Mu[:, 7 * dr + lv:7 * dr + lv + 1, :], [128, 2, 128])
                            Pq = ps[:, b, :].rearrange("p (a c t) -> p a c t", a=2, c=2)
                            for c in range(2):
                                last_ = dv.pick(AA[:, j:j + 2, c, 128 * c:128 * c + 128], mk, Pq[:, :, c, :], t, tmask, *tAA[j // 2])
                            tAA[j // 2] = [last_]
                        else:
                            sb_, tb_ = (0, 1) if dr == 0 else (1, 0)
                            last_ = dv.cp(AA[:, j:j + 4, sb_, 128 * tb_:128 * tb_ + 128],
                                          ps[:, b, :].rearrange("p (a t) -> p a t", a=4), t, ta0)
                        M.give(b, last_)
                    return last_

                steps = [(lv, i) for lv in range(8) for i in range(2)]
                decays(*steps[0])
                for n_ in range(17):
                    if n_ < 15:
                        decays(*steps[n_ + 1])
                    if n_ < 16:
                        scaled(*steps[n_])
                        between(*steps[n_])
                    if n_ > 0:
                        t1 = placed(*steps[n_ - 1])
                    if dr and n_ % 2:
                        M.fill(gjob)
                tq_ = []
                for i in range(2):
                    E3, Q3, _ = sets[i]
                    t = ac.act(E3, Bl[:, 4 * i:4 * i + 4, :], ACT.Exp, tsn, *use[i])
                    tq_.append(dv.tt(Q3, q[:, 4 * i:4 * i + 4, :], E3, ALU.mult, t))
                O = x[:, :, CTX]
                for j in range(0, 8, 2):
                    b, fr = M.bank()
                    parts = []
                    for a in range(2):
                        oo = ps[:, b, 256 * a:256 * a + 256]
                        parts.append((oo, St[:, j + a, :], sets[j // 4][1][:, (j + a) % 4, :], True, dr == 0))
                        if dr:
                            parts += [(oo, vt[:, c, 128 * (j + a):128 * (j + a) + 128], AA[:, j + a, c, :], False, c == 1)
                                      for c in range(2)]
                    t = pe.mm(parts, *tq_, tst, *([t1] if dr else []), *fr)
                    P = ps[:, b, :].rearrange("p (a b) -> p a b", a=2)
                    if dr == 0:
                        to = dv.cp(O[:, j:j + 2, :], P, t)
                    else:
                        to = dv.tt(O[:, j:j + 2, :], O[:, j:j + 2, :], P, ALU.add, t)
                    M.give(b, to)
                M.barrier()
            t = M.stats(O, 8, 1, 256, 1 / 128, ones, S["rs8"](A, AA), sq, eps, to)
            t = dv.tt(O, O, S["rs8"](A, AA), ALU.mult, t)
            to = dv.stt(O, O, V["hn"], g_, ALU.mult, ALU.mult, t, *tgg)
            os_ = [v[:, :, 0:256] for v in h]
            tos = M.splits(os_, O, [to])
            power = Power(M, ones, sq, 256, 8)
            M.lin("ho", 0, range(8), os_, 256, onto_x(16, 256, power), tos)
            n = 256
        A.at = keep
        th = modulated(A2, 24, n, power, jobs=[S["ada"][1]] * 3)
        A.at = early
        hid = A.pair(22, n)
        per = 512 // n
        places = A.at
        tmp2 = [A(per, n) for _ in range(3 * (2 // per))]
        free = [[] for _ in tmp2]
        ta_ = [None] * len(tmp2)

        thid = []

        def up(i, m, p, t):
            c, r = i // 4, i % 4
            s = (c * (2 // per) + (r % 2) // per) % len(tmp2)
            f = tmp2[s]
            if r < 2:
                ta_[s] = ac.act(f, p, ACT.Silu, t, *free[s])
                return [ta_[s]]
            at = 2 * c + r % 2
            t1 = dv.tt(f, f, p, ALU.mult, t, ta_[s])
            free[s] = [M.split([v[:, at:at + m, :] for v in hid], f, t1)]
            thid.extend(free[s] * m)
            return [t1]
        M.lin("fi", layer, range(44), h, n, up, th)
        places = M.slab[:, places:places + 4 * n].rearrange("p (a b) -> p a b", a=4)
        power = None if last else Power(M, ones, places, n, 8)
        M.lin("fo", layer, range(8), hid, n, onto_x(40, n, power), thid)
        tx = [dv.here()]
        A.at = base
    return tx[0]


def self_neg_max(dv, out, src, w):
    return dv(lambda e: e.tensor_reduce(out, src, AX.X, ALU.max, negate=True), w)


def program(nc, d, out, plan=None):
    with ExitStack() as ctx:
        M = Machine(nc, ctx, d, plan)
        x2 = M.sb("x2", [128, 8, 512])
        cst = M.sb("cst", [128, len(CONSTS), 128])
        o1, n1 = offsets(VEC1)
        o2, n2 = offsets(VEC2)
        v1 = M.sb("v1", [128, 2, n1])
        v2 = M.sb("v2", [128, 2, n2])
        posi = M.sb("posi", [128, T], I32)
        trig = M.sb("trig", [128, 2 * T])
        eps = M.sb("eps", [128, 1])
        cvec, silc = M.sb("cvec", [128, 8, 2]), M.sb("silc", [128, 8, 2])
        row = M.sb("row", [2, 2, 256])
        A = Arena(M)
        mods = M.sb("mods", [128, 2, 48, 2])
        sx, sv, s2 = M.sem("x"), M.sem("v"), M.sem("v2")
        for o, i in ((x2[:, :, 0:256], d["x"]), (cst[:, :, :], d["cst"]),
                     (posi[:, :], d["pos"]), (cvec[:, :, :], d["c"]), (v1[:, :, :], d["v1"]), (v2[:, :, :], d["v2"])):
            M.dma(o, i, sx)
        M.dma(x2[:, :, 256:512], d["ctx"], sv)
        te = M.po.fill(eps[:, :], EPS)
        tx = [(sx, 16 * 6), te]
        C = {k: cst[:, i, :] for i, k in enumerate(CONSTS)}
        vec = lambda v, o, l: {k: v[:, l, a:b] for k, (a, b) in o.items()}
        S = {"c": C, "x": x2[:, :, 0:256], "x2": x2[:, :, :], "eps": eps[:, :], "tx": tx, "pos": posi[:, :],
             "cos": trig[:, 0:T], "sin": trig[:, T:2 * T], "trig": trig[:, :], "vec1": (vec(v1, o1, 0), tx), "vec1b": (vec(v1, o1, 1), tx),
             "vec2": [(vec(v2, o2, l), tx) for l in range(2)], "cvec": cvec[:, :, :], "tctx": (sv, 16), "row": [row[:, i, :] for i in range(2)], "silc": silc[:, :, :], "mods": [mods[:, l, :, :] for l in range(2)],
             "bsem": [M.sem("b0"), M.sem("b1")], "isem": M.sem("im"),
             
             "rs8": lambda A, AA: AA.rearrange("p a b c -> p (a b c)")[:, 0:2048].rearrange("p (a b) -> p a b", a=8)}
        so = M.sem("out")
        modulation(M, S)
        t = first_block(M, A, S)
        if STAGE == 2:
            t = second_block(M, A, S, t)
        if plan is None:
            return M.asked
        M.dma(out, x2[:, :, 0:256], so, [t])
        M.sp.items.append((lambda e: e.wait_ge(so, 16), [], False))
        block = ctx.enter_context(nc.Block())

        @block.sync
        def _(e):
            M.sp.play(e)

        @block.tensor
        def _(e):
            M.pe.play(e)

        @block.vector
        def _(e):
            M.dv.play(e)

        @block.scalar
        def _(e):
            M.ac.play(e)

        @block.gpsimd
        def _(e):
            M.po.play(e)
        return A.top


STAGE = 2
ARENA = 34432


def constants():
    i, j = np.meshgrid(np.arange(128), np.arange(128), indexing="ij")
    f = lambda m: m.astype(np.float32)
    same = i // 64 == j // 64
    lev = lambda h: (i // (2 * h) == j // (2 * h)) & (i % (2 * h) < h) & (j % (2 * h) >= h)
    m = {"ident": f(i == j), "ones": f(i == i), "tri": f(i <= j), "bd64": f(same), "btri": f(same & (i <= j)),
         "bstrict": f(same & (i < j)), "cone0": f(i < 64), "cone1": f(i >= 64), "m0": f(lev(1)).T,
         "causal": np.where(j > i, np.float32(NEG), np.float32(0)).astype(np.float32)}
    for n in range(6):
        m[f"t{n}"] = f(lev(1 << n))
    cst = np.stack([m[k] for k in CONSTS], 1)
    ints = [lev(1 << n) for n in range(7)] + [lev(1 << n).T for n in range(7)] + [i == j]
    return np.ascontiguousarray(cst), np.ascontiguousarray(np.stack(ints, 1).astype(np.float32).reshape(128, 1920))


def tiled(name, w):
    k, n, c, parts = MATS[name]
    w = np.asarray(w).reshape(-1, k // 128, 128, n // c, c).transpose(0, 3, 2, 1, 4)
    most = -(-(k // 128) // parts)
    w = np.pad(w, ((0, 0), (0, 0), (0, 0), (0, most * parts - k // 128), (0, 0)))
    w = w.reshape(w.shape[0], n // c, 128, parts, most * c).transpose(0, 1, 3, 2, 4).reshape(w.shape[0], -1, 128, most * c)
    if w.shape[1] > 1:
        w = w.reshape(w.shape[0], -1, 2, 128, most * c).transpose(0, 1, 3, 2, 4)
    return np.ascontiguousarray(w).reshape(w.shape[0], w.shape[1], 128, -1)


def cols(v):
    v = np.asarray(v)
    return v.reshape(*v.shape[:-1], -1, 128).swapaxes(-1, -2)


def layout(a):
    d = {}
    win = a["w_in"]
    z, xbc, dt, cq, ckv, kr, qkv, gz, gb, ga, gate = np.split(
        win, np.cumsum([1024, 1536, 16, 512, 256, 64, 2048, 1024, 8, 8]).tolist(), axis=-1)
    r1, r2 = np.tile(kr[..., 0:32], (1, 1, 4)), np.tile(kr[..., 32:64], (1, 1, 4))
    d["win"] = tiled("win", np.concatenate([qkv, xbc, cq, ckv, r1, r2, z, gz, gate], -1))
    d["wsm"] = tiled("wsm", np.concatenate([dt, ga, gb], -1))
    uq = a["mla_w_uq"].reshape(2, 512, 8, 192)
    d["wuq"] = tiled("wuq", np.concatenate([uq[..., 0:128].reshape(2, 512, 1024), uq[..., 128:160].reshape(2, 512, 256),
                                            uq[..., 160:192].reshape(2, 512, 256)], -1))
    ukv = a["mla_w_ukv"].reshape(2, 256, 8, 256)
    d["wuk"] = tiled("wuk", ukv[..., 0:128].reshape(2, 256, 1024))
    d["wuv"] = tiled("wuv", ukv[..., 128:256].reshape(2, 256, 1024))
    for k, n in (("wso", "w_ssd_out"), ("wmo", "w_mla_out"), ("wgo", "w_gdn_out"), ("wo", "w_out"), ("wup", "w_up"),
                 ("wdn", "w_down"), ("ada", "ada_w_2"), ("nqkv", "na_w_qkv_2"), ("no", "na_w_o_2"), ("hin", "hg_w_in_2"),
                 ("ho", "hg_w_o_2"), ("fo", "ffn_w_out_2")):
        d[k] = tiled(k, a[n])
    fi = a["ffn_w_in_2"].reshape(2, 1024, 2, 11, 256)
    d["fi"] = tiled("fi", fi.transpose(0, 1, 3, 2, 4).reshape(2, 1024, 5632))
    d["x"] = np.ascontiguousarray(a["x"][0].T.reshape(8, 128, 256).transpose(1, 0, 2))
    d["ctx"] = np.ascontiguousarray(a["ctx_2"][0].T.reshape(8, 128, 256).transpose(1, 0, 2))
    d["pos"] = np.ascontiguousarray(np.broadcast_to(a["positions"], (128, 256)))
    d["c"] = np.ascontiguousarray(np.stack([cols(a["c_2"][0]), cols(a["c_ctx_2"])], -1))
    rows = lambda v: np.broadcast_to(v[:, None, :], (2, 128, v.shape[-1]))
    taps = lambda w: w.reshape(2, 4, -1, 128).transpose(0, 3, 2, 1).reshape(2, 128, -1)
    inv = (10000.0 ** (-np.arange(0, 64, 2, dtype=np.float32) / np.float32(64))).astype(np.float32)
    fn = np.broadcast_to(cols(a["final_norm_g"])[None], (2, 128, 8))
    v1 = {"n1": cols(a["norm1_g"]), "n2": cols(a["norm2_g"]), "cw": taps(a["ssd_conv_w"]), "cb": cols(a["ssd_conv_b"]),
          "gw": taps(a["gdn_conv_w"]), "qn": cols(a["mla_q_norm_g"]), "kn": cols(a["mla_kv_norm_g"]),
          "sn": cols(a["ssd_norm_g"]), "gn": cols(a["gdn_norm_g"]), "sd": cols(np.repeat(a["ssd_d"], 64, -1)),
          "bias": rows(np.concatenate([a["ssd_dt_bias"], a["gdn_dt_bias"]], -1)),
          "alog": rows(np.concatenate([a["ssd_a_log"], a["gdn_a_log"]], -1)), "fn": fn,
          "inv": np.broadcast_to(np.tile(inv, 4)[None, :, None], (2, 128, 1))}
    d["v1"] = np.ascontiguousarray(np.concatenate([v1[k] for k in VEC1], -1).transpose(1, 0, 2))
    two = lambda g: np.broadcast_to(np.tile(g[0], 2)[None, :, None], (2, 128, 1))
    hl = a["hg_lower_2"].reshape(32, 128).T[None]
    v2 = {"adab": cols(a["ada_b_2"]), "n1": cols(a["norm1_g_2"]), "n2": cols(a["norm2_g_2"]),
          "qg": two(a["na_q_gain_2"]), "kg": two(a["na_k_gain_2"]), "hl": np.broadcast_to(hl, (2, 128, 32)),
          "hn": np.broadcast_to(a["hg_norm_g_2"].reshape(1, 128, 1), (2, 128, 1))}
    d["v2"] = np.ascontiguousarray(np.concatenate([v2[k] for k in VEC2], -1).transpose(1, 0, 2))
    rpb = np.pad(a["na_rpb_2"][0], ((0, 0), (0, 0), (0, 1)), constant_values=NEG)
    qi = np.arange(256)
    r, c = qi // 64, qi % 64
    lo = np.clip(c - 8, 0, 48)[:, None]
    inside = (c[None, :] >= lo) & (c[None, :] < lo + 16)
    ri = r[None, :] - r[:, None] + 7
    ci = np.where(inside, np.clip(c[None, :] - c[:, None] + 15, 0, 30), 31)
    tab = rpb[:, ri, ci]
    d["rpb"] = np.ascontiguousarray(tab.reshape(2, 8, 2, 128, 256).transpose(2, 0, 3, 1, 4))
    d["cst"], d["imask"] = constants()
    return d


def kernel(**inputs):
    import numpy as _np
    import concourse.bacc as _bacc
    from concourse import mybir as _mybir
    from concourse.bass_utils import run_bass_kernel_spmd as _run

    d = layout({k: _np.asarray(v) for k, v in inputs.items()})
    nc = _bacc.Bacc("TRN2", target_bir_lowering=False, num_devices=1)
    arrays, aps = {}, {}
    for name, v in d.items():
        arrays[f"in_{name}"] = v
        aps[name] = nc.dram_tensor(f"in_{name}", v.shape, _mybir.dt.from_np(v.dtype), kind="ExternalInput").ap()
    out = nc.dram_tensor("out_0", (128, 8, 256), F32, kind="ExternalOutput").ap()
    order = program(_bacc.Bacc("TRN2", target_bir_lowering=False, num_devices=1), aps, out)
    program(nc, aps, out, order)
    r = _run(nc, [arrays], core_ids=[0])
    y = r.results[0]["out_0"]
    return _np.ascontiguousarray(y.transpose(1, 0, 2).reshape(1024, 256).T)[None]
```
